# Optimizing a Trainium2 kernel written in Bass

```python
import math
import jax
import jax.numpy as jnp
from jax import lax
import numpy as np

D_MODEL = 1024
BATCH = 1
SEQ = 256
DEPTH = 2

SSM_GROUP = 16
SSM_GROUPS = 32
SSM_WIDTH = SSM_GROUP * SSM_GROUPS
SSM_STATE = 64
N_HEADS = 8
HEAD_DIM = 64
V_DIM = 2 * HEAD_DIM
QK_WIDTH = N_HEADS * 2 * HEAD_DIM
ATTN_WIDTH = N_HEADS * V_DIM
Q_BLOCK = 128
ROPE_THETA = 10000.0
IN_COLS = SSM_WIDTH + 2 * QK_WIDTH + ATTN_WIDTH + 2 * D_MODEL
SPLITS = [SSM_WIDTH,
          SSM_WIDTH + QK_WIDTH,
          SSM_WIDTH + 2 * QK_WIDTH,
          SSM_WIDTH + 2 * QK_WIDTH + ATTN_WIDTH,
          SSM_WIDTH + 2 * QK_WIDTH + ATTN_WIDTH + D_MODEL]
D_FF = 2816
N_EXPERTS = 8
TOP_K = 2
N_DENSE = (DEPTH + 1) // 2
N_MOE = DEPTH // 2
EPS = 1e-6
SUBLN_EPS = 1e-5

kernel_name = 'hybrid_s5_diffattn_moe_trunk'

def rms_norm(x, g, eps=EPS):
    x32 = x.astype(jnp.float32)
    y = x32 * lax.rsqrt(jnp.mean(x32 * x32, axis=-1, keepdims=True) + eps)
    return (y * g.astype(jnp.float32)).astype(x.dtype)

def apply_rope(t, cos, sin):
    t32 = t.astype(jnp.float32)
    t1, t2 = jnp.split(t32, 2, axis=-1)
    rot = jnp.concatenate([-t2, t1], axis=-1)
    return (t32 * cos + rot * sin).astype(t.dtype)

def _complex_affine_combine(c1, c2):
    a1r, a1i, b1r, b1i = c1
    a2r, a2i, b2r, b2i = c2
    ar = a2r * a1r - a2i * a1i
    ai = a2r * a1i + a2i * a1r
    br = a2r * b1r - a2i * b1i + b2r
    bi = a2r * b1i + a2i * b1r + b2i
    return (ar, ai, br, bi)

def s5_branch(u, lam_re, lam_im, log_dt, b_re, b_im, c_re, c_im, d):
    f32 = jnp.float32
    bsz, s, _ = u.shape
    u32 = u.astype(f32).reshape(bsz, s, SSM_GROUPS, SSM_GROUP)
    lr = lam_re.astype(f32)
    li = lam_im.astype(f32)
    dt = jnp.exp(log_dt.astype(f32))[:, None]
    mag = jnp.exp(lr * dt)
    ar = mag * jnp.cos(li * dt)
    ai = mag * jnp.sin(li * dt)
    den = lr * lr + li * li
    nr = ar - 1.0
    ni = ai
    fr = (nr * lr + ni * li) / den
    fi = (ni * lr - nr * li) / den
    br = b_re.astype(f32)
    bi = b_im.astype(f32)
    bbr = fr[..., None] * br - fi[..., None] * bi
    bbi = fr[..., None] * bi + fi[..., None] * br
    bu_r = jnp.einsum('gpj,bsgj->bsgp', bbr, u32)
    bu_i = jnp.einsum('gpj,bsgj->bsgp', bbi, u32)
    a_r = jnp.broadcast_to(ar, (1, s) + ar.shape)
    a_i = jnp.broadcast_to(ai, (1, s) + ai.shape)
    _, _, st_r, st_i = lax.associative_scan(_complex_affine_combine, (a_r, a_i, bu_r, bu_i), axis=1)
    y = (jnp.einsum('gjp,bsgp->bsgj', c_re.astype(f32), st_r)
         - jnp.einsum('gjp,bsgp->bsgj', c_im.astype(f32), st_i)
         + d.astype(f32) * u32)
    return y.reshape(bsz, s, SSM_WIDTH).astype(u.dtype)

def diff_attention(q, k, v, lam):
    bsz, s = q.shape[0], q.shape[1]
    n_blk = s // Q_BLOCK
    scale = HEAD_DIM ** -0.5
    kpos = jnp.arange(s)
    neg = jnp.finfo(jnp.float32).min

    def one_block(i):
        qs = lax.dynamic_slice_in_dim(q, i * Q_BLOCK, Q_BLOCK, axis=1)
        sc = jnp.einsum('bqhcd,bkhcd->bhcqk', qs, k).astype(jnp.float32) * scale
        qpos = i * Q_BLOCK + jnp.arange(Q_BLOCK)
        mask = qpos[:, None] >= kpos[None, :]
        p = jax.nn.softmax(jnp.where(mask, sc, neg), axis=-1)
        w = p[:, :, 0] - lam * p[:, :, 1]
        return jnp.einsum('bhqk,bkhd->bqhd', w.astype(v.dtype), v)

    out = lax.map(one_block, jnp.arange(n_blk))
    return jnp.moveaxis(out, 0, 1).reshape(bsz, s, N_HEADS, V_DIM)

def swiglu(h, wg, wu, wd):
    return (jax.nn.silu(h @ wg) * (h @ wu)) @ wd

def moe_swiglu(h, router_w, wg, wu, wd):
    bsz, s, dm = h.shape
    hf = h.reshape(-1, dm)
    logits = hf.astype(jnp.float32) @ router_w.astype(jnp.float32)
    top_vals, top_idx = lax.top_k(logits, TOP_K)
    top_w = jax.nn.softmax(top_vals, axis=-1)
    gates = jnp.sum(jax.nn.one_hot(top_idx, N_EXPERTS, dtype=jnp.float32) * top_w[..., None], axis=1)
    gates = gates.astype(h.dtype)
    y = jnp.zeros_like(hf)
    for e in range(N_EXPERTS):
        y = y + gates[:, e:e + 1] * swiglu(hf, wg[e], wu[e], wd[e])
    return y.reshape(bsz, s, dm)

def setup_inputs(seed: int = 0) -> dict:
    key = jax.random.key(seed)
    ks = jax.random.split(key, 32)
    f32 = jnp.float32
    L, D, G, P, J = DEPTH, D_MODEL, SSM_GROUPS, SSM_STATE, SSM_GROUP

    def nrm(k, shape, std):
        return jax.random.normal(k, shape, f32) * std

    x = jax.random.normal(ks[0], (BATCH, SEQ, D), f32)
    positions = jnp.broadcast_to(jnp.arange(SEQ, dtype=jnp.int32), (BATCH, SEQ))
    mix_norm = 1.0 + nrm(ks[1], (L, D), 0.02)
    w_in = nrm(ks[2], (L, D, IN_COLS), D ** -0.5)
    ssm_lambda_re = -0.5 + nrm(ks[3], (L, G, P), 0.01)
    ssm_lambda_im = math.pi * jnp.arange(P, dtype=f32)[None, None, :] + nrm(ks[4], (L, G, P), 0.01)
    ssm_log_dt = jax.random.uniform(ks[5], (L, G), f32, math.log(1e-3), math.log(1e-1))
    ssm_b_re = nrm(ks[6], (L, G, P, J), (2.0 * J) ** -0.5)
    ssm_b_im = nrm(ks[7], (L, G, P, J), (2.0 * J) ** -0.5)
    ssm_c_re = nrm(ks[8], (L, G, J, P), (2.0 * P) ** -0.5 * 4.0)
    ssm_c_im = nrm(ks[9], (L, G, J, P), (2.0 * P) ** -0.5 * 4.0)
    ssm_d = nrm(ks[10], (L, G, J), 1.0)
    w_glu = nrm(ks[11], (L, SSM_WIDTH, SSM_WIDTH), SSM_WIDTH ** -0.5)
    b_glu = nrm(ks[12], (L, SSM_WIDTH), 0.01)
    lambda_q1 = nrm(ks[13], (L, HEAD_DIM), 0.1)
    lambda_k1 = nrm(ks[14], (L, HEAD_DIM), 0.1)
    lambda_q2 = nrm(ks[15], (L, HEAD_DIM), 0.1)
    lambda_k2 = nrm(ks[16], (L, HEAD_DIM), 0.1)
    subln = 1.0 + nrm(ks[17], (L, V_DIM), 0.02)
    w_proj_ssm = nrm(ks[18], (L, SSM_WIDTH, D), SSM_WIDTH ** -0.5)
    w_proj_attn = nrm(ks[19], (L, ATTN_WIDTH, D), ATTN_WIDTH ** -0.5)
    w_out = nrm(ks[20], (L, D, D), D ** -0.5)
    ffn_norm = 1.0 + nrm(ks[21], (L, D), 0.02)
    dense_w_gate = nrm(ks[22], (N_DENSE, D, D_FF), D ** -0.5)
    dense_w_up = nrm(ks[23], (N_DENSE, D, D_FF), D ** -0.5)
    dense_w_down = nrm(ks[24], (N_DENSE, D_FF, D), D_FF ** -0.5)
    router_w = nrm(ks[25], (N_MOE, D, N_EXPERTS), D ** -0.5)
    moe_w_gate = nrm(ks[26], (N_MOE, N_EXPERTS, D, D_FF), D ** -0.5)
    moe_w_up = nrm(ks[27], (N_MOE, N_EXPERTS, D, D_FF), D ** -0.5)
    moe_w_down = nrm(ks[28], (N_MOE, N_EXPERTS, D_FF, D), D_FF ** -0.5)
    final_norm = 1.0 + nrm(ks[29], (D,), 0.02)
    return {'x': x, 'positions': positions, 'mix_norm': mix_norm, 'w_in': w_in,
            'ssm_lambda_re': ssm_lambda_re, 'ssm_lambda_im': ssm_lambda_im, 'ssm_log_dt': ssm_log_dt,
            'ssm_b_re': ssm_b_re, 'ssm_b_im': ssm_b_im, 'ssm_c_re': ssm_c_re, 'ssm_c_im': ssm_c_im,
            'ssm_d': ssm_d, 'w_glu': w_glu, 'b_glu': b_glu,
            'lambda_q1': lambda_q1, 'lambda_k1': lambda_k1, 'lambda_q2': lambda_q2, 'lambda_k2': lambda_k2,
            'subln': subln, 'w_proj_ssm': w_proj_ssm, 'w_proj_attn': w_proj_attn, 'w_out': w_out,
            'ffn_norm': ffn_norm, 'dense_w_gate': dense_w_gate, 'dense_w_up': dense_w_up,
            'dense_w_down': dense_w_down, 'router_w': router_w, 'moe_w_gate': moe_w_gate,
            'moe_w_up': moe_w_up, 'moe_w_down': moe_w_down, 'final_norm': final_norm}

def reference(x, positions, mix_norm, w_in, ssm_lambda_re, ssm_lambda_im, ssm_log_dt,
              ssm_b_re, ssm_b_im, ssm_c_re, ssm_c_im, ssm_d, w_glu, b_glu,
              lambda_q1, lambda_k1, lambda_q2, lambda_k2, subln, w_proj_ssm, w_proj_attn, w_out,
              ffn_norm, dense_w_gate, dense_w_up, dense_w_down, router_w, moe_w_gate,
              moe_w_up, moe_w_down, final_norm):
    bsz, s, _ = x.shape
    f32 = jnp.float32
    inv_freq = ROPE_THETA ** (-jnp.arange(0, HEAD_DIM, 2, dtype=f32) / HEAD_DIM)
    ang = positions.astype(f32)[..., None] * inv_freq
    emb = jnp.concatenate([ang, ang], axis=-1)[:, :, None, None, :]
    cos = jnp.cos(emb)
    sin = jnp.sin(emb)

    for l in range(DEPTH):
        h = rms_norm(x, mix_norm[l])
        z = h @ w_in[l]
        u, q, k, v, g_ssm, g_attn = jnp.split(z, SPLITS, axis=-1)

        y_a = s5_branch(u, ssm_lambda_re[l], ssm_lambda_im[l], ssm_log_dt[l], ssm_b_re[l], ssm_b_im[l],
                        ssm_c_re[l], ssm_c_im[l], ssm_d[l])
        y_a = jax.nn.gelu(y_a)
        y_a = y_a * jax.nn.sigmoid(y_a @ w_glu[l] + b_glu[l])

        q = apply_rope(q.reshape(bsz, s, N_HEADS, 2, HEAD_DIM), cos, sin)
        k = apply_rope(k.reshape(bsz, s, N_HEADS, 2, HEAD_DIM), cos, sin)
        v = v.reshape(bsz, s, N_HEADS, V_DIM)
        lam_init = 0.8 - 0.6 * math.exp(-0.3 * l)
        lam = (jnp.exp(jnp.sum(lambda_q1[l].astype(f32) * lambda_k1[l].astype(f32)))
               - jnp.exp(jnp.sum(lambda_q2[l].astype(f32) * lambda_k2[l].astype(f32))) + lam_init)
        o = diff_attention(q, k, v, lam)
        o = rms_norm(o, subln[l], SUBLN_EPS) * (1.0 - lam_init)
        y_b = o.reshape(bsz, s, ATTN_WIDTH)

        m = jax.nn.sigmoid(g_ssm) * (y_a @ w_proj_ssm[l]) + jax.nn.sigmoid(g_attn) * (y_b @ w_proj_attn[l])
        x = x + m @ w_out[l]

        h = rms_norm(x, ffn_norm[l])
        if l % 2 == 0:
            i = l // 2
            f = swiglu(h, dense_w_gate[i], dense_w_up[i], dense_w_down[i])
        else:
            i = l // 2
            f = moe_swiglu(h, router_w[i], moe_w_gate[i], moe_w_up[i], moe_w_down[i])
        x = x + f

    return rms_norm(x, final_norm)


_drawn_inputs = setup_inputs


def setup_inputs(seed=0):
    import zlib

    import numpy as np

    out = dict(_drawn_inputs(seed))
    spreads = {}
    factors = {'ssm_lambda_re': 6.132, 'b_glu': 8.0, 'final_norm': 2.936}
    for name, (base, spread) in spreads.items():
        noise = np.random.default_rng([zlib.crc32(name.encode()), seed]).standard_normal(out[name].shape)
        drawn = base * np.exp(spread * noise) if base else spread * noise
        out[name] = jnp.asarray(drawn.astype(out[name].dtype))
    for name, factor in factors.items():
        out[name] = (out[name] * factor).astype(out[name].dtype)
    return out
```

```python
import math
from contextlib import ExitStack

import numpy as np

import concourse.bass as bass
from concourse import mybir

F32 = mybir.dt.float32
F32R = mybir.dt.float32r
BF16 = mybir.dt.bfloat16
I32 = mybir.dt.int32
U32 = mybir.dt.uint32
ALU = mybir.AluOpType
ACT = mybir.ActivationFunctionType
AX_X = mybir.AxisListType.X

P = 128
SEQ, D, DEPTH = 256, 1024, 2
NT = SEQ // P
KD = D // P
GROUPS, GCH, STATE = 32, 16, 64
PAIRS = GROUPS * STATE // P
SSM_W = GROUPS * GCH
CT = SSM_W // P
CHUNKS = PAIRS // 2
HEADS, HD = 8, 64
SCALE = HD ** -0.5
FF, EXPERTS = 2816, 8
FB = 256
NJ = FF // FB
EPS, SUB_EPS = 1e-6, 1e-5
NEG = -1.0e30
MAX_ROUNDS = EXPERTS + 3
TWO_PI_HI, TWO_PI_MID = 6.28125, 0.0019350051879882812
TWO_PI_LO = 2 * math.pi - TWO_PI_HI - TWO_PI_MID
ROUND = 12582912.0
PI_IN = 3.1415925

SLOT = 2048
SEG = 33
NRAW, NW, AHEAD = 4, 3, 2
RAW_POS = [i % 4 if i < 24 else (i - 24) % 3 for i in range(SEG)]
RAW_USES = [RAW_POS.count(p) for p in range(NRAW)]
GROUP_BLOCK = 512
BLOCK_COUNT = 18
U_BLOCK, GLU, PS0, PA0, WO0 = 0, 11, 12, 14, 16
PAIR_OF = [0, 1, 0, 1, 0, 1, 0, 0, 0, 0, 0, 0, 0, 1, 0, 1, 0, 1]
EVAC_BY_ACT = {0, 5, 6, 7, 8, 9, 10, 11}
ACCA_L = 2 * len(EVAC_BY_ACT)
ACCV_L = 2 * (BLOCK_COUNT - len(EVAC_BY_ACT))


def slot_block(i):
    if i < 22:
        return i // 2, i % 2, 2
    if i < 25:
        return i - 22 + GLU, 0, 1
    return PA0 + (i - 25) // 2, (i - 25) % 2, 2


def lam_init(l):
    return 0.8 - 0.6 * math.exp(-0.3 * l)


FFN_SLOTS = [("g", 0), ("u", 0)]
for _j in range(NJ - 1):
    FFN_SLOTS += [("g", _j + 1), ("u", _j + 1), ("d", _j)]
FFN_SLOTS += [("d", NJ - 1)]
FFN_AT = {what: i for i, what in enumerate(FFN_SLOTS)}


def raw_before(i):
    for back in range(i - 1, i - 1 - SEG, -1):
        if RAW_POS[back % SEG] == RAW_POS[i]:
            return back


def mixer_tail(s):
    todo = []
    if 0 <= s - 15 < HEADS:
        todo.append(("scores", s - 15))
    if 0 <= s - 16 < HEADS:
        todo.append(("wT", s - 16))
    if 0 <= s - 17 < HEADS:
        todo.append(("o", s - 17))
    if 0 <= s - 18 < HEADS:
        todo.append(("oT", s - 18))
    if s in (5, 7, 9, 11):
        todo.append(("qkT", (s - 3) // 2))
    if 0 <= s - 2 < PAIRS:
        todo.append(("bu", s - 2))
    if s >= 6 and (s - 6) % 2 == 0 and (s - 6) // 2 < CHUNKS:
        todo.append(("y", (s - 6) // 2))
    return todo


TR = []
for _l in range(DEPTH):
    TR += [(_l, "h1", g) for g in range(4)]
    for _s in range(SEG):
        for _w, _h in mixer_tail(_s):
            if _w in ("wT", "o", "oT"):
                TR.append((_l, _w, _h))
            if _w == "qkT":
                TR += [(_l, "qkT", 2 * _h), (_l, "qkT", 2 * _h + 1)]
        if _s == 28:
            TR += [(_l, "mT", g) for g in range(4)]
    TR += [(_l, "h2", g) for g in range(4)]
    TR += [(_l, "act", j) for j in range(NJ)] if _l == 0 else [(1, "logits", 0), (1, "places", 0)]
TR_AT = {what: n for n, what in enumerate(TR)}
ROUND_TR = ["hs0", "hs1", "ST"] + [f"act{j}" for j in range(NJ)]


def trunk(nc, t):
    ctx = ExitStack()
    with ctx:
        here = [(nc.sbuf_base + 63) // 64 * 64]

        def at(name, shape, dt, addr):
            return nc.alloc_sbuf_tensor_at(name, list(shape), dt, offset=addr)

        def size(shape, dt):
            n = 2 if dt == BF16 else 4
            for s in shape[1:]:
                n *= s
            return (n + 31) // 32 * 32

        def sb(name, shape, dt=F32):
            a = here[0]
            here[0] += size(shape, dt)
            return at(name, shape, dt, a)

        def room(nbytes):
            a = here[0]
            here[0] += nbytes
            return a

        def sem(name):
            return ctx.enter_context(nc.semaphore(name))

        x = sb("x_tok", [P, NT, D])
        hTh = sb("hT_hi", [P, KD, SEQ], F32R)
        hTl = sb("hT_lo", [P, KD, SEQ], F32R)
        raw = sb("w_raw", [P, NRAW, SLOT])
        wh = sb("w_hi", [P, NW, SLOT], F32R)
        wl = sb("w_lo", [P, NW, SLOT], F32R)
        ident = sb("ident", [P, P])
        identb = sb("identb", [P, P], BF16)
        maskb = sb("maskb", [P, P], BF16)
        cosT = sb("rope_cos", [P, NT, 32])
        sinT = sb("rope_sin", [P, NT, 32])
        nsinT = sb("rope_nsin", [P, NT, 32])
        gains = sb("gains", [P, 2, DEPTH, KD])
        subg = sb("subln_gain", [P, DEPTH])
        bglu = sb("half_b_glu", [P, DEPTH, CT])
        dskip = sb("ssm_d", [P, DEPTH, CT])
        nlam = sb("minus_lambda", [P, DEPTH])
        mhalf = sb("minus_half", [P, 4])
        s5m = sb("s5_mag", [P, DEPTH, PAIRS])
        s5c = sb("s5_cos", [P, DEPTH, PAIRS])
        s5s = sb("s5_sin", [P, DEPTH, PAIRS])
        s5fr = sb("s5_fr", [P, DEPTH, PAIRS])
        s5fi = sb("s5_fi", [P, DEPTH, PAIRS])
        stat = sb("norm_stat", [P, 4])
        mean = sb("norm_mean", [P, 4])
        rstd = sb("norm_rstd", [P, 4])
        mx = sb("score_max", [P, 4])
        nb = sb("exp_bias", [P, 4])
        sm = sb("exp_sum", [P, 4])
        rs = sb("exp_rsum", [P, 4])
        c2 = sb("second_map_coef", [P, 2])
        oss = sb("o_stat", [P, 2])
        oms = sb("o_mean", [P, 2])
        ors = sb("o_rstd", [P, 2])
        wpow = sb("turn_dve", [P, 8, 4])
        wpowp = sb("turn_pool", [P, 8, 4])

        a_q, a_k, a_v = room(8192), room(8192), room(8192)
        a_u, a_yh, a_yl = room(4096), room(4096), room(4096)
        a_tab = room(32768)
        a_rr, a_ri, a_sr, a_tt, a_t12 = room(4096), room(4096), room(4096), room(2048), room(2048)
        a_att = room(6144)
        qT = at("qT", [P, HEADS, SEQ], F32, a_q)
        kT = at("kT", [P, HEADS, SEQ], F32, a_k)
        v = at("v_tok", [P, NT, D], F32, a_v)
        outsq = at("square_out", [P, NT, D], F32, a_q)
        xn = at("x_normed", [P, NT, D], F32, a_v)
        uT = at("uT", [P, CT, SEQ], F32, a_u)
        ySh = at("yS_hi", [P, CT, SEQ], F32R, a_yh)
        ySl = at("yS_lo", [P, CT, SEQ], F32R, a_yl)
        tab = at("s5_turns", [P, PAIRS, 2, SEQ], F32, a_tab)
        gs = at("gate_ssm", [P, NT, D], F32, a_tab)
        ga = at("gate_attn", [P, NT, D], F32, a_tab + 8192)
        yBh = at("yB_hi", [P, KD, SEQ], F32R, a_tab + 16384)
        yBl = at("yB_lo", [P, KD, SEQ], F32R, a_tab + 24576)
        rr = at("s5_r_re", [P, 2, 2, SEQ], F32, a_rr)
        ri = at("s5_r_im", [P, 2, 2, SEQ], F32, a_ri)
        sr = at("s5_s_re", [P, 2, 2, SEQ], F32, a_sr)
        tt = at("s5_pool_tmp", [P, 2, SEQ], F32, a_tt)
        t12 = at("s5_dve_tmp", [P, 2, SEQ], F32, a_t12)
        tabt = at("turn_tmp_dve", [P, 8, P], F32, a_rr)
        tabp = at("turn_tmp_pool", [P, 8, P], F32, a_sr)
        gel = at("gelu_tmp", [P, CT, SEQ], F32, a_rr)
        gth = at("gelu_tanh", [P, CT, SEQ], F32, a_ri)
        ropeA = at("rope_a", [P, 512], F32, a_att)
        ropeB = at("rope_b", [P, 512], F32, a_att + 2048)
        ropeC = at("rope_c", [P, 512], F32, a_att + 4096)
        prob = at("prob", [P, 2, 384], F32, a_att)
        wT = at("attn_wT", [P, 384], F32, a_att + 3072)
        osq = sb("o_square_out", [P, 256])
        osb = at("o_tok", [P, 256], F32, a_att + 4608)
        Bre = sb("s5_b_re", [P, CT, P])
        Bim = sb("s5_b_im", [P, CT, P])
        Cre = sb("s5_c_re", [P, PAIRS, 32])
        Cin = sb("s5_c_nim", [P, PAIRS, 32])
        act_t = at("act_tok", [P, NT, FB], F32, a_q)
        sg = at("silu_g", [P, NT, FB], F32, a_q + 2048)
        aTh = at("actT_hi", [P, 2, SEQ], F32R, a_q + 4096)
        aTl = at("actT_lo", [P, 2, SEQ], F32R, a_q + 6144)
        hsh = at("hsT_hi", [P, KD, P], F32R, a_k)
        hsl = at("hsT_lo", [P, KD, P], F32R, a_k + 4096)
        bTh = at("eactT_hi", [P, 2, P], F32R, a_yl)
        bTl = at("eactT_lo", [P, 2, P], F32R, a_yl + 1024)
        ysb = at("y_slots", [P, D], F32, a_yh)
        S = at("select", [P, NT, P], F32, a_att)
        ST = at("selectT", [P, SEQ], F32, a_att + 1024)
        gfin = at("final_gain", [P, D], F32, a_u)
        outt = at("out_tok", [P, NT, D], F32, a_k)
        mp = [a_tab]

        def rt(name, shape, dt=F32):
            a = mp[0]
            mp[0] += size(shape, dt)
            return at(name, shape, dt, a)

        rw = rt("router_w", [P, KD, EXPERTS])
        lg = rt("logits", [P, NT, 8])
        top = rt("top8", [P, NT, 8])
        topi = rt("top8_at", [P, NT, 8], U32)
        topf = rt("top_at_f", [P, NT, 8])
        iota8 = rt("iota8", [P, 8])
        oh1 = rt("first_choice", [P, NT, 8])
        oh2 = rt("second_choice", [P, NT, 8])
        ex2 = rt("second_exp", [P, NT])
        den = rt("gate_den", [P, NT])
        g1 = rt("gate_first", [P, NT])
        g2 = rt("gate_second", [P, NT])
        G = rt("gates", [P, NT, 8])
        M = rt("chosen", [P, NT, 8])
        below = rt("below", [P, P])
        ones = rt("ones", [P, P])
        placed = rt("place_plus_1", [P, NT, 8])
        cnt = rt("expert_counts", [P, 8])
        over = rt("over", [P, 8])
        overc = rt("over_cum", [P, 8])
        ohr = rt("over_round", [P, 3, 8])
        prod = rt("over_prod", [P, 8])
        placeR = rt("round_place", [P, NT, 12])
        gateR = rt("round_gate", [P, NT, 12])
        eF = rt("round_expert_f", [P, 12])
        eI = rt("round_expert", [P, 12], I32)
        rF = rt("rounds_f", [P, 1])
        rI = rt("rounds", [P, 1], I32)
        iota128 = rt("iota128", [P, P])
        iotai = rt("iota_int", [P, P], I32)
        pcol = rt("place_now", [P, NT])
        gcol = rt("gate_now", [P, NT])
        sp_ = [a_k]

        def su(name, shape, dt=F32):
            a = sp_[0]
            sp_[0] += size(shape, dt)
            return at(name, shape, dt, a)

        posi = su("positions_int", [P, NT], I32)
        posf = su("positions_f", [P, NT])
        invf = su("inv_freq", [P, 32])
        ang = su("angle", [P, NT * 32 + DEPTH * PAIRS])
        angk = su("angle_turns", [P, NT * 32 + DEPTH * PAIRS])
        angr = su("angle_rest", [P, NT * 32 + DEPTH * PAIRS])
        lamv = su("lambda_vecs", [P, 4, DEPTH, HD])
        lamp = su("lambda_prod", [P, 2, DEPTH, HD])
        lams = su("lambda_sum", [P, 2, DEPTH])
        lame = su("lambda_exp", [P, 2, DEPTH])
        lre = su("ssm_lre", [P, DEPTH, PAIRS])
        lim = su("ssm_lim", [P, DEPTH, PAIRS])
        ldt = su("ssm_ldt", [P, DEPTH, PAIRS])
        dtt = su("ssm_dt", [P, DEPTH, PAIRS])
        q1 = su("ssm_q1", [P, DEPTH, PAIRS])
        q2 = su("ssm_q2", [P, DEPTH, PAIRS])
        q3 = su("ssm_q3", [P, DEPTH, PAIRS])
        q4 = su("ssm_q4", [P, DEPTH, PAIRS])
        Craw = at("s5_c_raw", [P, 2, PAIRS, GCH], F32, a_att)
        Ctmp = at("s5_c_tmp", [P, 2, PAIRS, GCH], F32, a_att + 2048)
        assert here[0] <= nc.sbuf_usable_end, (here[0], nc.sbuf_usable_end)
        assert mp[0] <= a_tab + 32768 and sp_[0] <= a_k + 8192

        PS = ctx.enter_context(nc.psum_tensor("psum", [P, 8, 512], F32))

        def bank(b):
            return PS[:, b, :]

        s_raw = [sem(f"raw_landed{p}") for p in range(NRAW)]
        s_hi, s_lo, s_used = sem("w_hi_ready"), sem("w_lo_ready"), sem("w_used")
        s_x0, s_set, s_s5l, s_c, s_b = sem("x_landed"), sem("setup_landed"), sem("s5_landed"), sem("c_landed"), sem("b_landed")
        s_gf, s_rw, s_out = sem("final_gain_landed"), sem("router_landed"), sem("out_stored")
        s_pool, s_dve, s_actc = sem("pool_step"), sem("dve_step"), sem("act_step")
        s_const, s_bz = sem("constants_ready"), sem("b_zeroed")
        s_ang, s_trig, s_dt = sem("angles_ready"), sem("trig_ready"), sem("dt_ready")
        s_tabd, s_tabp, s_prep = sem("turns_by_dve"), sem("turns_by_pool"), sem("c_scaled")
        s_ss, s_rstd, s_xn = sem("norm_sum"), sem("norm_rstd_ready"), sem("x_normed_ready")
        s_tr, s_thi, s_trf = sem("tr_written"), sem("tr_hi_taken"), sem("tr_free")
        s_acc, s_accA, s_accV = sem("acc_written"), sem("acc_taken_act"), sem("acc_taken_dve")
        s_rope = sem("roped")
        s_bu, s_buf, s_scan, s_rot = sem("bu_written"), sem("bu_taken"), sem("scanned"), sem("turned_back")
        s_yc, s_yv = sem("y_products"), sem("y_taken")
        s_gsq, s_gin, s_gth, s_yg, s_ygh, s_ygl = (sem("gelu_square"), sem("gelu_inner"), sem("gelu_tanh_ready"),
                                                   sem("gelu_ready"), sem("yS_hi_ready"), sem("yS_lo_ready"))
        s_sc, s_nb, s_ex, s_w = sem("scores_written"), sem("exp_bias_ready"), sem("exp_ready"), sem("attn_w_ready")
        s_osq, s_ors, s_on = sem("o_squared"), sem("o_rstd_ready"), sem("o_normed")
        s_m = sem("m_ready")
        s_gu, s_sg, s_act = sem("gate_up_written"), sem("silu_ready"), sem("act_ready")
        s_lg, s_route = sem("exp_second_ready"), sem("routed")
        s_M = sem("choices_ready")
        s_S, s_ysb, s_scat, s_scatv = sem("select_ready"), sem("y_copied"), sem("scattered"), sem("scatter_taken")
        s_fin = sem("out_ready")

        R_TR = len(ROUND_TR)
        TR0 = len(TR)
        USED_MIX, USED_FFN = 15, 2 * NJ
        GU0 = NT * NJ

        def used(seg, i, r=None):
            if seg in (0, 2):
                blk, h, n = slot_block(i)
                if h == n - 1:
                    return s_acc, 2 * (BLOCK_COUNT * (seg // 2) + blk + 1)
                mine = sum(1 for k in range(i + 1) if slot_block(k)[1] != slot_block(k)[2] - 1)
                return s_used, (0 if seg == 0 else USED_MIX + USED_FFN) + mine
            kind, j = FFN_SLOTS[i]
            if kind == "u":
                return s_gu, NT * (j + 1) if seg == 1 else r * NJ + (GU0 + j + 1)
            mine = sum(1 for k in range(i + 1) if FFN_SLOTS[k][0] != "u")
            if seg == 1:
                return s_used, USED_MIX + mine
            return s_used, r * USED_FFN + (2 * USED_MIX + USED_FFN + mine)

        def wait_ring_free(eng, seg, i, r=None):
            if i >= NW or seg > 0:
                if i >= NW:
                    s, val = used(seg, i - NW, r)
                elif seg < 3:
                    s, val = used(seg - 1, i - NW + SEG)
                else:
                    return
                eng.wait_ge(s, val)

        def nslot(seg, i, r=None):
            return seg * SEG + i if seg < 3 else r * SEG + (3 * SEG + i)

        def act_split(act, seg, i, r=None):
            p = RAW_POS[i]
            k = RAW_POS[:i].count(p) + 1
            landed = 16 * (seg * RAW_USES[p] + k) if seg < 3 else r * (16 * RAW_USES[p]) + 16 * (3 * RAW_USES[p] + k)
            act.wait_ge(s_raw[p], landed)
            wait_ring_free(act, seg, i, r)
            nc.scalar.activation(wh[:, i % NW, :], raw[:, p, :], ACT.Copy).then_inc(s_hi, 1)

        def dve_split(dve, seg, i, r=None):
            dve.wait_ge(s_hi, nslot(seg, i, r) + 1)
            nc.vector.tensor_tensor(wl[:, i % NW, :], raw[:, RAW_POS[i], :], wh[:, i % NW, :].bitcast(F32),
                                    ALU.subtract).then_inc(s_lo, 1)

        def split_ahead(split, eng, seg, i):
            if i + AHEAD < SEG:
                split(eng, seg, i + AHEAD)
            elif seg < 2:
                split(eng, seg + 1, i + AHEAD - SEG)

        def whv(i, k):
            return wh[:, i % NW, :].rearrange("p (k n) -> p k n", k=k)

        def wlv(i, k):
            return wl[:, i % NW, :].rearrange("p (k n) -> p k n", k=k)

        class Own:

            def __init__(self, eng, s):
                self.eng, self.s, self.n, self.r, self.per = eng, s, 0, None, 0

            def do(self, ins):
                ins.then_inc(self.s, 1)
                self.n += 1

            def settle(self):
                if self.r is None:
                    self.eng.wait_ge(self.s, self.n)
                else:
                    self.eng.wait_ge(self.s, self.r * self.per + self.n)

        block = ctx.enter_context(nc.Block())

        @block.sync
        def _(sp):
            win = t["w_in"].rearrange("l (c p) n -> l p c n", p=P)
            wglu = t["w_glu"].rearrange("l (c p) n -> l p c n", p=P)
            wps = t["w_proj_ssm"].rearrange("l (c p) n -> l p c n", p=P)
            wpa = t["w_proj_attn"].rearrange("l (c p) n -> l p c n", p=P)
            wo = t["w_out"].rearrange("l (c p) n -> l p c n", p=P)

            def ffn_src(wg, wu, wd, i, e):
                kind, j = FFN_SLOTS[i]
                if kind == "d":
                    a = wd.rearrange("e (c p) n -> e p c n", p=P)[e, :, 2 * j:2 * j + 2, :]
                else:
                    w = wg if kind == "g" else wu
                    a = w.rearrange("e (c p) n -> e p c n", p=P)[e, :, :, j * FB:(j + 1) * FB]
                return a.rearrange("e p c n -> (e p) c n")

            def mixer_src(l, i):
                blk, h, n = slot_block(i)
                half = slice(4 * h, 4 * h + 4)
                if blk < GLU:
                    return win[l, :, half, blk * 512:(blk + 1) * 512]
                if blk == GLU:
                    return wglu[l]
                c = (blk % 2) * 512
                if blk < PA0:
                    return wps[l, :, :, c:c + 512]
                return (wpa if blk < WO0 else wo)[l, :, half, c:c + 512]

            def load(seg, i, src, r=None):
                before = raw_before(i)
                if seg < 3:
                    if seg * SEG + before >= 0:
                        sp.wait_ge(s_lo, seg * SEG + before + 1)
                else:
                    sp.wait_ge(s_lo, r * SEG + (3 * SEG + before + 1))
                k = src.shape[1]
                sp.dma_start(raw[:, RAW_POS[i], :].rearrange("p (k n) -> p k n", k=k), src).then_inc(s_raw[RAW_POS[i]], 16)

            for seg in range(3):
                for i in range(SEG):
                    if seg == 1:
                        src = ffn_src(t["dense_w_gate"], t["dense_w_up"], t["dense_w_down"], i, slice(0, 1))
                    else:
                        src = mixer_src(seg // 2, i)
                    load(seg, i, src)
            sp.wait_ge(s_route, 1)
            rounds = sp.value_load(rI[0:1, 0:1], min_val=EXPERTS, max_val=MAX_ROUNDS)
            with sp.Fori(0, rounds) as r:
                e = sp.value_load(eI[0:1, bass.ds(r, 1)], min_val=0, max_val=EXPERTS - 1)
                for i in range(SEG):
                    load(3, i, ffn_src(t["moe_w_gate"], t["moe_w_up"], t["moe_w_down"], i, bass.ds(e, 1)), r)
            o = t["out"].rearrange("(t p) d -> p t d", p=P)
            for q in range(NT):
                sp.wait_ge(s_fin, q + 1)
                sp.dma_start(o[:, q, :], outt[:, q, :]).then_inc(s_out, 16)
            sp.wait_ge(s_out, 16 * NT)

        def build_turns(e, own, l, p0, w, tmp, tell):
            T = tab[:, p0:p0 + 8]
            own.do(e.memset(T[:, :, 0, 0:1], 1.0))
            own.do(e.memset(T[:, :, 1, 0:1], 0.0))
            own.do(e.tensor_copy(w[:, :, 0:1], s5c[:, l, p0:p0 + 8].rearrange("p (q o) -> p q o", o=1)))
            own.do(e.tensor_copy(w[:, :, 1:2], s5s[:, l, p0:p0 + 8].rearrange("p (q o) -> p q o", o=1)))
            own.settle()
            n = 1
            while n < SEQ:
                wr, wi = w[:, :, 0:1].to_broadcast([P, 8, n]), w[:, :, 1:2].to_broadcast([P, 8, n])
                er, ei = T[:, :, 0, 0:n], T[:, :, 1, 0:n]
                fr, fi = T[:, :, 0, n:2 * n], T[:, :, 1, n:2 * n]
                u = tmp[:, :, 0:n]
                own.do(e.tensor_tensor(fr, er, wr, ALU.mult))
                own.do(e.tensor_tensor(u, ei, wi, ALU.mult))
                own.do(e.tensor_tensor(fi, ei, wr, ALU.mult))
                own.settle()
                own.do(e.tensor_tensor(fr, fr, u, ALU.subtract))
                own.settle()
                own.do(e.tensor_tensor(u, er, wi, ALU.mult))
                own.do(e.tensor_tensor(w[:, :, 2:3], w[:, :, 0:1], w[:, :, 0:1], ALU.mult))
                own.do(e.tensor_tensor(w[:, :, 3:4], w[:, :, 1:2], w[:, :, 1:2], ALU.mult))
                own.settle()
                own.do(e.tensor_tensor(fi, fi, u, ALU.add))
                own.do(e.tensor_tensor(w[:, :, 1:2], w[:, :, 0:1], w[:, :, 1:2], ALU.mult))
                own.settle()
                own.do(e.tensor_tensor(w[:, :, 0:1], w[:, :, 2:3], w[:, :, 3:4], ALU.subtract))
                own.do(e.tensor_tensor(w[:, :, 1:2], w[:, :, 1:2], w[:, :, 1:2], ALU.add))
                own.settle()
                n *= 2
            e.memset(w[:, :, 2:3], 0.0).then_inc(tell, 1)

        @block.gpsimd
        def _(pool):
            own = Own(pool, s_pool)

            own.do(nc.gpsimd.memset(ident[:, :], 0.0))
            own.do(nc.gpsimd.memset(maskb[:, :], 0.0))
            own.settle()
            own.do(nc.gpsimd.affine_select(out=ident[:, :], in_=ident[:, :], compare_op=ALU.not_equal, fill=1.0,
                                           base=0, pattern=[[-1, P]], channel_multiplier=1))
            own.do(nc.gpsimd.affine_select(out=maskb[:, :], in_=maskb[:, :], compare_op=ALU.is_ge, fill=NEG,
                                           base=0, pattern=[[-1, P]], channel_multiplier=1))
            own.do(nc.gpsimd.memset(mhalf[:, :], -0.5))
            own.settle()
            nc.gpsimd.tensor_copy(identb[:, :], ident[:, :]).then_inc(s_const, 1)

            def rms_power(n, m, src, dst, k, scale, eps, got, tell):
                pool.wait_ge(got, n)
                own.do(nc.gpsimd.tensor_scalar(m[:, 0:k], src[:, 0:k], scale, eps, ALU.mult, ALU.add))
                own.settle()
                nc.gpsimd.tensor_tensor(dst[:, 0:k], m[:, 0:k], mhalf[:, 0:k], ALU.pow).then_inc(tell, 1)

            rms_power(1, mean, stat, rstd, NT, 1.0 / D, EPS, s_ss, s_rstd)
            for l in range(DEPTH):
                pool.wait_ge(s_trig, 3)
                if l == 1:
                    pool.wait_ge(s_xn, 2)
                build_turns(nc.gpsimd, own, l, 8, wpowp, tabp, s_tabp)
                if l == 1:
                    rms_power(3, mean, stat, rstd, NT, 1.0 / D, EPS, s_ss, s_rstd)
                for s in range(SEG):
                    c = (s - 4) // 2
                    if s >= 5 and (s - 5) % 2 == 0 and (s - 5) // 2 < CHUNKS:
                        c = (s - 5) // 2
                        b = c % 2
                        pool.wait_ge(s_scan, CHUNKS * l + c + 1)
                        if c >= 2:
                            pool.wait_ge(s_yc, CHUNKS * l + c - 1)
                        er, ei = tab[:, 2 * c:2 * c + 2, 0, :], tab[:, 2 * c:2 * c + 2, 1, :]
                        own.do(nc.gpsimd.tensor_tensor(sr[:, b], er, rr[:, b], ALU.mult))
                        own.do(nc.gpsimd.tensor_tensor(tt[:, :, :], ei, ri[:, b], ALU.mult))
                        own.settle()
                        own.do(nc.gpsimd.tensor_tensor(ri[:, b], er, ri[:, b], ALU.mult))
                        own.do(nc.gpsimd.tensor_tensor(rr[:, b], ei, rr[:, b], ALU.mult))
                        own.do(nc.gpsimd.tensor_tensor(sr[:, b], sr[:, b], tt[:, :, :], ALU.subtract))
                        own.settle()
                        nc.gpsimd.tensor_tensor(ri[:, b], ri[:, b], rr[:, b], ALU.add).then_inc(s_rot, 1)
                    if 0 <= s - 18 < HEADS:
                        rms_power(HEADS * l + s - 17, oms, oss, ors, 2, 1.0 / P, SUB_EPS, s_osq, s_ors)
                rms_power(2 + 2 * l, mean, stat, rstd, NT, 1.0 / D, EPS, s_ss, s_rstd)
            own.do(nc.gpsimd.memset(below[:, :], 1.0))
            own.do(nc.gpsimd.iota(iotai[:, :], pattern=[[1, P]], base=0, channel_multiplier=0))
            own.settle()
            own.do(nc.gpsimd.memset(ones[:, :], 1.0))
            own.do(nc.gpsimd.tensor_copy(iota128[:, :], iotai[:, :]))
            own.do(nc.gpsimd.tensor_copy(iota8[:, :], iotai[:, 0:8]))
            nc.gpsimd.affine_select(out=below[:, :], in_=below[:, :], compare_op=ALU.is_gt, fill=0.0,
                                    base=0, pattern=[[1, P]], channel_multiplier=-1).then_inc(s_const, 1)
            rms_power(5, mean, stat, rstd, NT, 1.0 / D, EPS, s_ss, s_rstd)

        @block.scalar
        def _(act):
            own = Own(act, s_actc)
            xd = t["x"].rearrange("(t p) d -> p t d", p=P)
            act.dma_start(x[:, :, :], xd).then_inc(s_x0, 16)
            act.dma_start(lre[:, :, :], t["lam_re"]).then_inc(s_s5l, 16)
            act.dma_start(lim[:, :, :], t["lam_im"]).then_inc(s_s5l, 16)
            act.dma_start(gains[:, 0], t["mix_norm"]).then_inc(s_set, 16)
            act.dma_start(gains[:, 1], t["ffn_norm"]).then_inc(s_set, 16)
            act.dma_start(subg[:, :], t["subln"]).then_inc(s_set, 16)
            act.dma_start(bglu[:, :, :], t["b_glu"]).then_inc(s_set, 16)
            act.dma_start(dskip[:, :, :], t["ssm_d"]).then_inc(s_set, 16)
            act.dma_start(posi[:, :], t["positions"]).then_inc(s_set, 16)
            act.dma_start(invf[:, :], t["inv_freq"].rearrange("(o f) -> o f", o=1).to_broadcast([P, 32])).then_inc(s_set, 16)
            for g in range(2):
                act.dma_start(ldt[g * 64:(g + 1) * 64, :, :],
                              t["log_dt"][g:g + 1].to_broadcast([64, DEPTH, PAIRS])).then_inc(s_s5l, 16)
            for n, name in enumerate(("lambda_q1", "lambda_k1", "lambda_q2", "lambda_k2")):
                act.dma_start(lamv[:, n], t[name].rearrange("(o l) d -> o l d", o=1).to_broadcast([P, DEPTH, HD])).then_inc(s_set, 16)

            def load_s5(l):
                act.dma_start(Craw[:, 0], t["c_re"][l]).then_inc(s_c, 16)
                act.dma_start(Craw[:, 1], t["c_im"][l]).then_inc(s_c, 16)
                for dst, name in ((Bre, "b_re"), (Bim, "b_im")):
                    for g in range(8):
                        src = t[name][l].rearrange("(k c) s -> c k s", k=CT)[16 * g:16 * g + 16]
                        act.dma_start(dst[16 * g:16 * g + 16, :, (g % 2) * 64:(g % 2) * 64 + 64], src).then_inc(s_b, 16)

            def norm_sums(n):
                for q in range(NT):
                    i = nc.scalar.activation(outsq[:, q, :], x[:, q, :], ACT.Square, accum_out=stat[:, q:q + 1])
                    if q == NT - 1:
                        i.then_inc(s_ss, 1)

            act.wait_ge(s_x0, 16)
            norm_sums(0)
            act.wait_ge(s_bz, 1)
            load_s5(0)
            act.wait_ge(s_s5l, 64)
            nc.scalar.activation(dtt[:, :, :], ldt[:, :, :], ACT.Exp).then_inc(s_dt, 1)
            act.wait_ge(s_ang, 1)
            own.do(nc.scalar.activation(s5m[:, :, :], q1[:, :, :], ACT.Exp))
            nc.scalar.activation(lame[:, :, :], lams[:, :, :], ACT.Exp).then_inc(s_trig, 1)
            act.wait_ge(s_ang, 2)
            NA = NT * 32
            own.do(nc.scalar.activation(sinT[:, :, :], angr[:, 0:NA].rearrange("p (t f) -> p t f", t=NT), ACT.Sin))
            nc.scalar.activation(s5s[:, :, :], angr[:, NA:].rearrange("p (l q) -> p l q", l=DEPTH), ACT.Sin).then_inc(s_trig, 1)
            own.do(nc.scalar.activation(cosT[:, :, :], angk[:, 0:NA].rearrange("p (t f) -> p t f", t=NT), ACT.Sin))
            nc.scalar.activation(s5c[:, :, :], angk[:, NA:].rearrange("p (l q) -> p l q", l=DEPTH), ACT.Sin).then_inc(s_trig, 1)
            act_split(act, 0, 0)
            act_split(act, 0, 1)

            def norm_hi(l, which):
                for g in range(4):
                    n = TR_AT[l, ("h1", "h2")[which], g]
                    act.wait_ge(s_tr, n + 1)
                    for kk in range(2):
                        k = 2 * g + kk
                        i = nc.scalar.activation(hTh[:, k, :], bank(4 + n % 2)[:, kk * 256:(kk + 1) * 256], ACT.Copy,
                                                 scale=gains[:, which, l, k:k + 1])
                        if kk:
                            i.then_inc(s_thi, 1)

            for l in range(DEPTH):
                seg = 2 * l
                if l == 0:
                    act.wait_ge(s_set, 16 * 11)
                norm_hi(l, 0)
                B0 = BLOCK_COUNT * l
                for s in range(SEG):
                    if 0 <= s - 16 < HEADS:
                        h = s - 16
                        act.wait_ge(s_nb, HEADS * l + h + 1)
                        if h:
                            act.wait_ge(s_tr, TR_AT[l, "wT", h - 1] + 1)
                        for q in range(NT):
                            n, off = (q + 1) * P, q * P
                            for c in range(2):
                                src = bank(2 + c)[:, (1 - q) * 256:(1 - q) * 256 + n]
                                i = nc.scalar.activation(prob[:, c, off:off + n], src, ACT.Exp, scale=SCALE,
                                                         bias=nb[:, 2 * q + c:2 * q + c + 1],
                                                         accum_out=sm[:, 2 * q + c:2 * q + c + 1])
                        i.then_inc(s_ex, 1)
                    if 0 <= s - 18 < HEADS:
                        act.wait_ge(s_trf, TR_AT[l, "o", s - 18] + 1)
                        for q in range(NT):
                            i = nc.scalar.activation(osq[:, q * P:(q + 1) * P], osb[:, q * P:(q + 1) * P], ACT.Square,
                                                     accum_out=oss[:, q:q + 1])
                        i.then_inc(s_osq, 1)
                    split_ahead(act_split, act, seg, s)
                    if 0 <= s - 19 < HEADS:
                        h = s - 19
                        n = TR_AT[l, "oT", h]
                        act.wait_ge(s_tr, n + 1)
                        if h == 0:
                            act.wait_ge(s_rot, CHUNKS * (l + 1))
                        nc.scalar.activation(yBh[:, h, :], bank(4 + n % 2)[:, 0:256], ACT.Copy,
                                             scale=subg[:, l:l + 1]).then_inc(s_thi, 1)
                    if s == 2:
                        for q in range(2):
                            act.wait_ge(s_acc, 2 * B0 + q + 1)
                            nc.scalar.activation(uT[:, 2 * q:2 * q + 2, :],
                                                 bank(q).rearrange("p (c n) -> p c n", c=2), ACT.Copy).then_inc(s_accA, 1)
                    if s in (12, 14):
                        b = 5 + (s - 12) // 2
                        for q in range(NT):
                            act.wait_ge(s_acc, 2 * (B0 + b) + q + 1)
                            nc.scalar.activation(v[:, q, (b - 5) * 512:(b - 4) * 512],
                                                 bank(2 * PAIR_OF[b] + q), ACT.Copy).then_inc(s_accA, 1)
                    if s in (16, 18, 20, 22):
                        b = 7 + (s - 16) // 2
                        dst = gs if b < 9 else ga
                        if s == 16:
                            act.wait_ge(s_rot, CHUNKS * l + 4)
                        for q in range(NT):
                            act.wait_ge(s_acc, 2 * (B0 + b) + q + 1)
                            nc.scalar.activation(dst[:, q, ((b - 7) % 2) * 512:((b - 7) % 2 + 1) * 512],
                                                 bank(q), ACT.Tanh, scale=0.5).then_inc(s_accA, 1)
                    if s == 21:
                        act.wait_ge(s_yv, CT * (l + 1))
                        nc.scalar.activation(gel[:, :, :], uT[:, :, :], ACT.Square).then_inc(s_gsq, 1)
                        act.wait_ge(s_gin, l + 1)
                        nc.scalar.activation(gth[:, :, :], gel[:, :, :], ACT.Tanh, scale=math.sqrt(2 / math.pi)).then_inc(s_gth, 1)
                        act.wait_ge(s_yg, 2 * l + 1)
                        nc.scalar.activation(ySh[:, :, :], uT[:, :, :], ACT.Copy, scale=0.5).then_inc(s_ygh, 1)
                    if s == 23:
                        for c in range(CT):
                            act.wait_ge(s_acc, 2 * (B0 + GLU) + c // 2 + 1)
                            i = nc.scalar.activation(gth[:, c, :], bank(c // 2)[:, (c % 2) * 256:(c % 2 + 1) * 256],
                                                     ACT.Tanh, scale=0.5, bias=bglu[:, l, c:c + 1])
                            if c % 2:
                                i.then_inc(s_accA, 1)
                        act.wait_ge(s_yg, 2 * l + 2)
                        nc.scalar.activation(ySh[:, :, :], uT[:, :, :], ACT.Copy, scale=0.25).then_inc(s_ygh, 1)
                    if s == 29:
                        for g in range(4):
                            n = TR_AT[l, "mT", g]
                            act.wait_ge(s_tr, n + 1)
                            nc.scalar.activation(hTh[:, 2 * g:2 * g + 2, :],
                                                 bank(4 + n % 2).rearrange("p (k n) -> p k n", k=2), ACT.Copy,
                                                 scale=0.5).then_inc(s_thi, 1)
                act.wait_ge(s_accV, ACCV_L * (l + 1))
                norm_sums(1)
                norm_hi(l, 1)
                if l == 0:
                    load_s5(1)
                    for j in range(NJ):
                        if j < NJ - 1:
                            split_ahead(act_split, act, 1, FFN_AT["g", j + 1] - AHEAD)
                            split_ahead(act_split, act, 1, FFN_AT["u", j + 1] - AHEAD)
                        for q in range(NT):
                            act.wait_ge(s_gu, NT * j + q + 1)
                            nc.scalar.activation(sg[:, q, :], bank(6 + q)[:, 0:FB], ACT.Silu).then_inc(s_sg, 1)
                        split_ahead(act_split, act, 1, FFN_AT["d", j] - AHEAD)
                        n = TR_AT[0, "act", j]
                        act.wait_ge(s_tr, n + 1)
                        nc.scalar.activation(aTh[:, :, :], bank(4 + n % 2).rearrange("p (k n) -> p k n", k=2),
                                             ACT.Copy).then_inc(s_thi, 1)
                    for i in range(SEG - AHEAD, SEG):
                        split_ahead(act_split, act, 1, i)
                    act.wait_ge(s_xn, 3)
                    norm_sums(2)

            act.dma_start(rw[:, :, :], t["router_w"].rearrange("(c p) e -> p c e", p=P)).then_inc(s_rw, 16)
            act.dma_start(gfin[:, :], t["final_norm"].rearrange("(o d) -> o d", o=1).to_broadcast([P, D])).then_inc(s_gf, 16)
            act.wait_ge(s_lg, 1)
            nc.scalar.activation(den[:, :], ex2[:, :], ACT.Exp).then_inc(s_lg, 1)
            act.wait_ge(s_route, 1)
            rounds = act.value_load(rI[0:1, 0:1], min_val=EXPERTS, max_val=MAX_ROUNDS)
            with act.Fori(0, rounds) as r:
                for g in range(2):
                    n = TR0 + ROUND_TR.index(f"hs{g}")
                    act.wait_ge(s_tr, r * R_TR + (n + 1))
                    for kk in range(4):
                        k = 4 * g + kk
                        i = nc.scalar.activation(hsh[:, k, :], bank(4 + n % 2)[:, kk * P:(kk + 1) * P], ACT.Copy,
                                                 scale=gains[:, 1, 1, k:k + 1])
                    i.then_inc(s_thi, 1)
                act_split(act, 3, 0, r)
                act_split(act, 3, 1, r)
                for j in range(NJ):
                    if j < NJ - 1:
                        act_split(act, 3, FFN_AT["g", j + 1], r)
                        act_split(act, 3, FFN_AT["u", j + 1], r)
                    act.wait_ge(s_gu, r * NJ + (GU0 + j + 1))
                    nc.scalar.activation(sg[:, 0, :], bank(6 + j % 2)[:, 0:FB], ACT.Silu).then_inc(s_sg, 1)
                    act_split(act, 3, FFN_AT["d", j], r)
                    n = TR0 + ROUND_TR.index(f"act{j}")
                    act.wait_ge(s_tr, r * R_TR + (n + 1))
                    nc.scalar.activation(bTh[:, :, :], bank(4 + n % 2)[:, 0:256].rearrange("p (k n) -> p k n", k=2),
                                         ACT.Copy).then_inc(s_thi, 1)
                act.wait_ge(s_used, r * USED_FFN + (2 * USED_MIX + 2 * USED_FFN))
                nc.scalar.activation(ysb[:, :].rearrange("p (n c) -> p n c", n=2), PS[:, 0:2, :], ACT.Copy).then_inc(s_ysb, 1)
            act.wait_ge(s_xn, 6)
            norm_sums(3)

        @block.vector
        def _(dve):
            own = Own(dve, s_dve)
            V = nc.vector

            def norm(n):
                dve.wait_ge(s_rstd, n)
                for q in range(NT):
                    i = V.tensor_scalar(xn[:, q, :], x[:, q, :], rstd[:, q:q + 1], None, ALU.mult)
                i.then_inc(s_xn, 1)

            own.do(V.memset(Bre[:, :, :], 0.0))
            own.do(V.memset(Cre[:, :, :], 0.0))
            own.do(V.memset(Cin[:, :, :], 0.0))
            V.memset(Bim[:, :, :], 0.0).then_inc(s_bz, 1)
            dve.wait_ge(s_set, 16 * 11)
            own.do(V.tensor_tensor(lamp[:, 0], lamv[:, 0], lamv[:, 1], ALU.mult))
            own.do(V.tensor_tensor(lamp[:, 1], lamv[:, 2], lamv[:, 3], ALU.mult))
            own.settle()
            own.do(V.tensor_reduce(lams[:, :, :], lamp[:, :, :, :], AX_X, ALU.add))
            NA = NT * 32
            own.do(V.tensor_copy(posf[:, :], posi[:, :]))
            own.settle()
            for q in range(NT):
                own.do(V.tensor_scalar(ang[:, q * 32:(q + 1) * 32], invf[:, :], posf[:, q:q + 1], None, ALU.mult))
            dve.wait_ge(s_dt, 1)
            own.do(V.tensor_tensor(ang[:, NA:].rearrange("p (l q) -> p l q", l=DEPTH), lim[:, :, :], dtt[:, :, :], ALU.mult))
            V.tensor_tensor(q1[:, :, :], lre[:, :, :], dtt[:, :, :], ALU.mult).then_inc(s_ang, 1)
            own.settle()
            own.do(V.tensor_scalar(angk[:, :], ang[:, :], 1 / (2 * math.pi), ROUND, ALU.mult, ALU.add))
            own.settle()
            own.do(V.tensor_scalar(angk[:, :], angk[:, :], -ROUND, None, ALU.add))
            own.settle()
            own.do(V.scalar_tensor_tensor(angr[:, :], angk[:, :], -TWO_PI_HI, ang[:, :], ALU.mult, ALU.add))
            own.settle()
            own.do(V.scalar_tensor_tensor(angr[:, :], angk[:, :], -TWO_PI_MID, angr[:, :], ALU.mult, ALU.add))
            own.settle()
            own.do(V.scalar_tensor_tensor(angr[:, :], angk[:, :], -TWO_PI_LO, angr[:, :], ALU.mult, ALU.add))
            own.settle()
            own.do(V.tensor_scalar(angr[:, :], angr[:, :], PI_IN, -PI_IN, ALU.min, ALU.max))
            own.settle()
            own.do(V.tensor_scalar(angk[:, :], angr[:, :], -1.0, None, ALU.mult))
            own.settle()
            own.do(V.tensor_tensor(angk[:, :], angk[:, :], angr[:, :], ALU.min))
            own.settle()
            V.tensor_scalar(angk[:, :], angk[:, :], math.pi / 2, None, ALU.add).then_inc(s_ang, 1)
            norm(1)
            dve.wait_ge(s_trig, 3)
            own.do(V.tensor_tensor(nlam[:, :], lame[:, 1], lame[:, 0], ALU.subtract))
            own.do(V.tensor_scalar(nsinT[:, :, :], sinT[:, :, :], -1.0, None, ALU.mult))
            own.do(V.tensor_scalar(bglu[:, :, :], bglu[:, :, :], 0.5, None, ALU.mult))
            own.settle()
            for l in range(DEPTH):
                own.do(V.tensor_scalar(nlam[:, l:l + 1], nlam[:, l:l + 1], -lam_init(l), None, ALU.add))
                own.do(V.tensor_scalar(subg[:, l:l + 1], subg[:, l:l + 1], 1.0 - lam_init(l), None, ALU.mult))
            f = lambda a: a[:, :, :]
            own.do(V.tensor_tensor(f(q1), f(s5m), f(s5c), ALU.mult))
            own.do(V.tensor_tensor(f(q2), f(s5m), f(s5s), ALU.mult))
            own.settle()
            own.do(V.tensor_scalar(f(q1), f(q1), -1.0, None, ALU.add))
            own.do(V.tensor_tensor(f(q3), f(lre), f(lre), ALU.mult))
            own.do(V.tensor_tensor(f(q4), f(lim), f(lim), ALU.mult))
            own.settle()
            own.do(V.tensor_tensor(f(q3), f(q3), f(q4), ALU.add))
            own.settle()
            own.do(V.reciprocal(f(dtt), f(q3)))
            own.settle()
            own.do(V.tensor_tensor(f(s5fr), f(q1), f(lre), ALU.mult))
            own.do(V.tensor_tensor(f(q4), f(q2), f(lim), ALU.mult))
            own.do(V.tensor_tensor(f(s5fi), f(q2), f(lre), ALU.mult))
            own.do(V.tensor_tensor(f(q3), f(q1), f(lim), ALU.mult))
            own.settle()
            own.do(V.tensor_tensor(f(s5fr), f(s5fr), f(q4), ALU.add))
            own.do(V.tensor_tensor(f(s5fi), f(s5fi), f(q3), ALU.subtract))
            own.settle()
            own.do(V.tensor_tensor(f(s5fr), f(s5fr), f(dtt), ALU.mult))
            own.do(V.tensor_tensor(f(s5fi), f(s5fi), f(dtt), ALU.mult))
            own.settle()

            def scale_c(l):
                dve.wait_ge(s_c, 32 * (l + 1))
                fr = s5fr[:, l, :].rearrange("p (q o) -> p q o", o=1).to_broadcast([P, PAIRS, GCH])
                fi = s5fi[:, l, :].rearrange("p (q o) -> p q o", o=1).to_broadcast([P, PAIRS, GCH])
                own.do(V.tensor_tensor(Ctmp[:, 0], Craw[:, 0], fr, ALU.mult))
                own.do(V.tensor_tensor(Ctmp[:, 1], Craw[:, 1], fi, ALU.mult))
                own.settle()
                for g in range(2):
                    a, b = slice(g * 64, g * 64 + 64), slice(g * 16, g * 16 + 16)
                    own.do(V.tensor_tensor(Cre[a, :, b], Ctmp[a, 0], Ctmp[a, 1], ALU.subtract))
                own.settle()
                own.do(V.tensor_tensor(Ctmp[:, 0], Craw[:, 0], fi, ALU.mult))
                own.do(V.tensor_tensor(Ctmp[:, 1], Craw[:, 1], fr, ALU.mult))
                own.settle()
                own.do(V.tensor_scalar(Ctmp[:, 0], Ctmp[:, 0], -1.0, None, ALU.mult))
                own.settle()
                for g in range(2):
                    a, b = slice(g * 64, g * 64 + 64), slice(g * 16, g * 16 + 16)
                    i = V.tensor_tensor(Cin[a, :, b], Ctmp[a, 0], Ctmp[a, 1], ALU.subtract)
                    if g:
                        i.then_inc(s_prep, 1)

            thi = [0]

            def lo_of(dst, src, hi, scale, last=True):
                i = V.scalar_tensor_tensor(dst, src, scale, hi.bitcast(F32), ALU.mult, ALU.subtract)
                if last:
                    i.then_inc(s_trf, 1)

            def norm_lo(l, which):
                for g in range(4):
                    n = TR_AT[l, ("h1", "h2")[which], g]
                    thi[0] += 1
                    dve.wait_ge(s_thi, thi[0])
                    for kk in range(2):
                        k = 2 * g + kk
                        lo_of(hTl[:, k, :], bank(4 + n % 2)[:, kk * 256:(kk + 1) * 256], hTh[:, k, :],
                              gains[:, which, l, k:k + 1], last=bool(kk))

            def rope(l, b, q):
                blk = BLOCK_COUNT * l + b
                dve.wait_ge(s_acc, 2 * blk + q + 1)
                if b > 1 and q == 0:
                    dve.wait_ge(s_tr, TR_AT[l, "qkT", 2 * (b - 1) + 1] + 1)
                src = bank(2 * PAIR_OF[b] + q).rearrange("p (g h f) -> p g h f", g=8, h=2)
                A = ropeA if q == 0 else ropeC
                Av = A[:, :].rearrange("p (g h f) -> p g h f", g=8, h=2)
                Bv = ropeB[:, :].rearrange("p (g h f) -> p g h f", g=8, h=2)
                cs, sn, ns = cosT[:, q, :], sinT[:, q, :], nsinT[:, q, :]
                bc3 = lambda a: a.rearrange("p (g f) -> p g f", g=1).to_broadcast([P, 8, 32])
                own.do(V.tensor_tensor(Av[:, :, 0, :], src[:, :, 0, :], bc3(cs), ALU.mult))
                own.do(V.tensor_tensor(Av[:, :, 1, :], src[:, :, 1, :], bc3(cs), ALU.mult))
                own.do(V.tensor_tensor(Bv[:, :, 0, :], src[:, :, 1, :], bc3(ns), ALU.mult))
                V.tensor_tensor(Bv[:, :, 1, :], src[:, :, 0, :], bc3(sn), ALU.mult).then_inc(s_accV, 1)
                accv[0] += 1
                dve.wait_ge(s_accV, accv[0])
                V.tensor_tensor(A[:, :], A[:, :], ropeB[:, :], ALU.add).then_inc(s_rope, 1)
                rp[0] += 1
                dve.wait_ge(s_rope, rp[0])

            accv, rp = [0], [0]

            def out_block(l, b):
                pair, cs = PAIR_OF[b], slice((b % 2) * 512, (b % 2 + 1) * 512)
                for q in range(NT):
                    dve.wait_ge(s_acc, 2 * (BLOCK_COUNT * l + b) + q + 1)
                    src = bank(2 * pair + q)
                    if b < WO0:
                        g_ = gs if b < PA0 else ga
                        i = V.scalar_tensor_tensor(g_[:, q, cs], g_[:, q, cs], 1.0, src, ALU.add, ALU.mult)
                    else:
                        i = V.tensor_tensor(x[:, q, cs], x[:, q, cs], src, ALU.add)
                    i.then_inc(s_accV, 1)
                    accv[0] += 1

            scale_c(0)
            build_turns(V, own, 0, 0, wpow, tabt, s_tabd)
            dve_split(dve, 0, 0)
            dve_split(dve, 0, 1)
            for l in range(DEPTH):
                seg = 2 * l
                norm_lo(l, 0)
                B0 = BLOCK_COUNT * l
                for s in range(SEG):
                    if 0 <= s - 16 < HEADS:
                        h = s - 16
                        dve.wait_ge(s_sc, HEADS * l + h + 1)
                        own.do(V.tensor_reduce(mx[:, 0:2], PS[:, 2:4, 256:384], AX_X, ALU.max))
                        own.do(V.tensor_reduce(mx[:, 2:4], PS[:, 2:4, 0:256], AX_X, ALU.max))
                        own.settle()
                        V.tensor_scalar(nb[:, :], mx[:, :], -SCALE, None, ALU.mult).then_inc(s_nb, 1)
                    if 0 <= s - 17 < HEADS:
                        h = s - 17
                        n = TR_AT[l, "wT", h]
                        dve.wait_ge(s_tr, n + 1)
                        if h:
                            dve.wait_ge(s_tr, TR_AT[l, "o", h - 1] + 1)
                        V.tensor_copy(wT[:, :], bank(4 + n % 2)[:, 0:384]).then_inc(s_trf, 1)
                    if 0 <= s - 18 < HEADS:
                        h = s - 18
                        n = TR_AT[l, "o", h]
                        dve.wait_ge(s_tr, n + 1)
                        if h:
                            dve.wait_ge(s_tr, TR_AT[l, "oT", h - 1] + 1)
                        V.tensor_copy(osb[:, :], bank(4 + n % 2)[:, 0:256]).then_inc(s_trf, 1)
                    split_ahead(dve_split, dve, seg, s)
                    if 0 <= s - 19 < HEADS:
                        h = s - 19
                        n = TR_AT[l, "oT", h]
                        thi[0] += 1
                        dve.wait_ge(s_thi, thi[0])
                        lo_of(yBl[:, h, :], bank(4 + n % 2)[:, 0:256], yBh[:, h, :], subg[:, l:l + 1])
                    if 0 <= s - 3 < PAIRS:
                        p = s - 3
                        c, b = p // 2, (p // 2) % 2
                        dve.wait_ge(s_bu, PAIRS * l + p + 1)
                        if p == 8:
                            dve.wait_ge(s_tabp, l + 1)
                        if p % 2 == 0 and c >= 2:
                            dve.wait_ge(s_yc, CHUNKS * l + c - 1)
                        R_, I_ = rr[:, b, p % 2, :], ri[:, b, p % 2, :]
                        br, bi = bank(6)[:, 0:256], bank(6)[:, 256:512]
                        own.do(V.tensor_tensor(R_, br, tab[:, p, 0, :], ALU.mult))
                        own.do(V.tensor_tensor(t12[:, 0, :], bi, tab[:, p, 1, :], ALU.mult))
                        own.do(V.tensor_tensor(I_, bi, tab[:, p, 0, :], ALU.mult))
                        V.tensor_tensor(t12[:, 1, :], br, tab[:, p, 1, :], ALU.mult).then_inc(s_buf, 1)
                        dve.wait_ge(s_buf, PAIRS * l + p + 1)
                        own.do(V.tensor_tensor(R_, R_, t12[:, 0, :], ALU.add))
                        own.do(V.tensor_tensor(I_, I_, t12[:, 1, :], ALU.subtract))
                        own.settle()
                        m = s5m[:, l, p:p + 1].to_broadcast([P, SEQ])
                        own.do(V.tensor_tensor_scan(R_, m, R_, 0.0, ALU.mult, ALU.add))
                        i = V.tensor_tensor_scan(I_, m, I_, 0.0, ALU.mult, ALU.add)
                        if p % 2:
                            i.then_inc(s_scan, 1)
                        else:
                            own.do(i)
                    if s in (4, 6, 8, 10):
                        rope(l, (s - 2) // 2, 0)
                    if s in (5, 7, 9, 11):
                        rope(l, (s - 3) // 2, 1)
                    if s in (6, 8, 10, 12):
                        b = (s - 4) // 2
                        dst = qT if b < 3 else kT
                        for q in range(NT):
                            n = TR_AT[l, "qkT", 2 * b + q]
                            dve.wait_ge(s_tr, n + 1)
                            h0 = ((b - 1) % 2) * 4
                            V.tensor_copy(dst[:, h0:h0 + 4, q * P:(q + 1) * P],
                                          bank(4 + n % 2).rearrange("p (h n) -> p h n", h=4)).then_inc(s_trf, 1)
                    if s in (9, 13, 17, 21):
                        kt = (s - 9) // 4
                        dve.wait_ge(s_yc, CHUNKS * l + 2 * kt + 2)
                        V.scalar_tensor_tensor(uT[:, kt, :], uT[:, kt, :], dskip[:, l, kt:kt + 1],
                                               bank(7)[:, (kt % 2) * 256:(kt % 2 + 1) * 256],
                                               ALU.mult, ALU.add).then_inc(s_yv, 1)
                    if s == 21:
                        dve.wait_ge(s_gsq, l + 1)
                        own.do(V.tensor_scalar(gel[:, :, :], gel[:, :, :], 0.044715, 1.0, ALU.mult, ALU.add))
                        own.settle()
                        V.tensor_tensor(gel[:, :, :], gel[:, :, :], uT[:, :, :], ALU.mult).then_inc(s_gin, 1)
                        dve.wait_ge(s_gth, l + 1)
                        V.scalar_tensor_tensor(uT[:, :, :].rearrange("p c n -> p (c n)"), gth[:, :, :].rearrange("p c n -> p (c n)"), 1.0,
                                               uT[:, :, :].rearrange("p c n -> p (c n)"), ALU.add, ALU.mult).then_inc(s_yg, 1)
                        dve.wait_ge(s_ygh, 2 * l + 1)
                        V.scalar_tensor_tensor(ySl[:, :, :].rearrange("p c n -> p (c n)"), uT[:, :, :].rearrange("p c n -> p (c n)"), 0.5,
                                               ySh[:, :, :].rearrange("p c n -> p (c n)").bitcast(F32), ALU.mult,
                                               ALU.subtract).then_inc(s_ygl, 1)
                    if s == 23:
                        dve.wait_ge(s_accA, ACCA_L * (l + 1))
                        V.scalar_tensor_tensor(uT[:, :, :].rearrange("p c n -> p (c n)"), gth[:, :, :].rearrange("p c n -> p (c n)"), 1.0,
                                               uT[:, :, :].rearrange("p c n -> p (c n)"), ALU.add, ALU.mult).then_inc(s_yg, 1)
                        dve.wait_ge(s_ygh, 2 * l + 2)
                        V.scalar_tensor_tensor(ySl[:, :, :].rearrange("p c n -> p (c n)"), uT[:, :, :].rearrange("p c n -> p (c n)"), 0.25,
                                               ySh[:, :, :].rearrange("p c n -> p (c n)").bitcast(F32), ALU.mult,
                                               ALU.subtract).then_inc(s_ygl, 1)
                    if 0 <= s - 16 < HEADS:
                        h = s - 16
                        dve.wait_ge(s_ex, HEADS * l + h + 1)
                        own.do(V.reciprocal(rs[:, :], sm[:, :]))
                        own.settle()
                        own.do(V.tensor_scalar(c2[:, :], rs[:, 1:4:2], nlam[:, l:l + 1], None, ALU.mult))
                        own.settle()
                        for q in range(NT):
                            sl = slice(q * P, q * P + (q + 1) * P)
                            own.do(V.tensor_scalar(prob[:, 1, sl], prob[:, 1, sl], c2[:, q:q + 1], None, ALU.mult))
                        own.settle()
                        for q in range(NT):
                            sl = slice(q * P, q * P + (q + 1) * P)
                            i = V.scalar_tensor_tensor(prob[:, 0, sl], prob[:, 0, sl], rs[:, 2 * q:2 * q + 1],
                                                       prob[:, 1, sl], ALU.mult, ALU.add)
                        i.then_inc(s_w, 1)
                    if 0 <= s - 18 < HEADS:
                        h = s - 18
                        dve.wait_ge(s_ors, HEADS * l + h + 1)
                        for q in range(NT):
                            i = V.tensor_scalar(osb[:, q * P:(q + 1) * P], osb[:, q * P:(q + 1) * P], ors[:, q:q + 1],
                                                None, ALU.mult)
                        i.then_inc(s_on, 1)
                    if s in (24, 25, 27, 29, 31):
                        out_block(l, {24: 12, 25: 13, 27: 14, 29: 15, 31: 16}[s])
                    if s == 29:
                        dve.wait_ge(s_accV, accv[0])
                        for q in range(NT):
                            i = V.tensor_tensor(gs[:, q, :], gs[:, q, :], ga[:, q, :], ALU.add)
                        i.then_inc(s_m, 1)
                        for g in range(4):
                            n = TR_AT[l, "mT", g]
                            thi[0] += 1
                            dve.wait_ge(s_thi, thi[0])
                            lo_of(hTl[:, 2 * g:2 * g + 2, :].rearrange("p k n -> p (k n)"), bank(4 + n % 2),
                                  hTh[:, 2 * g:2 * g + 2, :].rearrange("p k n -> p (k n)"), 0.5)
                out_block(l, 17)
                norm(2 + 2 * l)
                norm_lo(l, 1)
                if l == 0:
                    scale_c(1)
                    build_turns(V, own, 1, 0, wpow, tabt, s_tabd)
                    for j in range(NJ):
                        if j < NJ - 1:
                            split_ahead(dve_split, dve, 1, FFN_AT["g", j + 1] - AHEAD)
                            split_ahead(dve_split, dve, 1, FFN_AT["u", j + 1] - AHEAD)
                        for q in range(NT):
                            dve.wait_ge(s_sg, NT * j + q + 1)
                            V.tensor_tensor(act_t[:, q, :], sg[:, q, :], bank(6 + q)[:, FB:2 * FB],
                                            ALU.mult).then_inc(s_act, 1)
                        split_ahead(dve_split, dve, 1, FFN_AT["d", j] - AHEAD)
                        n = TR_AT[0, "act", j]
                        thi[0] += 1
                        dve.wait_ge(s_thi, thi[0])
                        V.tensor_tensor(aTl[:, :, :].rearrange("p k n -> p (k n)"), bank(4 + n % 2),
                                        aTh[:, :, :].rearrange("p k n -> p (k n)").bitcast(F32),
                                        ALU.subtract).then_inc(s_trf, 1)
                    for i in range(SEG - AHEAD, SEG):
                        split_ahead(dve_split, dve, 1, i)
                    dve.wait_ge(s_used, USED_MIX + USED_FFN)
                    for q in range(NT):
                        for c in range(2):
                            i = V.tensor_tensor(x[:, q, c * 512:(c + 1) * 512], x[:, q, c * 512:(c + 1) * 512],
                                                bank(2 * q + c), ALU.add)
                    i.then_inc(s_xn, 1)
                    dve.wait_ge(s_xn, 3)
                    norm(3)

            n = TR_AT[1, "logits", 0]
            dve.wait_ge(s_tr, n + 1)
            V.tensor_copy(lg[:, :, :], bank(4 + n % 2)[:, 0:16].rearrange("p (t e) -> p t e", t=NT)).then_inc(s_trf, 1)
            dve.wait_ge(s_trf, n + 1)
            for q in range(NT):
                own.do(V.max(top[:, q, :], lg[:, q, :]))
            own.settle()
            for q in range(NT):
                own.do(V.max_index(topi[:, q, :], top[:, q, :], lg[:, q, :]))
            own.settle()
            own.do(V.tensor_copy(topf[:, :, :], topi[:, :, :]))
            V.tensor_tensor(ex2[:, :], top[:, :, 1], top[:, :, 0], ALU.subtract).then_inc(s_lg, 1)
            own.settle()
            dve.wait_ge(s_const, 2)
            for q in range(NT):
                own.do(V.tensor_scalar(oh1[:, q, :], iota8[:, :], topf[:, q, 0:1], None, ALU.is_equal))
                own.do(V.tensor_scalar(oh2[:, q, :], iota8[:, :], topf[:, q, 1:2], None, ALU.is_equal))
            own.settle()
            V.tensor_tensor(M[:, :, :], oh1[:, :, :], oh2[:, :, :], ALU.add).then_inc(s_M, 1)
            dve.wait_ge(s_lg, 2)
            own.do(V.tensor_scalar(g1[:, :], den[:, :], 1.0, None, ALU.add))
            own.settle()
            own.do(V.reciprocal(g1[:, :], g1[:, :]))
            own.settle()
            own.do(V.tensor_tensor(g2[:, :], g1[:, :], den[:, :], ALU.mult))
            own.settle()
            for q in range(NT):
                own.do(V.tensor_scalar(oh1[:, q, :], oh1[:, q, :], g1[:, q:q + 1], None, ALU.mult))
                own.do(V.tensor_scalar(oh2[:, q, :], oh2[:, q, :], g2[:, q:q + 1], None, ALU.mult))
            own.settle()
            own.do(V.tensor_tensor(G[:, :, :], oh1[:, :, :], oh2[:, :, :], ALU.add))
            n = TR_AT[1, "places", 0]
            dve.wait_ge(s_tr, n + 1)
            own.do(V.scalar_tensor_tensor(placed[:, :, :].rearrange("p t e -> p (t e)"), bank(4 + n % 2)[:, 0:16], 1.0,
                                          M[:, :, :].rearrange("p t e -> p (t e)"), ALU.add, ALU.mult))
            V.tensor_copy(cnt[:, :], bank(4 + n % 2)[:, 16:24]).then_inc(s_trf, 1)
            dve.wait_ge(s_trf, n + 1)
            own.do(V.tensor_scalar(over[:, :], cnt[:, :], float(P), None, ALU.is_gt))
            own.settle()
            own.do(V.tensor_tensor_scan(overc[:, :], ones[:, 0:8], over[:, :], 0.0, ALU.mult, ALU.add))
            own.settle()
            own.do(V.tensor_scalar(rF[:, :], overc[:, 7:8], float(EXPERTS), None, ALU.add))
            for k in range(3):
                own.do(V.tensor_scalar(ohr[:, k, :], overc[:, :], float(k + 1), None, ALU.is_equal))
            own.settle()
            for k in range(3):
                own.do(V.tensor_tensor(ohr[:, k, :], ohr[:, k, :], over[:, :], ALU.mult))
            own.do(V.memset(eF[:, 8:12], 0.0))
            own.do(V.tensor_copy(eF[:, 0:8], iota8[:, :]))
            for q in range(NT):
                own.do(V.tensor_scalar(placeR[:, q, 0:8], placed[:, q, :], -1.0, None, ALU.add))
                own.do(V.tensor_copy(gateR[:, q, 0:8], G[:, q, :]))
            own.settle()
            for k in range(3):
                for src, dst in ([(iota8[:, :], eF[:, 8 + k:9 + k])]
                                 + [(placed[:, q, :], placeR[:, q, 8 + k:9 + k]) for q in range(NT)]
                                 + [(G[:, q, :], gateR[:, q, 8 + k:9 + k]) for q in range(NT)]):
                    own.do(V.tensor_tensor(prod[:, :], ohr[:, k, :], src, ALU.mult))
                    own.settle()
                    own.do(V.tensor_reduce(dst, prod[:, :], AX_X, ALU.add))
                    own.settle()
            for q in range(NT):
                own.do(V.tensor_scalar(placeR[:, q, 8:11], placeR[:, q, 8:11], -1.0 - P, None, ALU.add))
            own.do(V.tensor_copy(eI[:, :], eF[:, :]))
            own.settle()
            V.tensor_copy(rI[:, :], rF[:, :]).then_inc(s_route, 1)
            dve.wait_ge(s_route, 1)
            rounds = dve.value_load(rI[0:1, 0:1], min_val=EXPERTS, max_val=MAX_ROUNDS)
            own.per = 3
            base = own.n
            THI0 = thi[0]
            with dve.Fori(0, rounds) as r:
                own.r = r
                own.do(V.tensor_copy(pcol[:, :], placeR[:, :, bass.ds(r, 1)].rearrange("p t o -> p (t o)")))
                own.do(V.tensor_copy(gcol[:, :], gateR[:, :, bass.ds(r, 1)].rearrange("p t o -> p (t o)")))
                own.settle()
                for q in range(NT):
                    i = V.tensor_scalar(S[:, q, :], iota128[:, :], pcol[:, q:q + 1], None, ALU.is_equal)
                    if q:
                        i.then_inc(s_S, 1)
                    else:
                        own.do(i)
                for g in range(2):
                    n = TR0 + ROUND_TR.index(f"hs{g}")
                    dve.wait_ge(s_thi, r * (2 + NJ) + (THI0 + g + 1))
                    for kk in range(4):
                        k = 4 * g + kk
                        lo_of(hsl[:, k, :], bank(4 + n % 2)[:, kk * P:(kk + 1) * P], hsh[:, k, :],
                              gains[:, 1, 1, k:k + 1], last=(kk == 3))
                n = TR0 + ROUND_TR.index("ST")
                dve.wait_ge(s_tr, r * R_TR + (n + 1))
                V.tensor_copy(ST[:, :], bank(4 + n % 2)[:, 0:256]).then_inc(s_trf, 1)
                dve_split(dve, 3, 0, r)
                dve_split(dve, 3, 1, r)
                for j in range(NJ):
                    if j < NJ - 1:
                        dve_split(dve, 3, FFN_AT["g", j + 1], r)
                        dve_split(dve, 3, FFN_AT["u", j + 1], r)
                    dve.wait_ge(s_sg, r * NJ + (GU0 + j + 1))
                    V.tensor_tensor(act_t[:, 0, :], sg[:, 0, :], bank(6 + j % 2)[:, FB:2 * FB], ALU.mult).then_inc(s_act, 1)
                    dve_split(dve, 3, FFN_AT["d", j], r)
                    n = TR0 + ROUND_TR.index(f"act{j}")
                    dve.wait_ge(s_thi, r * (2 + NJ) + (THI0 + 2 + j + 1))
                    V.tensor_tensor(bTl[:, :, :].rearrange("p k n -> p (k n)"), bank(4 + n % 2)[:, 0:256],
                                    bTh[:, :, :].rearrange("p k n -> p (k n)").bitcast(F32), ALU.subtract).then_inc(s_trf, 1)
                for q in range(NT):
                    for c in range(2):
                        dve.wait_ge(s_scat, r * 4 + (2 * q + c + 1))
                        V.scalar_tensor_tensor(x[:, q, c * 512:(c + 1) * 512], bank(2 + c), gcol[:, q:q + 1],
                                               x[:, q, c * 512:(c + 1) * 512], ALU.mult, ALU.add).then_inc(s_scatv, 1)
                dve.wait_ge(s_scatv, r * 4 + 4)
            assert own.n - base == own.per
            V.tensor_copy(pcol[:, 0:1], rF[:, :]).then_inc(s_xn, 1)
            dve.wait_ge(s_gf, 16)
            dve.wait_ge(s_rstd, 5)
            for q in range(NT):
                V.scalar_tensor_tensor(outt[:, q, :], x[:, q, :], rstd[:, q:q + 1], gfin[:, :], ALU.mult,
                                       ALU.mult).then_inc(s_fin, 1)

        @block.tensor
        def _(pe):
            mm = nc.tensor.matmul

            def mm3(out, lh, ll, rh, rl, start, stop):
                mm(out, lh, rh, start=start, stop=False)
                mm(out, ll, rh, start=False, stop=False)
                return mm(out, lh, rl, start=False, stop=stop)

            def tr_bank(n):
                if n >= 2:
                    pe.wait_ge(s_trf, n - 1)
                return bank(4 + n % 2)

            def tr_bank_r(r, name):
                n = TR0 + ROUND_TR.index(name)
                pe.wait_ge(s_trf, r * R_TR + (n - 1))
                return bank(4 + n % 2)

            def transposes(dst, srcs):
                for k, s in enumerate(srcs):
                    i = nc.tensor.transpose(dst[:, k * P:(k + 1) * P], s, ident[:, :])
                i.then_inc(s_tr, 1)

            def to_T(l, name, src):
                for g in range(4):
                    transposes(tr_bank(TR_AT[l, name, g]),
                               [src[:, q, k * P:(k + 1) * P] for k in (2 * g, 2 * g + 1) for q in range(NT)])

            def tail(l, s):
                for what, h in mixer_tail(s):
                    if what == "scores":
                        if h == 0:
                            acc_free(l, 5)
                            pe.wait_ge(s_trf, TR_AT[l, "qkT", 9] + 1)
                        else:
                            pe.wait_ge(s_ex, HEADS * l + h)
                        for c in range(2):
                            for q in (1, 0):
                                n, off = (q + 1) * P, (1 - q) * 256
                                mm(bank(2 + c)[:, off:off + n], qT[c * 64:(c + 1) * 64, h, q * P:(q + 1) * P],
                                   kT[c * 64:(c + 1) * 64, h, 0:n], start=(q == 1), stop=False)
                                i = mm(bank(2 + c)[:, off + q * P:off + n], identb[:, :], maskb[:, :],
                                       start=False, stop=(q == 0))
                        i.then_inc(s_sc, 1)
                    elif what == "wT":
                        b = tr_bank(TR_AT[l, "wT", h])
                        pe.wait_ge(s_w, HEADS * l + h + 1)
                        transposes(b, [prob[:, 0, k * P:(k + 1) * P] for k in range(3)])
                    elif what == "o":
                        b = tr_bank(TR_AT[l, "o", h])
                        pe.wait_ge(s_trf, TR_AT[l, "wT", h] + 1)
                        if h == 0:
                            pe.wait_ge(s_accA, ACCA_L * l + 6)
                        vh = [v[:, q, h * P:(h + 1) * P] for q in range(NT)]
                        mm(b[:, 0:P], wT[:, 0:P], vh[0], start=True, stop=False)
                        mm(b[:, P:2 * P], wT[:, P:2 * P], vh[0], start=False, stop=False)
                        mm(b[:, P:2 * P], wT[:, 2 * P:3 * P], vh[1], start=False, stop=True).then_inc(s_tr, 1)
                    elif what == "oT":
                        b = tr_bank(TR_AT[l, "oT", h])
                        pe.wait_ge(s_on, HEADS * l + h + 1)
                        transposes(b, [osb[:, q * P:(q + 1) * P] for q in range(NT)])
                    elif what == "qkT":
                        for q in range(NT):
                            b = tr_bank(TR_AT[l, "qkT", 2 * h + q])
                            pe.wait_ge(s_rope, 8 * l + 2 * (h - 1) + q + 1)
                            src = ropeA if q == 0 else ropeC
                            transposes(b, [src[:, k * P:(k + 1) * P] for k in range(4)])
                    elif what == "bu":
                        kt, q = h // 4, h % 4
                        if h == 0:
                            pe.wait_ge(s_accA, ACCA_L * l + 2)
                            pe.wait_ge(s_b, 256 * (l + 1))
                        if h or l:
                            pe.wait_ge(s_buf, PAIRS * l + h)
                        rows = slice(32 * q, 32 * q + 32)
                        mm(bank(6)[:, 0:256], Bre[rows, kt, :], uT[rows, kt, :], start=True, stop=False)
                        mm(bank(6)[:, 256:512], Bim[rows, kt, :], uT[rows, kt, :], start=False, stop=True).then_inc(s_bu, 1)
                    elif what == "y":
                        pe.wait_ge(s_rot, CHUNKS * l + h + 1)
                        kt = h // 2
                        if h == 0:
                            pe.wait_ge(s_prep, l + 1)
                        if kt >= 2:
                            pe.wait_ge(s_yv, CT * l + kt - 1)
                        for k in range(2):
                            p = 2 * h + k
                            q = p % 4
                            o = PS[32 * q:32 * q + 32, 7, (kt % 2) * 256:(kt % 2 + 1) * 256]
                            mm(o, Cre[:, p, :], sr[:, h % 2, k, :], start=True, stop=False)
                            i = mm(o, Cin[:, p, :], ri[:, h % 2, k, :], start=False, stop=True)
                        i.then_inc(s_yc, 1)

            def acc_free(l, b):
                if b in EVAC_BY_ACT:
                    pe.wait_ge(s_accA, ACCA_L * l + 2 * sum(1 for k in range(b + 1) if k in EVAC_BY_ACT))
                else:
                    pe.wait_ge(s_accV, ACCV_L * l + 2 * sum(1 for k in range(b + 1) if k not in EVAC_BY_ACT))

            pe.wait_ge(s_const, 1)
            for l in range(DEPTH):
                seg = 2 * l
                pe.wait_ge(s_xn, 1 if l == 0 else 4)
                to_T(l, "h1", xn)
                pe.wait_ge(s_trf, TR_AT[l, "h1", 3] + 1)
                for s in range(SEG):
                    blk, h, nh = slot_block(s)
                    pair = PAIR_OF[blk]
                    if h == 0:
                        before = [k for k in range(blk) if PAIR_OF[k] == pair]
                        if before:
                            acc_free(l, before[-1])
                        if blk == PS0 + 1:
                            pe.wait_ge(s_ex, HEADS * (l + 1))
                    if blk == GLU:
                        pe.wait_ge(s_ygl, 2 * l + 1)
                    if blk == PS0:
                        pe.wait_ge(s_ygl, 2 * l + 2)
                    if blk == PA0:
                        pe.wait_ge(s_trf, TR_AT[l, "oT", 3 + 4 * h] + 1)
                    if blk == WO0 and h == 0:
                        pe.wait_ge(s_trf, TR_AT[l, "mT", 3] + 1)
                    pe.wait_ge(s_lo, nslot(seg, s) + 1)
                    H, L = whv(s, 4), wlv(s, 4)
                    if blk in (U_BLOCK, GLU):
                        ah, al = (hTh, hTl) if blk == U_BLOCK else (ySh, ySl)
                        for c in range(CT):
                            o = bank(2 * pair + c // 2)[:, (c % 2) * 256:(c % 2 + 1) * 256]
                            for kk in range(4):
                                k = 4 * h + kk
                                cs = slice(c * P, (c + 1) * P)
                                i = mm3(o, H[:, kk, cs], L[:, kk, cs], ah[:, k, :], al[:, k, :],
                                        start=(k == 0 and c % 2 == 0), stop=(kk == 3 and h == nh - 1 and c % 2 == 1))
                            if h == nh - 1 and c % 2:
                                i.then_inc(s_acc, 1)
                            elif h < nh - 1 and c == CT - 1:
                                i.then_inc(s_used, 1)
                    else:
                        ah, al = ((ySh, ySl) if blk in (PS0, PS0 + 1) else (yBh, yBl) if blk in (PA0, PA0 + 1)
                                  else (hTh, hTl))
                        for q in range(NT):
                            o = bank(2 * pair + q)
                            for kk in range(4):
                                k = 4 * h + kk
                                tk = slice(q * P, (q + 1) * P)
                                i = mm3(o, ah[:, k, tk], al[:, k, tk], H[:, kk, :], L[:, kk, :],
                                        start=(k == 0), stop=(kk == 3 and h == nh - 1))
                            if h == nh - 1:
                                i.then_inc(s_acc, 1)
                            elif q == NT - 1:
                                i.then_inc(s_used, 1)
                    tail(l, s)
                    if s == 28:
                        pe.wait_ge(s_m, l + 1)
                        to_T(l, "mT", gs)
                pe.wait_ge(s_xn, 2 + 3 * l)
                to_T(l, "h2", xn)
                pe.wait_ge(s_trf, TR_AT[l, "h2", 3] + 1)
                if l == 0:
                    def gate_up2(j):
                        ig, iu = FFN_AT["g", j], FFN_AT["u", j]
                        for q in range(NT):
                            tk = slice(q * P, (q + 1) * P)
                            if j:
                                pe.wait_ge(s_act, NT * (j - 1) + q + 1)
                            for n, i_ in enumerate((ig, iu)):
                                if q == 0:
                                    pe.wait_ge(s_lo, nslot(1, i_) + 1)
                                H, L = whv(i_, KD), wlv(i_, KD)
                                for k in range(KD):
                                    i = mm3(bank(6 + q)[:, n * FB:(n + 1) * FB], hTh[:, k, tk], hTl[:, k, tk],
                                            H[:, k, :], L[:, k, :], start=(k == 0 and n == 0), stop=(k == KD - 1 and n == 1))
                                if n == 0 and q == NT - 1:
                                    i.then_inc(s_used, 1)
                            i.then_inc(s_gu, 1)

                    gate_up2(0)
                    for j in range(NJ):
                        if j < NJ - 1:
                            gate_up2(j + 1)
                        b = tr_bank(TR_AT[0, "act", j])
                        pe.wait_ge(s_act, NT * (j + 1))
                        transposes(b, [act_t[:, q, k * P:(k + 1) * P] for k in range(2) for q in range(NT)])
                        i_ = FFN_AT["d", j]
                        pe.wait_ge(s_trf, TR_AT[0, "act", j] + 1)
                        pe.wait_ge(s_lo, nslot(1, i_) + 1)
                        H, L = whv(i_, 2), wlv(i_, 2)
                        for q in range(NT):
                            for c in range(2):
                                for k in range(2):
                                    i = mm3(bank(2 * q + c), aTh[:, k, q * P:(q + 1) * P], aTl[:, k, q * P:(q + 1) * P],
                                            H[:, k, c * 512:(c + 1) * 512], L[:, k, c * 512:(c + 1) * 512],
                                            start=(j == 0 and k == 0), stop=(j == NJ - 1 and k == 1))
                        i.then_inc(s_used, 1)

            pe.wait_ge(s_rw, 16)
            b = tr_bank(TR_AT[1, "logits", 0])
            for q in range(NT):
                for k in range(KD):
                    for n, a in enumerate((hTh, hTl)):
                        i = mm(b[:, q * 8:(q + 1) * 8], a[:, k, q * P:(q + 1) * P].bitcast(F32), rw[:, k, :],
                               start=(q == 0 and k == 0 and n == 0), stop=(q == 1 and k == KD - 1 and n == 1))
            i.then_inc(s_tr, 1)
            b = tr_bank(TR_AT[1, "places", 0])
            pe.wait_ge(s_M, 1)
            mm(b[:, 0:8], below[:, :], M[:, 0, :], start=True, stop=False)
            mm(b[:, 8:16], ones[:, :], M[:, 0, :], start=False, stop=False)
            mm(b[:, 8:16], below[:, :], M[:, 1, :], start=False, stop=False)
            mm(b[:, 16:24], ones[:, :], M[:, 0, :], start=False, stop=False)
            mm(b[:, 16:24], ones[:, :], M[:, 1, :], start=False, stop=True).then_inc(s_tr, 1)
            pe.wait_ge(s_route, 1)
            rounds = pe.value_load(rI[0:1, 0:1], min_val=EXPERTS, max_val=MAX_ROUNDS)
            with pe.Fori(0, rounds) as r:
                pe.wait_ge(s_S, r + 1)
                for g in range(2):
                    b = tr_bank_r(r, f"hs{g}")
                    for kk in range(4):
                        k = 4 * g + kk
                        for q in range(NT):
                            i = mm(b[:, kk * P:(kk + 1) * P], xn[:, q, k * P:(k + 1) * P], S[:, q, :],
                                   start=(kk == 0 and q == 0), stop=(kk == 3 and q == 1))
                    i.then_inc(s_tr, 1)
                b = tr_bank_r(r, "ST")
                transposes(b, [S[:, q, :] for q in range(NT)])
                pe.wait_ge(s_trf, r * R_TR + (TR0 + 3))

                def gate_up1(j):
                    if j >= 2:
                        pe.wait_ge(s_act, r * NJ + (GU0 + j - 1))
                    for n, kind in enumerate("gu"):
                        i_ = FFN_AT[kind, j]
                        pe.wait_ge(s_lo, nslot(3, i_, r) + 1)
                        H, L = whv(i_, KD), wlv(i_, KD)
                        for k in range(KD):
                            i = mm3(bank(6 + j % 2)[:, n * FB:(n + 1) * FB], hsh[:, k, :], hsl[:, k, :],
                                    H[:, k, :], L[:, k, :], start=(k == 0 and n == 0), stop=(k == KD - 1 and n == 1))
                        i.then_inc(s_gu if n else s_used, 1)

                gate_up1(0)
                for j in range(NJ):
                    if j < NJ - 1:
                        gate_up1(j + 1)
                    b = tr_bank_r(r, f"act{j}")
                    pe.wait_ge(s_act, r * NJ + (GU0 + j + 1))
                    transposes(b, [act_t[:, 0, k * P:(k + 1) * P] for k in range(2)])
                    i_ = FFN_AT["d", j]
                    pe.wait_ge(s_lo, nslot(3, i_, r) + 1)
                    pe.wait_ge(s_trf, r * R_TR + (TR0 + ROUND_TR.index(f"act{j}") + 1))
                    H, L = whv(i_, 2), wlv(i_, 2)
                    for c in range(2):
                        for k in range(2):
                            last = mm3(bank(c), bTh[:, k, :], bTl[:, k, :], H[:, k, c * 512:(c + 1) * 512],
                                       L[:, k, c * 512:(c + 1) * 512], start=(j == 0 and k == 0),
                                       stop=(j == NJ - 1 and k == 1))
                    last.then_inc(s_used, 1)
                pe.wait_ge(s_ysb, r + 1)
                for q in range(NT):
                    for c in range(2):
                        if q:
                            pe.wait_ge(s_scatv, r * 4 + (c + 1))
                        mm(bank(2 + c), ST[:, q * P:(q + 1) * P], ysb[:, c * 512:(c + 1) * 512],
                           start=True, stop=True).then_inc(s_scat, 1)


INPUTS = {
    "x": lambda a: a["x"].reshape(SEQ, D),
    "positions": lambda a: a["positions"].reshape(NT, P).transpose(1, 0),
    "mix_norm": lambda a: a["mix_norm"].reshape(DEPTH, KD, P).transpose(2, 0, 1),
    "ffn_norm": lambda a: a["ffn_norm"].reshape(DEPTH, KD, P).transpose(2, 0, 1),
    "subln": lambda a: a["subln"].transpose(1, 0),
    "b_glu": lambda a: a["b_glu"].reshape(DEPTH, CT, P).transpose(2, 0, 1),
    "ssm_d": lambda a: a["ssm_d"].reshape(DEPTH, CT, P).transpose(2, 0, 1),
    "lam_re": lambda a: a["ssm_lambda_re"].reshape(DEPTH, PAIRS, P).transpose(2, 0, 1),
    "lam_im": lambda a: a["ssm_lambda_im"].reshape(DEPTH, PAIRS, P).transpose(2, 0, 1),
    "log_dt": lambda a: a["ssm_log_dt"].reshape(DEPTH, PAIRS, 2).transpose(2, 0, 1),
    "b_re": lambda a: a["ssm_b_re"].transpose(0, 1, 3, 2).reshape(DEPTH, SSM_W, STATE),
    "b_im": lambda a: a["ssm_b_im"].transpose(0, 1, 3, 2).reshape(DEPTH, SSM_W, STATE),
    "c_re": lambda a: a["ssm_c_re"].reshape(DEPTH, PAIRS, 2, GCH, STATE).transpose(0, 2, 4, 1, 3).reshape(DEPTH, P, PAIRS, GCH),
    "c_im": lambda a: a["ssm_c_im"].reshape(DEPTH, PAIRS, 2, GCH, STATE).transpose(0, 2, 4, 1, 3).reshape(DEPTH, P, PAIRS, GCH),
    "inv_freq": lambda a: (10000.0 ** (-np.arange(0, HD, 2, dtype=np.float32) / HD)).astype(np.float32),
    "router_w": lambda a: a["router_w"].reshape(D, EXPERTS),
    "moe_w_gate": lambda a: a["moe_w_gate"].reshape(EXPERTS, D, FF),
    "moe_w_up": lambda a: a["moe_w_up"].reshape(EXPERTS, D, FF),
    "moe_w_down": lambda a: a["moe_w_down"].reshape(EXPERTS, FF, D),
}
for _n in ("w_in", "w_glu", "w_proj_ssm", "w_proj_attn", "w_out", "lambda_q1", "lambda_k1", "lambda_q2", "lambda_k2",
           "dense_w_gate", "dense_w_up", "dense_w_down", "final_norm"):
    INPUTS[_n] = (lambda n: lambda a: a[n])(_n)


def kernel(**inputs):
    import concourse.bacc as bacc
    from concourse.bass_utils import run_bass_kernel_spmd

    nc = bacc.Bacc("TRN2", target_bir_lowering=False, num_devices=1)
    arrays, t = {}, {}
    given = {k: np.asarray(v) for k, v in inputs.items()}
    for name, lay in INPUTS.items():
        a = np.ascontiguousarray(lay(given))
        arrays[f"in_{name}"] = a
        t[name] = nc.dram_tensor(f"in_{name}", a.shape, mybir.dt.from_np(a.dtype), kind="ExternalInput").ap()
    t["out"] = nc.dram_tensor("out_trunk", (SEQ, D), F32, kind="ExternalOutput").ap()
    trunk(nc, t)
    r = run_bass_kernel_spmd(nc, [arrays], core_ids=[0])
    return r.results[0]["out_trunk"].reshape(1, SEQ, D)
```

```python
import math
from contextlib import ExitStack

import numpy as np

import concourse.bass as bass
from concourse import mybir

F32 = mybir.dt.float32
F32R = mybir.dt.float32r
BF16 = mybir.dt.bfloat16
I32 = mybir.dt.int32
U32 = mybir.dt.uint32
ALU = mybir.AluOpType
ACT = mybir.ActivationFunctionType
AX_X = mybir.AxisListType.X

P = 128
SEQ, D, DEPTH = 256, 1024, 2
NT = SEQ // P
KD = D // P
GROUPS, GCH, STATE = 32, 16, 64
PAIRS = GROUPS * STATE // P
SSM_W = GROUPS * GCH
CT = SSM_W // P
CHUNKS = PAIRS // 2
HEADS, HD = 8, 64
SCALE = HD ** -0.5
FF, EXPERTS = 2816, 8
FB = 256
NJ = FF // FB
EPS, SUB_EPS = 1e-6, 1e-5
PROLOGUE = 0
NEG = -1.0e30
MAX_ROUNDS = EXPERTS + 3
TWO_PI_HI, TWO_PI_MID = 6.28125, 0.0019350051879882812
TWO_PI_LO = 2 * math.pi - TWO_PI_HI - TWO_PI_MID
ROUND = 12582912.0
PI_IN = 3.1415925

SLOT = 2048
SEG = 33
NRAW, NW, AHEAD = 4, 3, 2
RAW_POS = [i % 4 if i < 24 else (i - 24) % 3 for i in range(SEG)]
RAW_USES = [RAW_POS.count(p) for p in range(NRAW)]
GROUP_BLOCK = 512
BLOCK_COUNT = 18
U_BLOCK, GLU, PS0, PA0, WO0 = 0, 11, 12, 14, 16
PAIR_OF = [0, 1, 0, 1, 0, 1, 0, 0, 0, 0, 0, 0, 0, 1, 0, 1, 0, 1]
EVAC_BY_ACT = {0, 5, 6, 7, 8, 9, 10, 11}
ACCA_L = 2 * len(EVAC_BY_ACT)
ACCV_L = 2 * (BLOCK_COUNT - len(EVAC_BY_ACT))


def slot_block(i):
    if i < 22:
        return i // 2, i % 2, 2
    if i < 25:
        return i - 22 + GLU, 0, 1
    return PA0 + (i - 25) // 2, (i - 25) % 2, 2


def lam_init(l):
    return 0.8 - 0.6 * math.exp(-0.3 * l)


FFN_SLOTS = [("g", 0), ("u", 0)]
for _j in range(NJ - 1):
    FFN_SLOTS += [("g", _j + 1), ("u", _j + 1), ("d", _j)]
FFN_SLOTS += [("d", NJ - 1)]
FFN_AT = {what: i for i, what in enumerate(FFN_SLOTS)}

ROUND_SLOTS = [("g", 0), ("u", 0), ("g", 1), ("u", 1)]
for _j in range(NJ - 2):
    ROUND_SLOTS += [("g", _j + 2), ("d", _j), ("u", _j + 2)]
ROUND_SLOTS += [("d", NJ - 2), ("d", NJ - 1)]
ROUND_AT = {what: i for i, what in enumerate(ROUND_SLOTS)}
NR, RAHEAD = 5, 3
ROUND_POS = [i % 5 if i < 25 else (i - 25) % 4 for i in range(SEG)]
ROUND_USES = [ROUND_POS.count(p) for p in range(NR)]


def before_in(pos, i):
    for back in range(i - 1, i - 1 - SEG, -1):
        if pos[back % SEG] == pos[i]:
            return back


def mixer_tail(s):
    todo = []
    if 0 <= s - 15 < HEADS:
        todo.append(("scores", s - 15))
    if 0 <= s - 16 < HEADS:
        todo.append(("wT", s - 16))
    if 0 <= s - 17 < HEADS:
        todo.append(("o", s - 17))
    if 0 <= s - 18 < HEADS:
        todo.append(("oT", s - 18))
    if s in (5, 7, 9, 11):
        todo.append(("qkT", (s - 3) // 2))
    if 0 <= s - 2 < PAIRS:
        todo.append(("bu", s - 2))
    if s >= 6 and (s - 6) % 2 == 0 and (s - 6) // 2 < CHUNKS:
        todo.append(("y", (s - 6) // 2))
    return todo


TR = []
for _l in range(DEPTH):
    TR += [(_l, "h1", g) for g in range(4)]
    for _s in range(SEG):
        for _w, _h in mixer_tail(_s):
            if _w in ("wT", "o", "oT"):
                TR.append((_l, _w, _h))
            if _w == "qkT":
                TR += [(_l, "qkT", 2 * _h), (_l, "qkT", 2 * _h + 1)]
        if _s == 28:
            TR += [(_l, "mT", g) for g in range(4)]
    TR += [(_l, "h2", g) for g in range(4)]
    TR += [(_l, "act", j) for j in range(NJ)] if _l == 0 else [(1, "logits", 0), (1, "places", 0),
                                                                    (1, "hs", 0), (1, "hs", 1)]
TR_AT = {what: n for n, what in enumerate(TR)}
ROUND_TR = ["ST"] + [f"act{j}" for j in range(NJ - 1)] + ["hs0", f"act{NJ - 1}", "hs1"]


def trunk(nc, t):
    ctx = ExitStack()
    with ctx:
        here = [(nc.sbuf_base + 63) // 64 * 64]

        def at(name, shape, dt, addr):
            return nc.alloc_sbuf_tensor_at(name, list(shape), dt, offset=addr)

        def size(shape, dt):
            n = 2 if dt == BF16 else 4
            for s in shape[1:]:
                n *= s
            return (n + 31) // 32 * 32

        def sb(name, shape, dt=F32):
            a = here[0]
            here[0] += size(shape, dt)
            return at(name, shape, dt, a)

        def room(nbytes):
            a = here[0]
            here[0] += nbytes
            return a

        def sem(name):
            return ctx.enter_context(nc.semaphore(name))

        x = sb("x_tok", [P, NT, D])
        hTh = sb("hT_hi", [P, KD, SEQ], F32R)
        hTl = sb("hT_lo", [P, KD, SEQ], F32R)
        raw = sb("w_raw", [P, NRAW, SLOT])
        wh = sb("w_hi", [P, NW, SLOT], F32R)
        wl = sb("w_lo", [P, NW, SLOT], F32R)
        ident = sb("ident", [P, P])
        identb = sb("identb", [P, P], BF16)
        maskb = sb("maskb", [P, P], BF16)
        cosT = sb("rope_cos", [P, NT, 32])
        sinT = sb("rope_sin", [P, NT, 32])
        nsinT = sb("rope_nsin", [P, NT, 32])
        gains = sb("gains", [P, 2, DEPTH, KD])
        subg = sb("subln_gain", [P, DEPTH])
        bglu = sb("half_b_glu", [P, DEPTH, CT])
        dskip = sb("ssm_d", [P, DEPTH, CT])
        nlam = sb("minus_lambda", [P, DEPTH])
        mhalf = sb("minus_half", [P, 4])
        s5m = sb("s5_mag", [P, DEPTH, PAIRS])
        s5c = sb("s5_cos", [P, DEPTH, PAIRS])
        s5s = sb("s5_sin", [P, DEPTH, PAIRS])
        s5fr = sb("s5_fr", [P, DEPTH, PAIRS])
        s5fi = sb("s5_fi", [P, DEPTH, PAIRS])
        stat = sb("norm_stat", [P, 4])
        mean = sb("norm_mean", [P, 4])
        rstd = sb("norm_rstd", [P, 4])
        mx = sb("score_max", [P, 4])
        nb = sb("exp_bias", [P, 4])
        sm = sb("exp_sum", [P, 4])
        rs = sb("exp_rsum", [P, 4])
        c2 = sb("second_map_coef", [P, 2])
        oss = sb("o_stat", [P, 2])
        oms = sb("o_mean", [P, 2])
        ors = sb("o_rstd", [P, 2])
        wpow = sb("turn_dve", [P, 8, 4])
        wpowp = sb("turn_pool", [P, 8, 4])

        a_q, a_k, a_v = room(8192), room(8192), room(8192)
        a_u, a_yh, a_yl = room(4096), room(4096), room(4096)
        a_tab = room(32768)
        a_rr, a_ri, a_sr, a_tt, a_t12 = room(4096), room(4096), room(4096), room(2048), room(2048)
        a_att = room(6144)
        qT = at("qT", [P, HEADS, SEQ], F32, a_q)
        kT = at("kT", [P, HEADS, SEQ], F32, a_k)
        v = at("v_tok", [P, NT, D], F32, a_v)
        outsq = at("square_out", [P, NT, D], F32, a_q)
        xn = at("x_normed", [P, NT, D], F32, a_v)
        uT = at("uT", [P, CT, SEQ], F32, a_u)
        ySh = at("yS_hi", [P, CT, SEQ], F32R, a_yh)
        ySl = at("yS_lo", [P, CT, SEQ], F32R, a_yl)
        tab = at("s5_turns", [P, PAIRS, 2, SEQ], F32, a_tab)
        gs = at("gate_ssm", [P, NT, D], F32, a_tab)
        ga = at("gate_attn", [P, NT, D], F32, a_tab + 8192)
        yBh = at("yB_hi", [P, KD, SEQ], F32R, a_tab + 16384)
        yBl = at("yB_lo", [P, KD, SEQ], F32R, a_tab + 24576)
        rr = at("s5_r_re", [P, 2, 2, SEQ], F32, a_rr)
        ri = at("s5_r_im", [P, 2, 2, SEQ], F32, a_ri)
        sr = at("s5_s_re", [P, 2, 2, SEQ], F32, a_sr)
        tt = at("s5_pool_tmp", [P, 2, SEQ], F32, a_tt)
        t12 = at("s5_dve_tmp", [P, 2, SEQ], F32, a_t12)
        tabt = at("turn_tmp_dve", [P, 8, P], F32, a_rr)
        tabp = at("turn_tmp_pool", [P, 8, P], F32, a_sr)
        gel = at("gelu_tmp", [P, CT, SEQ], F32, a_rr)
        gth = at("gelu_tanh", [P, CT, SEQ], F32, a_ri)
        ropeA = at("rope_a", [P, 512], F32, a_att)
        ropeB = at("rope_b", [P, 512], F32, a_att + 2048)
        ropeC = at("rope_c", [P, 512], F32, a_att + 4096)
        prob = at("prob", [P, 2, 384], F32, a_att)
        wT = at("attn_wT", [P, 384], F32, a_att + 3072)
        osq = sb("o_square_out", [P, 256])
        osb = at("o_tok", [P, 256], F32, a_att + 4608)
        Bre = sb("s5_b_re", [P, CT, P])
        Bim = sb("s5_b_im", [P, CT, P])
        Cre = sb("s5_c_re", [P, PAIRS, 32])
        Cin = sb("s5_c_nim", [P, PAIRS, 32])
        act_t = at("act_tok", [P, NT, FB], F32, a_q)
        sg = at("silu_g", [P, NT, FB], F32, a_q + 2048)
        aTh = at("actT_hi", [P, 2, SEQ], F32R, a_q + 4096)
        aTl = at("actT_lo", [P, 2, SEQ], F32R, a_q + 6144)
        hsh = at("hsT_hi", [P, KD, P], F32R, a_k)
        hsl = at("hsT_lo", [P, KD, P], F32R, a_k + 4096)
        bTh = at("eactT_hi", [P, 2, 2, P], F32R, a_yl)
        bTl = at("eactT_lo", [P, 2, 2, P], F32R, a_yl + 2048)
        rawx = at("w_raw_more", [P, 1, SLOT], F32, a_tab + 8192)
        whx = [at("w_hi_more0", [P, 1, SLOT], F32R, a_rr), at("w_hi_more1", [P, 1, SLOT], F32R, a_tab + 16384)]
        wlx = [at("w_lo_more0", [P, 1, SLOT], F32R, a_rr + 8192), at("w_lo_more1", [P, 1, SLOT], F32R, a_tab + 24576)]
        ysb = at("y_slots", [P, D], F32, a_yh)
        S = at("select", [P, NT, P], F32, a_att)
        ST = at("selectT", [P, SEQ], F32, a_att + 1024)
        gfin = at("final_gain", [P, D], F32, a_u)
        outt = at("out_tok", [P, NT, D], F32, a_k)
        mp = [a_tab]

        def rt(name, shape, dt=F32):
            a = mp[0]
            mp[0] += size(shape, dt)
            return at(name, shape, dt, a)

        rw = rt("router_w", [P, KD, EXPERTS])
        lg = rt("logits", [P, NT, 8])
        top = rt("top8", [P, NT, 8])
        topi = rt("top8_at", [P, NT, 8], U32)
        topf = rt("top_at_f", [P, NT, 8])
        iota8 = rt("iota8", [P, 8])
        oh1 = rt("first_choice", [P, NT, 8])
        oh2 = rt("second_choice", [P, NT, 8])
        ex2 = rt("second_exp", [P, NT])
        den = rt("gate_den", [P, NT])
        g1 = rt("gate_first", [P, NT])
        g2 = rt("gate_second", [P, NT])
        G = rt("gates", [P, NT, 8])
        M = rt("chosen", [P, NT, 8])
        below = rt("below", [P, P])
        ones = rt("ones", [P, P])
        placed = rt("place_plus_1", [P, NT, 8])
        cnt = rt("expert_counts", [P, 8])
        over = rt("over", [P, 8])
        overc = rt("over_cum", [P, 8])
        ohr = rt("over_round", [P, 3, 8])
        prod = rt("over_prod", [P, 8])
        placeR = rt("round_place", [P, NT, 12])
        gateR = rt("round_gate", [P, NT, 12])
        eF = rt("round_expert_f", [P, 12])
        eI = rt("round_expert", [P, 12], I32)
        rF = rt("rounds_f", [P, 1])
        rI = rt("rounds", [P, 1], I32)
        iota128 = rt("iota128", [P, P])
        iotai = rt("iota_int", [P, P], I32)
        pcol = rt("place_now", [P, NT])
        gcol = rt("gate_now", [P, NT])
        sp_ = [a_k]

        def su(name, shape, dt=F32):
            a = sp_[0]
            sp_[0] += size(shape, dt)
            return at(name, shape, dt, a)

        posi = su("positions_int", [P, NT], I32)
        posf = su("positions_f", [P, NT])
        invf = su("inv_freq", [P, 32])
        ang = su("angle", [P, NT * 32 + DEPTH * PAIRS])
        angk = su("angle_turns", [P, NT * 32 + DEPTH * PAIRS])
        angr = su("angle_rest", [P, NT * 32 + DEPTH * PAIRS])
        lamv = su("lambda_vecs", [P, 4, DEPTH, HD])
        lamp = su("lambda_prod", [P, 2, DEPTH, HD])
        lams = su("lambda_sum", [P, 2, DEPTH])
        lame = su("lambda_exp", [P, 2, DEPTH])
        lre = su("ssm_lre", [P, DEPTH, PAIRS])
        lim = su("ssm_lim", [P, DEPTH, PAIRS])
        ldt = su("ssm_ldt", [P, DEPTH, PAIRS])
        dtt = su("ssm_dt", [P, DEPTH, PAIRS])
        q1 = su("ssm_q1", [P, DEPTH, PAIRS])
        q2 = su("ssm_q2", [P, DEPTH, PAIRS])
        q3 = su("ssm_q3", [P, DEPTH, PAIRS])
        q4 = su("ssm_q4", [P, DEPTH, PAIRS])
        Craw = at("s5_c_raw", [P, 2, PAIRS, GCH], F32, a_att)
        Ctmp = at("s5_c_tmp", [P, 2, PAIRS, GCH], F32, a_att + 2048)
        assert here[0] <= nc.sbuf_usable_end, (here[0], nc.sbuf_usable_end)
        assert mp[0] <= a_tab + 8192 and sp_[0] <= a_k + 8192

        PS = ctx.enter_context(nc.psum_tensor("psum", [P, 8, 512], F32))

        def bank(b):
            return PS[:, b, :]

        s_raw = [sem(f"raw_landed{p}") for p in range(NR)]
        s_hi, s_lo, s_used = sem("w_hi_ready"), sem("w_lo_ready"), sem("w_used")
        s_x0, s_set, s_s5l, s_c, s_b = sem("x_landed"), sem("setup_landed"), sem("s5_landed"), sem("c_landed"), sem("b_landed")
        s_gf, s_rw, s_out = sem("final_gain_landed"), sem("router_landed"), sem("out_stored")
        s_pool, s_dve, s_actc = sem("pool_step"), sem("dve_step"), sem("act_step")
        s_const, s_bz = sem("constants_ready"), sem("b_zeroed")
        s_ang, s_trig, s_dt = sem("angles_ready"), sem("trig_ready"), sem("dt_ready")
        s_tabd, s_tabp, s_prep = sem("turns_by_dve"), sem("turns_by_pool"), sem("c_scaled")
        s_ss, s_rstd, s_xn = sem("norm_sum"), sem("norm_rstd_ready"), sem("x_normed_ready")
        s_tr, s_thi, s_trf = sem("tr_written"), sem("tr_hi_taken"), sem("tr_free")
        s_acc, s_accA, s_accV = sem("acc_written"), sem("acc_taken_act"), sem("acc_taken_dve")
        s_rope = sem("roped")
        s_bu, s_buf, s_scan, s_rot = sem("bu_written"), sem("bu_taken"), sem("scanned"), sem("turned_back")
        s_yc, s_yv = sem("y_products"), sem("y_taken")
        s_gsq, s_gin, s_gth, s_yg, s_ygh, s_ygl = (sem("gelu_square"), sem("gelu_inner"), sem("gelu_tanh_ready"),
                                                   sem("gelu_ready"), sem("yS_hi_ready"), sem("yS_lo_ready"))
        s_sc, s_nb, s_ex, s_w = sem("scores_written"), sem("exp_bias_ready"), sem("exp_ready"), sem("attn_w_ready")
        s_osq, s_ors, s_on = sem("o_squared"), sem("o_rstd_ready"), sem("o_normed")
        s_m = sem("m_ready")
        s_gu, s_sg, s_act = sem("gate_up_written"), sem("silu_ready"), sem("act_ready")
        s_lg, s_route = sem("exp_second_ready"), sem("routed")
        s_M = sem("choices_ready")
        s_S, s_ysb, s_scat, s_scatv = sem("select_ready"), sem("y_copied"), sem("scattered"), sem("scatter_taken")
        s_fin = sem("out_ready")

        R_TR = len(ROUND_TR)
        TR0 = len(TR)
        USED_MIX, USED_FFN = 15, 2 * NJ
        GU0 = NT * NJ

        def used(seg, i, r=None):
            if seg in (0, 2):
                blk, h, n = slot_block(i)
                if h == n - 1:
                    return s_acc, 2 * (BLOCK_COUNT * (seg // 2) + blk + 1)
                mine = sum(1 for k in range(i + 1) if slot_block(k)[1] != slot_block(k)[2] - 1)
                return s_used, (0 if seg == 0 else USED_MIX + USED_FFN) + mine
            slots = FFN_SLOTS if seg == 1 else ROUND_SLOTS
            kind, j = slots[i]
            if kind == "u":
                return s_gu, NT * (j + 1) if seg == 1 else r * NJ + (GU0 + j + 1)
            mine = sum(1 for k in range(i + 1) if slots[k][0] != "u")
            if seg == 1:
                return s_used, USED_MIX + mine
            return s_used, r * USED_FFN + (2 * USED_MIX + USED_FFN + mine)

        def nslot(seg, i, r=None):
            return seg * SEG + i if seg < 3 else r * SEG + (3 * SEG + i)

        def raw_of(seg, i):
            p = (RAW_POS if seg < 3 else ROUND_POS)[i]
            return raw[:, p, :] if p < NRAW else rawx[:, 0, :]

        def split_of(seg, i):
            p = i % NW if seg < 3 else ROUND_POS[i]
            if p < NW:
                return wh[:, p, :], wl[:, p, :]
            return whx[p - NW][:, 0, :], wlx[p - NW][:, 0, :]

        def landed(seg, i, r=None):
            if seg < 3:
                p = RAW_POS[i]
                return s_raw[p], 16 * (seg * RAW_USES[p] + RAW_POS[:i + 1].count(p))
            p = ROUND_POS[i]
            n = (3 * RAW_USES[p] if p < NRAW else 0) + ROUND_POS[:i + 1].count(p)
            return s_raw[p], r * (16 * ROUND_USES[p]) + 16 * n

        def act_split(act, seg, i, r=None, ahead=False):
            s, val = landed(seg, i, r)
            act.wait_ge(s, val + 16 * ROUND_USES[ROUND_POS[i]] if ahead else val)
            if seg == 3 and (r is not PROLOGUE):
                back = before_in(ROUND_POS, i)
                if ahead:
                    s, val = used(3, back + SEG, r)
                elif back >= 0:
                    s, val = used(3, back, r)
                else:
                    s, val = used(3, back + SEG, r)
                    val = val - (NJ if s is s_gu else USED_FFN)
                act.wait_ge(s, val)
            elif seg == 3 or i < NW:
                if seg:
                    act.wait_ge(*used(seg - 1, i - NW + SEG))
            else:
                act.wait_ge(*used(seg, i - NW))
            nc.scalar.activation(split_of(seg, i)[0], raw_of(seg, i), ACT.Copy).then_inc(s_hi, 1)

        def dve_split(dve, seg, i, r=None, ahead=False):
            dve.wait_ge(s_hi, nslot(seg, i + (SEG + 1 if ahead else 1), r))
            h, l_ = split_of(seg, i)
            nc.vector.tensor_tensor(l_, raw_of(seg, i), h.bitcast(F32), ALU.subtract).then_inc(s_lo, 1)

        def split_ahead(split, eng, seg, i):
            if i + AHEAD < SEG:
                split(eng, seg, i + AHEAD)
            elif seg < 2:
                split(eng, seg + 1, i + AHEAD - SEG)

        def parts(seg, i, k):
            return [a.rearrange("p (k n) -> p k n", k=k) for a in split_of(seg, i)]

        def round_split(split, eng, i, r):
            n = i + RAHEAD
            split(eng, 3, n % SEG, r, ahead=n >= SEG)

        class Own:

            def __init__(self, eng, s):
                self.eng, self.s, self.n, self.r, self.per = eng, s, 0, None, 0

            def do(self, ins):
                ins.then_inc(self.s, 1)
                self.n += 1

            def settle(self):
                if self.r is None:
                    self.eng.wait_ge(self.s, self.n)
                else:
                    self.eng.wait_ge(self.s, self.r * self.per + self.n)

        block = ctx.enter_context(nc.Block())

        @block.sync
        def _(sp):
            win = t["w_in"].rearrange("l (c p) n -> l p c n", p=P)
            wglu = t["w_glu"].rearrange("l (c p) n -> l p c n", p=P)
            wps = t["w_proj_ssm"].rearrange("l (c p) n -> l p c n", p=P)
            wpa = t["w_proj_attn"].rearrange("l (c p) n -> l p c n", p=P)
            wo = t["w_out"].rearrange("l (c p) n -> l p c n", p=P)

            def ffn_src(wg, wu, wd, what, e):
                kind, j = what
                if kind == "d":
                    return wd.rearrange("e (c p) n -> p (e c) n", p=P)[:, bass.ds(e * (FF // P) + 2 * j, 2), :]
                w = wg if kind == "g" else wu
                one = slice(0, 1) if isinstance(e, int) else bass.ds(e, 1)
                return w.rearrange("e (c p) n -> e p c n", p=P)[one, :, :, j * FB:(j + 1) * FB].rearrange("e p c n -> (e p) c n")

            def mixer_src(l, i):
                blk, h, n = slot_block(i)
                half = slice(4 * h, 4 * h + 4)
                if blk < GLU:
                    return win[l, :, half, blk * 512:(blk + 1) * 512]
                if blk == GLU:
                    return wglu[l]
                c = (blk % 2) * 512
                if blk < PA0:
                    return wps[l, :, :, c:c + 512]
                return (wpa if blk < WO0 else wo)[l, :, half, c:c + 512]

            def load(seg, i, src, r=None, ahead=False):
                if seg < 3:
                    before = seg * SEG + before_in(RAW_POS, i)
                    if before >= 0:
                        sp.wait_ge(s_lo, before + 1)
                elif r is PROLOGUE:
                    sp.wait_ge(s_lo, 3 * SEG + before_in(RAW_POS, i) + 1)
                else:
                    sp.wait_ge(s_lo, nslot(3, before_in(ROUND_POS, i) + (SEG + 1 if ahead else 1), r))
                k = src.shape[1]
                sp.dma_start(raw_of(seg, i).rearrange("p (k n) -> p k n", k=k), src).then_inc(landed(seg, i, 0)[0], 16)

            for seg in range(3):
                for i in range(SEG):
                    if seg == 1:
                        src = ffn_src(t["dense_w_gate"], t["dense_w_up"], t["dense_w_down"], FFN_SLOTS[i], 0)
                    else:
                        src = mixer_src(seg // 2, i)
                    load(seg, i, src)
            moe = (t["moe_w_gate"], t["moe_w_up"], t["moe_w_down"])
            for i in range(RAHEAD):
                load(3, i, ffn_src(*moe, ROUND_SLOTS[i], 0), PROLOGUE)
            sp.wait_ge(s_route, 1)
            rounds = sp.value_load(rI[0:1, 0:1], min_val=EXPERTS, max_val=MAX_ROUNDS)
            with sp.Fori(0, rounds) as r:
                e = sp.value_load(eI[0:1, bass.ds(r, 1)], min_val=0, max_val=EXPERTS - 1)
                for i in range(RAHEAD, SEG):
                    load(3, i, ffn_src(*moe, ROUND_SLOTS[i], e), r)
                e = sp.value_load(eI[0:1, bass.ds(r + 1, 1)], min_val=0, max_val=EXPERTS - 1)
                for i in range(RAHEAD):
                    load(3, i, ffn_src(*moe, ROUND_SLOTS[i], e), r, ahead=True)
            o = t["out"].rearrange("(t p) d -> p t d", p=P)
            for q in range(NT):
                sp.wait_ge(s_fin, q + 1)
                sp.dma_start(o[:, q, :], outt[:, q, :]).then_inc(s_out, 16)
            sp.wait_ge(s_out, 16 * NT)

        def build_turns(e, own, l, p0, w, tmp, tell):
            T = tab[:, p0:p0 + 8]
            own.do(e.memset(T[:, :, 0, 0:1], 1.0))
            own.do(e.memset(T[:, :, 1, 0:1], 0.0))
            own.do(e.tensor_copy(w[:, :, 0:1], s5c[:, l, p0:p0 + 8].rearrange("p (q o) -> p q o", o=1)))
            own.do(e.tensor_copy(w[:, :, 1:2], s5s[:, l, p0:p0 + 8].rearrange("p (q o) -> p q o", o=1)))
            own.settle()
            n = 1
            while n < SEQ:
                wr, wi = w[:, :, 0:1].to_broadcast([P, 8, n]), w[:, :, 1:2].to_broadcast([P, 8, n])
                er, ei = T[:, :, 0, 0:n], T[:, :, 1, 0:n]
                fr, fi = T[:, :, 0, n:2 * n], T[:, :, 1, n:2 * n]
                u = tmp[:, :, 0:n]
                own.do(e.tensor_tensor(fr, er, wr, ALU.mult))
                own.do(e.tensor_tensor(u, ei, wi, ALU.mult))
                own.do(e.tensor_tensor(fi, ei, wr, ALU.mult))
                own.settle()
                own.do(e.tensor_tensor(fr, fr, u, ALU.subtract))
                own.settle()
                own.do(e.tensor_tensor(u, er, wi, ALU.mult))
                own.do(e.tensor_tensor(w[:, :, 2:3], w[:, :, 0:1], w[:, :, 0:1], ALU.mult))
                own.do(e.tensor_tensor(w[:, :, 3:4], w[:, :, 1:2], w[:, :, 1:2], ALU.mult))
                own.settle()
                own.do(e.tensor_tensor(fi, fi, u, ALU.add))
                own.do(e.tensor_tensor(w[:, :, 1:2], w[:, :, 0:1], w[:, :, 1:2], ALU.mult))
                own.settle()
                own.do(e.tensor_tensor(w[:, :, 0:1], w[:, :, 2:3], w[:, :, 3:4], ALU.subtract))
                own.do(e.tensor_tensor(w[:, :, 1:2], w[:, :, 1:2], w[:, :, 1:2], ALU.add))
                own.settle()
                n *= 2
            e.memset(w[:, :, 2:3], 0.0).then_inc(tell, 1)

        @block.gpsimd
        def _(pool):
            own = Own(pool, s_pool)

            own.do(nc.gpsimd.memset(ident[:, :], 0.0))
            own.do(nc.gpsimd.memset(maskb[:, :], 0.0))
            own.settle()
            own.do(nc.gpsimd.affine_select(out=ident[:, :], in_=ident[:, :], compare_op=ALU.not_equal, fill=1.0,
                                           base=0, pattern=[[-1, P]], channel_multiplier=1))
            own.do(nc.gpsimd.affine_select(out=maskb[:, :], in_=maskb[:, :], compare_op=ALU.is_ge, fill=NEG,
                                           base=0, pattern=[[-1, P]], channel_multiplier=1))
            own.do(nc.gpsimd.memset(mhalf[:, :], -0.5))
            own.settle()
            nc.gpsimd.tensor_copy(identb[:, :], ident[:, :]).then_inc(s_const, 1)

            def rms_power(n, m, src, dst, k, scale, eps, got, tell):
                pool.wait_ge(got, n)
                own.do(nc.gpsimd.tensor_scalar(m[:, 0:k], src[:, 0:k], scale, eps, ALU.mult, ALU.add))
                own.settle()
                nc.gpsimd.tensor_tensor(dst[:, 0:k], m[:, 0:k], mhalf[:, 0:k], ALU.pow).then_inc(tell, 1)

            rms_power(1, mean, stat, rstd, NT, 1.0 / D, EPS, s_ss, s_rstd)
            for l in range(DEPTH):
                pool.wait_ge(s_trig, 3)
                if l == 1:
                    pool.wait_ge(s_xn, 2)
                build_turns(nc.gpsimd, own, l, 8, wpowp, tabp, s_tabp)
                if l == 1:
                    rms_power(3, mean, stat, rstd, NT, 1.0 / D, EPS, s_ss, s_rstd)
                for s in range(SEG):
                    c = (s - 4) // 2
                    if s >= 5 and (s - 5) % 2 == 0 and (s - 5) // 2 < CHUNKS:
                        c = (s - 5) // 2
                        b = c % 2
                        pool.wait_ge(s_scan, CHUNKS * l + c + 1)
                        if c >= 2:
                            pool.wait_ge(s_yc, CHUNKS * l + c - 1)
                        er, ei = tab[:, 2 * c:2 * c + 2, 0, :], tab[:, 2 * c:2 * c + 2, 1, :]
                        own.do(nc.gpsimd.tensor_tensor(sr[:, b], er, rr[:, b], ALU.mult))
                        own.do(nc.gpsimd.tensor_tensor(tt[:, :, :], ei, ri[:, b], ALU.mult))
                        own.settle()
                        own.do(nc.gpsimd.tensor_tensor(ri[:, b], er, ri[:, b], ALU.mult))
                        own.do(nc.gpsimd.tensor_tensor(rr[:, b], ei, rr[:, b], ALU.mult))
                        own.do(nc.gpsimd.tensor_tensor(sr[:, b], sr[:, b], tt[:, :, :], ALU.subtract))
                        own.settle()
                        nc.gpsimd.tensor_tensor(ri[:, b], ri[:, b], rr[:, b], ALU.add).then_inc(s_rot, 1)
                    if 0 <= s - 18 < HEADS:
                        rms_power(HEADS * l + s - 17, oms, oss, ors, 2, 1.0 / P, SUB_EPS, s_osq, s_ors)
                rms_power(2 + 2 * l, mean, stat, rstd, NT, 1.0 / D, EPS, s_ss, s_rstd)
            own.do(nc.gpsimd.memset(below[:, :], 1.0))
            own.do(nc.gpsimd.iota(iotai[:, :], pattern=[[1, P]], base=0, channel_multiplier=0))
            own.settle()
            own.do(nc.gpsimd.memset(ones[:, :], 1.0))
            own.do(nc.gpsimd.tensor_copy(iota128[:, :], iotai[:, :]))
            own.do(nc.gpsimd.tensor_copy(iota8[:, :], iotai[:, 0:8]))
            nc.gpsimd.affine_select(out=below[:, :], in_=below[:, :], compare_op=ALU.is_gt, fill=0.0,
                                    base=0, pattern=[[1, P]], channel_multiplier=-1).then_inc(s_const, 1)
            rms_power(5, mean, stat, rstd, NT, 1.0 / D, EPS, s_ss, s_rstd)

        @block.scalar
        def _(act):
            own = Own(act, s_actc)
            xd = t["x"].rearrange("(t p) d -> p t d", p=P)
            act.dma_start(x[:, :, :], xd).then_inc(s_x0, 16)
            act.dma_start(lre[:, :, :], t["lam_re"]).then_inc(s_s5l, 16)
            act.dma_start(lim[:, :, :], t["lam_im"]).then_inc(s_s5l, 16)
            act.dma_start(gains[:, 0], t["mix_norm"]).then_inc(s_set, 16)
            act.dma_start(gains[:, 1], t["ffn_norm"]).then_inc(s_set, 16)
            act.dma_start(subg[:, :], t["subln"]).then_inc(s_set, 16)
            act.dma_start(bglu[:, :, :], t["b_glu"]).then_inc(s_set, 16)
            act.dma_start(dskip[:, :, :], t["ssm_d"]).then_inc(s_set, 16)
            act.dma_start(posi[:, :], t["positions"]).then_inc(s_set, 16)
            act.dma_start(invf[:, :], t["inv_freq"].rearrange("(o f) -> o f", o=1).to_broadcast([P, 32])).then_inc(s_set, 16)
            for g in range(2):
                act.dma_start(ldt[g * 64:(g + 1) * 64, :, :],
                              t["log_dt"][g:g + 1].to_broadcast([64, DEPTH, PAIRS])).then_inc(s_s5l, 16)
            for n, name in enumerate(("lambda_q1", "lambda_k1", "lambda_q2", "lambda_k2")):
                act.dma_start(lamv[:, n], t[name].rearrange("(o l) d -> o l d", o=1).to_broadcast([P, DEPTH, HD])).then_inc(s_set, 16)

            def load_s5(l):
                act.dma_start(Craw[:, 0], t["c_re"][l]).then_inc(s_c, 16)
                act.dma_start(Craw[:, 1], t["c_im"][l]).then_inc(s_c, 16)
                for dst, name in ((Bre, "b_re"), (Bim, "b_im")):
                    for g in range(8):
                        src = t[name][l].rearrange("(k c) s -> c k s", k=CT)[16 * g:16 * g + 16]
                        act.dma_start(dst[16 * g:16 * g + 16, :, (g % 2) * 64:(g % 2) * 64 + 64], src).then_inc(s_b, 16)

            def norm_sums(n):
                for q in range(NT):
                    i = nc.scalar.activation(outsq[:, q, :], x[:, q, :], ACT.Square, accum_out=stat[:, q:q + 1])
                    if q == NT - 1:
                        i.then_inc(s_ss, 1)

            act.wait_ge(s_x0, 16)
            norm_sums(0)
            act.wait_ge(s_bz, 1)
            load_s5(0)
            act.wait_ge(s_s5l, 64)
            nc.scalar.activation(dtt[:, :, :], ldt[:, :, :], ACT.Exp).then_inc(s_dt, 1)
            act.wait_ge(s_ang, 1)
            own.do(nc.scalar.activation(s5m[:, :, :], q1[:, :, :], ACT.Exp))
            nc.scalar.activation(lame[:, :, :], lams[:, :, :], ACT.Exp).then_inc(s_trig, 1)
            act.wait_ge(s_ang, 2)
            NA = NT * 32
            own.do(nc.scalar.activation(sinT[:, :, :], angr[:, 0:NA].rearrange("p (t f) -> p t f", t=NT), ACT.Sin))
            nc.scalar.activation(s5s[:, :, :], angr[:, NA:].rearrange("p (l q) -> p l q", l=DEPTH), ACT.Sin).then_inc(s_trig, 1)
            own.do(nc.scalar.activation(cosT[:, :, :], angk[:, 0:NA].rearrange("p (t f) -> p t f", t=NT), ACT.Sin))
            nc.scalar.activation(s5c[:, :, :], angk[:, NA:].rearrange("p (l q) -> p l q", l=DEPTH), ACT.Sin).then_inc(s_trig, 1)
            act_split(act, 0, 0)
            act_split(act, 0, 1)

            def norm_hi(l, which):
                for g in range(4):
                    n = TR_AT[l, ("h1", "h2")[which], g]
                    act.wait_ge(s_tr, n + 1)
                    for kk in range(2):
                        k = 2 * g + kk
                        i = nc.scalar.activation(hTh[:, k, :], bank(4 + n % 2)[:, kk * 256:(kk + 1) * 256], ACT.Copy,
                                                 scale=gains[:, which, l, k:k + 1])
                        if kk:
                            i.then_inc(s_thi, 1)

            for l in range(DEPTH):
                seg = 2 * l
                if l == 0:
                    act.wait_ge(s_set, 16 * 11)
                norm_hi(l, 0)
                B0 = BLOCK_COUNT * l
                for s in range(SEG):
                    if 0 <= s - 16 < HEADS:
                        h = s - 16
                        act.wait_ge(s_nb, HEADS * l + h + 1)
                        if h:
                            act.wait_ge(s_tr, TR_AT[l, "wT", h - 1] + 1)
                        for q in range(NT):
                            n, off = (q + 1) * P, q * P
                            for c in range(2):
                                src = bank(2 + c)[:, (1 - q) * 256:(1 - q) * 256 + n]
                                i = nc.scalar.activation(prob[:, c, off:off + n], src, ACT.Exp, scale=SCALE,
                                                         bias=nb[:, 2 * q + c:2 * q + c + 1],
                                                         accum_out=sm[:, 2 * q + c:2 * q + c + 1])
                        i.then_inc(s_ex, 1)
                    if 0 <= s - 18 < HEADS:
                        act.wait_ge(s_trf, TR_AT[l, "o", s - 18] + 1)
                        for q in range(NT):
                            i = nc.scalar.activation(osq[:, q * P:(q + 1) * P], osb[:, q * P:(q + 1) * P], ACT.Square,
                                                     accum_out=oss[:, q:q + 1])
                        i.then_inc(s_osq, 1)
                    split_ahead(act_split, act, seg, s)
                    if 0 <= s - 19 < HEADS:
                        h = s - 19
                        n = TR_AT[l, "oT", h]
                        act.wait_ge(s_tr, n + 1)
                        if h == 0:
                            act.wait_ge(s_rot, CHUNKS * (l + 1))
                        nc.scalar.activation(yBh[:, h, :], bank(4 + n % 2)[:, 0:256], ACT.Copy,
                                             scale=subg[:, l:l + 1]).then_inc(s_thi, 1)
                    if s == 2:
                        for q in range(2):
                            act.wait_ge(s_acc, 2 * B0 + q + 1)
                            nc.scalar.activation(uT[:, 2 * q:2 * q + 2, :],
                                                 bank(q).rearrange("p (c n) -> p c n", c=2), ACT.Copy).then_inc(s_accA, 1)
                    if s in (12, 14):
                        b = 5 + (s - 12) // 2
                        for q in range(NT):
                            act.wait_ge(s_acc, 2 * (B0 + b) + q + 1)
                            nc.scalar.activation(v[:, q, (b - 5) * 512:(b - 4) * 512],
                                                 bank(2 * PAIR_OF[b] + q), ACT.Copy).then_inc(s_accA, 1)
                    if s in (16, 18, 20, 22):
                        b = 7 + (s - 16) // 2
                        dst = gs if b < 9 else ga
                        if s == 16:
                            act.wait_ge(s_rot, CHUNKS * l + 4)
                        for q in range(NT):
                            act.wait_ge(s_acc, 2 * (B0 + b) + q + 1)
                            nc.scalar.activation(dst[:, q, ((b - 7) % 2) * 512:((b - 7) % 2 + 1) * 512],
                                                 bank(q), ACT.Tanh, scale=0.5).then_inc(s_accA, 1)
                    if s == 21:
                        act.wait_ge(s_yv, CT * (l + 1))
                        nc.scalar.activation(gel[:, :, :], uT[:, :, :], ACT.Square).then_inc(s_gsq, 1)
                        act.wait_ge(s_gin, l + 1)
                        nc.scalar.activation(gth[:, :, :], gel[:, :, :], ACT.Tanh, scale=math.sqrt(2 / math.pi)).then_inc(s_gth, 1)
                        act.wait_ge(s_yg, 2 * l + 1)
                        nc.scalar.activation(ySh[:, :, :], uT[:, :, :], ACT.Copy, scale=0.5).then_inc(s_ygh, 1)
                    if s == 23:
                        for c in range(CT):
                            act.wait_ge(s_acc, 2 * (B0 + GLU) + c // 2 + 1)
                            i = nc.scalar.activation(gth[:, c, :], bank(c // 2)[:, (c % 2) * 256:(c % 2 + 1) * 256],
                                                     ACT.Tanh, scale=0.5, bias=bglu[:, l, c:c + 1])
                            if c % 2:
                                i.then_inc(s_accA, 1)
                        act.wait_ge(s_yg, 2 * l + 2)
                        nc.scalar.activation(ySh[:, :, :], uT[:, :, :], ACT.Copy, scale=0.25).then_inc(s_ygh, 1)
                    if s == 29:
                        for g in range(4):
                            n = TR_AT[l, "mT", g]
                            act.wait_ge(s_tr, n + 1)
                            nc.scalar.activation(hTh[:, 2 * g:2 * g + 2, :],
                                                 bank(4 + n % 2).rearrange("p (k n) -> p k n", k=2), ACT.Copy,
                                                 scale=0.5).then_inc(s_thi, 1)
                act.wait_ge(s_accV, ACCV_L * (l + 1))
                norm_sums(1)
                if l == 1:
                    act.dma_start(rw[:, :, :], t["router_w"].rearrange("(c p) e -> p c e", p=P)).then_inc(s_rw, 16)
                    act.dma_start(gfin[:, :], t["final_norm"].rearrange("(o d) -> o d", o=1).to_broadcast([P, D])).then_inc(s_gf, 16)
                norm_hi(l, 1)
                if l == 0:
                    load_s5(1)
                    for j in range(NJ):
                        if j < NJ - 1:
                            split_ahead(act_split, act, 1, FFN_AT["g", j + 1] - AHEAD)
                            split_ahead(act_split, act, 1, FFN_AT["u", j + 1] - AHEAD)
                        for q in range(NT):
                            act.wait_ge(s_gu, NT * j + q + 1)
                            nc.scalar.activation(sg[:, q, :], bank(6 + q)[:, 0:FB], ACT.Silu).then_inc(s_sg, 1)
                        split_ahead(act_split, act, 1, FFN_AT["d", j] - AHEAD)
                        n = TR_AT[0, "act", j]
                        act.wait_ge(s_tr, n + 1)
                        nc.scalar.activation(aTh[:, :, :], bank(4 + n % 2).rearrange("p (k n) -> p k n", k=2),
                                             ACT.Copy).then_inc(s_thi, 1)
                    for i in range(SEG - AHEAD, SEG):
                        split_ahead(act_split, act, 1, i)
                    act.wait_ge(s_xn, 3)
                    norm_sums(2)

            for i in range(RAHEAD):
                act_split(act, 3, i, PROLOGUE)

            def hs_hi(b, g):
                for kk in range(4):
                    k = 4 * g + kk
                    i = nc.scalar.activation(hsh[:, k, :], b[:, kk * P:(kk + 1) * P], ACT.Copy,
                                             scale=gains[:, 1, 1, k:k + 1])
                i.then_inc(s_thi, 1)

            act.wait_ge(s_lg, 1)
            nc.scalar.activation(den[:, :], ex2[:, :], ACT.Exp).then_inc(s_lg, 1)
            for g in range(2):
                n = TR_AT[1, "hs", g]
                act.wait_ge(s_tr, n + 1)
                hs_hi(bank(4 + n % 2), g)
            act.wait_ge(s_route, 1)
            rounds = act.value_load(rI[0:1, 0:1], min_val=EXPERTS, max_val=MAX_ROUNDS)
            with act.Fori(0, rounds) as r:
                def written(name):
                    n = TR0 + ROUND_TR.index(name)
                    act.wait_ge(s_tr, r * R_TR + (n + 1))
                    return bank(4 + n % 2)

                def act_hi(j):
                    b = written(f"act{j}")
                    nc.scalar.activation(bTh[:, j % 2], b[:, 0:256].rearrange("p (k n) -> p k n", k=2),
                                         ACT.Copy).then_inc(s_thi, 1)

                for i in range(SEG):
                    round_split(act_split, act, i, r)
                    kind, j = ROUND_SLOTS[i]
                    if kind == "u":
                        if j:
                            act_hi(j - 1) if j < NJ - 1 else None
                        act.wait_ge(s_gu, r * NJ + (GU0 + j + 1))
                        if j:
                            act.wait_ge(s_act, r * NJ + (GU0 + j))
                        nc.scalar.activation(sg[:, 0, :], bank(6 + j % 2)[:, 0:FB], ACT.Silu).then_inc(s_sg, 1)
                        if j == NJ - 1:
                            act_hi(j - 1)
                            hs_hi(written("hs0"), 0)
                            act_hi(j)
                            hs_hi(written("hs1"), 1)
                act.wait_ge(s_used, r * USED_FFN + (2 * USED_MIX + 2 * USED_FFN))
                for c in range(2):
                    nc.scalar.activation(ysb[:, c * 512:(c + 1) * 512], bank(c), ACT.Copy).then_inc(s_ysb, 1)
            act.wait_ge(s_xn, 6)
            norm_sums(3)

        @block.vector
        def _(dve):
            own = Own(dve, s_dve)
            V = nc.vector

            def norm(n):
                dve.wait_ge(s_rstd, n)
                for q in range(NT):
                    i = V.tensor_scalar(xn[:, q, :], x[:, q, :], rstd[:, q:q + 1], None, ALU.mult)
                i.then_inc(s_xn, 1)

            own.do(V.memset(Bre[:, :, :], 0.0))
            own.do(V.memset(Cre[:, :, :], 0.0))
            own.do(V.memset(Cin[:, :, :], 0.0))
            V.memset(Bim[:, :, :], 0.0).then_inc(s_bz, 1)
            dve.wait_ge(s_set, 16 * 11)
            own.do(V.tensor_tensor(lamp[:, 0], lamv[:, 0], lamv[:, 1], ALU.mult))
            own.do(V.tensor_tensor(lamp[:, 1], lamv[:, 2], lamv[:, 3], ALU.mult))
            own.settle()
            own.do(V.tensor_reduce(lams[:, :, :], lamp[:, :, :, :], AX_X, ALU.add))
            NA = NT * 32
            own.do(V.tensor_copy(posf[:, :], posi[:, :]))
            own.settle()
            for q in range(NT):
                own.do(V.tensor_scalar(ang[:, q * 32:(q + 1) * 32], invf[:, :], posf[:, q:q + 1], None, ALU.mult))
            dve.wait_ge(s_dt, 1)
            own.do(V.tensor_tensor(ang[:, NA:].rearrange("p (l q) -> p l q", l=DEPTH), lim[:, :, :], dtt[:, :, :], ALU.mult))
            V.tensor_tensor(q1[:, :, :], lre[:, :, :], dtt[:, :, :], ALU.mult).then_inc(s_ang, 1)
            own.settle()
            own.do(V.tensor_scalar(angk[:, :], ang[:, :], 1 / (2 * math.pi), ROUND, ALU.mult, ALU.add))
            own.settle()
            own.do(V.tensor_scalar(angk[:, :], angk[:, :], -ROUND, None, ALU.add))
            own.settle()
            own.do(V.scalar_tensor_tensor(angr[:, :], angk[:, :], -TWO_PI_HI, ang[:, :], ALU.mult, ALU.add))
            own.settle()
            own.do(V.scalar_tensor_tensor(angr[:, :], angk[:, :], -TWO_PI_MID, angr[:, :], ALU.mult, ALU.add))
            own.settle()
            own.do(V.scalar_tensor_tensor(angr[:, :], angk[:, :], -TWO_PI_LO, angr[:, :], ALU.mult, ALU.add))
            own.settle()
            own.do(V.tensor_scalar(angr[:, :], angr[:, :], PI_IN, -PI_IN, ALU.min, ALU.max))
            own.settle()
            own.do(V.tensor_scalar(angk[:, :], angr[:, :], -1.0, None, ALU.mult))
            own.settle()
            own.do(V.tensor_tensor(angk[:, :], angk[:, :], angr[:, :], ALU.min))
            own.settle()
            V.tensor_scalar(angk[:, :], angk[:, :], math.pi / 2, None, ALU.add).then_inc(s_ang, 1)
            norm(1)
            dve.wait_ge(s_trig, 3)
            own.do(V.tensor_tensor(nlam[:, :], lame[:, 1], lame[:, 0], ALU.subtract))
            own.do(V.tensor_scalar(nsinT[:, :, :], sinT[:, :, :], -1.0, None, ALU.mult))
            own.do(V.tensor_scalar(bglu[:, :, :], bglu[:, :, :], 0.5, None, ALU.mult))
            own.settle()
            for l in range(DEPTH):
                own.do(V.tensor_scalar(nlam[:, l:l + 1], nlam[:, l:l + 1], -lam_init(l), None, ALU.add))
                own.do(V.tensor_scalar(subg[:, l:l + 1], subg[:, l:l + 1], 1.0 - lam_init(l), None, ALU.mult))
            f = lambda a: a[:, :, :]
            own.do(V.tensor_tensor(f(q1), f(s5m), f(s5c), ALU.mult))
            own.do(V.tensor_tensor(f(q2), f(s5m), f(s5s), ALU.mult))
            own.settle()
            own.do(V.tensor_scalar(f(q1), f(q1), -1.0, None, ALU.add))
            own.do(V.tensor_tensor(f(q3), f(lre), f(lre), ALU.mult))
            own.do(V.tensor_tensor(f(q4), f(lim), f(lim), ALU.mult))
            own.settle()
            own.do(V.tensor_tensor(f(q3), f(q3), f(q4), ALU.add))
            own.settle()
            own.do(V.reciprocal(f(dtt), f(q3)))
            own.settle()
            own.do(V.tensor_tensor(f(s5fr), f(q1), f(lre), ALU.mult))
            own.do(V.tensor_tensor(f(q4), f(q2), f(lim), ALU.mult))
            own.do(V.tensor_tensor(f(s5fi), f(q2), f(lre), ALU.mult))
            own.do(V.tensor_tensor(f(q3), f(q1), f(lim), ALU.mult))
            own.settle()
            own.do(V.tensor_tensor(f(s5fr), f(s5fr), f(q4), ALU.add))
            own.do(V.tensor_tensor(f(s5fi), f(s5fi), f(q3), ALU.subtract))
            own.settle()
            own.do(V.tensor_tensor(f(s5fr), f(s5fr), f(dtt), ALU.mult))
            own.do(V.tensor_tensor(f(s5fi), f(s5fi), f(dtt), ALU.mult))
            own.settle()

            def scale_c(l):
                dve.wait_ge(s_c, 32 * (l + 1))
                fr = s5fr[:, l, :].rearrange("p (q o) -> p q o", o=1).to_broadcast([P, PAIRS, GCH])
                fi = s5fi[:, l, :].rearrange("p (q o) -> p q o", o=1).to_broadcast([P, PAIRS, GCH])
                own.do(V.tensor_tensor(Ctmp[:, 0], Craw[:, 0], fr, ALU.mult))
                own.do(V.tensor_tensor(Ctmp[:, 1], Craw[:, 1], fi, ALU.mult))
                own.settle()
                for g in range(2):
                    a, b = slice(g * 64, g * 64 + 64), slice(g * 16, g * 16 + 16)
                    own.do(V.tensor_tensor(Cre[a, :, b], Ctmp[a, 0], Ctmp[a, 1], ALU.subtract))
                own.settle()
                own.do(V.tensor_tensor(Ctmp[:, 0], Craw[:, 0], fi, ALU.mult))
                own.do(V.tensor_tensor(Ctmp[:, 1], Craw[:, 1], fr, ALU.mult))
                own.settle()
                own.do(V.tensor_scalar(Ctmp[:, 0], Ctmp[:, 0], -1.0, None, ALU.mult))
                own.settle()
                for g in range(2):
                    a, b = slice(g * 64, g * 64 + 64), slice(g * 16, g * 16 + 16)
                    i = V.tensor_tensor(Cin[a, :, b], Ctmp[a, 0], Ctmp[a, 1], ALU.subtract)
                    if g:
                        i.then_inc(s_prep, 1)

            thi = [0]

            def lo_of(dst, src, hi, scale, last=True):
                i = V.scalar_tensor_tensor(dst, src, scale, hi.bitcast(F32), ALU.mult, ALU.subtract)
                if last:
                    i.then_inc(s_trf, 1)

            def norm_lo(l, which):
                for g in range(4):
                    n = TR_AT[l, ("h1", "h2")[which], g]
                    thi[0] += 1
                    dve.wait_ge(s_thi, thi[0])
                    for kk in range(2):
                        k = 2 * g + kk
                        lo_of(hTl[:, k, :], bank(4 + n % 2)[:, kk * 256:(kk + 1) * 256], hTh[:, k, :],
                              gains[:, which, l, k:k + 1], last=bool(kk))

            def rope(l, b, q):
                blk = BLOCK_COUNT * l + b
                dve.wait_ge(s_acc, 2 * blk + q + 1)
                if b > 1 and q == 0:
                    dve.wait_ge(s_tr, TR_AT[l, "qkT", 2 * (b - 1) + 1] + 1)
                src = bank(2 * PAIR_OF[b] + q).rearrange("p (g h f) -> p g h f", g=8, h=2)
                A = ropeA if q == 0 else ropeC
                Av = A[:, :].rearrange("p (g h f) -> p g h f", g=8, h=2)
                Bv = ropeB[:, :].rearrange("p (g h f) -> p g h f", g=8, h=2)
                cs, sn, ns = cosT[:, q, :], sinT[:, q, :], nsinT[:, q, :]
                bc3 = lambda a: a.rearrange("p (g f) -> p g f", g=1).to_broadcast([P, 8, 32])
                own.do(V.tensor_tensor(Av[:, :, 0, :], src[:, :, 0, :], bc3(cs), ALU.mult))
                own.do(V.tensor_tensor(Av[:, :, 1, :], src[:, :, 1, :], bc3(cs), ALU.mult))
                own.do(V.tensor_tensor(Bv[:, :, 0, :], src[:, :, 1, :], bc3(ns), ALU.mult))
                V.tensor_tensor(Bv[:, :, 1, :], src[:, :, 0, :], bc3(sn), ALU.mult).then_inc(s_accV, 1)
                accv[0] += 1
                dve.wait_ge(s_accV, accv[0])
                V.tensor_tensor(A[:, :], A[:, :], ropeB[:, :], ALU.add).then_inc(s_rope, 1)
                rp[0] += 1
                dve.wait_ge(s_rope, rp[0])

            accv, rp = [0], [0]

            def out_block(l, b):
                pair, cs = PAIR_OF[b], slice((b % 2) * 512, (b % 2 + 1) * 512)
                for q in range(NT):
                    dve.wait_ge(s_acc, 2 * (BLOCK_COUNT * l + b) + q + 1)
                    src = bank(2 * pair + q)
                    if b < WO0:
                        g_ = gs if b < PA0 else ga
                        i = V.scalar_tensor_tensor(g_[:, q, cs], g_[:, q, cs], 1.0, src, ALU.add, ALU.mult)
                    else:
                        i = V.tensor_tensor(x[:, q, cs], x[:, q, cs], src, ALU.add)
                    i.then_inc(s_accV, 1)
                    accv[0] += 1

            scale_c(0)
            build_turns(V, own, 0, 0, wpow, tabt, s_tabd)
            dve_split(dve, 0, 0)
            dve_split(dve, 0, 1)
            for l in range(DEPTH):
                seg = 2 * l
                norm_lo(l, 0)
                B0 = BLOCK_COUNT * l
                for s in range(SEG):
                    if 0 <= s - 16 < HEADS:
                        h = s - 16
                        dve.wait_ge(s_sc, HEADS * l + h + 1)
                        own.do(V.tensor_reduce(mx[:, 0:2], PS[:, 2:4, 256:384], AX_X, ALU.max))
                        own.do(V.tensor_reduce(mx[:, 2:4], PS[:, 2:4, 0:256], AX_X, ALU.max))
                        own.settle()
                        V.tensor_scalar(nb[:, :], mx[:, :], -SCALE, None, ALU.mult).then_inc(s_nb, 1)
                    if 0 <= s - 17 < HEADS:
                        h = s - 17
                        n = TR_AT[l, "wT", h]
                        dve.wait_ge(s_tr, n + 1)
                        if h:
                            dve.wait_ge(s_tr, TR_AT[l, "o", h - 1] + 1)
                        V.tensor_copy(wT[:, :], bank(4 + n % 2)[:, 0:384]).then_inc(s_trf, 1)
                    if 0 <= s - 18 < HEADS:
                        h = s - 18
                        n = TR_AT[l, "o", h]
                        dve.wait_ge(s_tr, n + 1)
                        if h:
                            dve.wait_ge(s_tr, TR_AT[l, "oT", h - 1] + 1)
                        V.tensor_copy(osb[:, :], bank(4 + n % 2)[:, 0:256]).then_inc(s_trf, 1)
                    split_ahead(dve_split, dve, seg, s)
                    if 0 <= s - 19 < HEADS:
                        h = s - 19
                        n = TR_AT[l, "oT", h]
                        thi[0] += 1
                        dve.wait_ge(s_thi, thi[0])
                        lo_of(yBl[:, h, :], bank(4 + n % 2)[:, 0:256], yBh[:, h, :], subg[:, l:l + 1])
                    if 0 <= s - 3 < PAIRS:
                        p = s - 3
                        c, b = p // 2, (p // 2) % 2
                        dve.wait_ge(s_bu, PAIRS * l + p + 1)
                        if p == 8:
                            dve.wait_ge(s_tabp, l + 1)
                        if p % 2 == 0 and c >= 2:
                            dve.wait_ge(s_yc, CHUNKS * l + c - 1)
                        R_, I_ = rr[:, b, p % 2, :], ri[:, b, p % 2, :]
                        br, bi = bank(6)[:, 0:256], bank(6)[:, 256:512]
                        own.do(V.tensor_tensor(R_, br, tab[:, p, 0, :], ALU.mult))
                        own.do(V.tensor_tensor(t12[:, 0, :], bi, tab[:, p, 1, :], ALU.mult))
                        own.do(V.tensor_tensor(I_, bi, tab[:, p, 0, :], ALU.mult))
                        V.tensor_tensor(t12[:, 1, :], br, tab[:, p, 1, :], ALU.mult).then_inc(s_buf, 1)
                        dve.wait_ge(s_buf, PAIRS * l + p + 1)
                        own.do(V.tensor_tensor(R_, R_, t12[:, 0, :], ALU.add))
                        own.do(V.tensor_tensor(I_, I_, t12[:, 1, :], ALU.subtract))
                        own.settle()
                        m = s5m[:, l, p:p + 1].to_broadcast([P, SEQ])
                        own.do(V.tensor_tensor_scan(R_, m, R_, 0.0, ALU.mult, ALU.add))
                        i = V.tensor_tensor_scan(I_, m, I_, 0.0, ALU.mult, ALU.add)
                        if p % 2:
                            i.then_inc(s_scan, 1)
                        else:
                            own.do(i)
                    if s in (4, 6, 8, 10):
                        rope(l, (s - 2) // 2, 0)
                    if s in (5, 7, 9, 11):
                        rope(l, (s - 3) // 2, 1)
                    if s in (6, 8, 10, 12):
                        b = (s - 4) // 2
                        dst = qT if b < 3 else kT
                        for q in range(NT):
                            n = TR_AT[l, "qkT", 2 * b + q]
                            dve.wait_ge(s_tr, n + 1)
                            h0 = ((b - 1) % 2) * 4
                            V.tensor_copy(dst[:, h0:h0 + 4, q * P:(q + 1) * P],
                                          bank(4 + n % 2).rearrange("p (h n) -> p h n", h=4)).then_inc(s_trf, 1)
                    if s in (9, 13, 17, 21):
                        kt = (s - 9) // 4
                        dve.wait_ge(s_yc, CHUNKS * l + 2 * kt + 2)
                        V.scalar_tensor_tensor(uT[:, kt, :], uT[:, kt, :], dskip[:, l, kt:kt + 1],
                                               bank(7)[:, (kt % 2) * 256:(kt % 2 + 1) * 256],
                                               ALU.mult, ALU.add).then_inc(s_yv, 1)
                    if s == 21:
                        dve.wait_ge(s_gsq, l + 1)
                        own.do(V.tensor_scalar(gel[:, :, :], gel[:, :, :], 0.044715, 1.0, ALU.mult, ALU.add))
                        own.settle()
                        V.tensor_tensor(gel[:, :, :], gel[:, :, :], uT[:, :, :], ALU.mult).then_inc(s_gin, 1)
                        dve.wait_ge(s_gth, l + 1)
                        V.scalar_tensor_tensor(uT[:, :, :].rearrange("p c n -> p (c n)"), gth[:, :, :].rearrange("p c n -> p (c n)"), 1.0,
                                               uT[:, :, :].rearrange("p c n -> p (c n)"), ALU.add, ALU.mult).then_inc(s_yg, 1)
                        dve.wait_ge(s_ygh, 2 * l + 1)
                        V.scalar_tensor_tensor(ySl[:, :, :].rearrange("p c n -> p (c n)"), uT[:, :, :].rearrange("p c n -> p (c n)"), 0.5,
                                               ySh[:, :, :].rearrange("p c n -> p (c n)").bitcast(F32), ALU.mult,
                                               ALU.subtract).then_inc(s_ygl, 1)
                    if s == 23:
                        dve.wait_ge(s_accA, ACCA_L * (l + 1))
                        V.scalar_tensor_tensor(uT[:, :, :].rearrange("p c n -> p (c n)"), gth[:, :, :].rearrange("p c n -> p (c n)"), 1.0,
                                               uT[:, :, :].rearrange("p c n -> p (c n)"), ALU.add, ALU.mult).then_inc(s_yg, 1)
                        dve.wait_ge(s_ygh, 2 * l + 2)
                        V.scalar_tensor_tensor(ySl[:, :, :].rearrange("p c n -> p (c n)"), uT[:, :, :].rearrange("p c n -> p (c n)"), 0.25,
                                               ySh[:, :, :].rearrange("p c n -> p (c n)").bitcast(F32), ALU.mult,
                                               ALU.subtract).then_inc(s_ygl, 1)
                    if 0 <= s - 16 < HEADS:
                        h = s - 16
                        dve.wait_ge(s_ex, HEADS * l + h + 1)
                        own.do(V.reciprocal(rs[:, :], sm[:, :]))
                        own.settle()
                        own.do(V.tensor_scalar(c2[:, :], rs[:, 1:4:2], nlam[:, l:l + 1], None, ALU.mult))
                        own.settle()
                        for q in range(NT):
                            sl = slice(q * P, q * P + (q + 1) * P)
                            own.do(V.tensor_scalar(prob[:, 1, sl], prob[:, 1, sl], c2[:, q:q + 1], None, ALU.mult))
                        own.settle()
                        for q in range(NT):
                            sl = slice(q * P, q * P + (q + 1) * P)
                            i = V.scalar_tensor_tensor(prob[:, 0, sl], prob[:, 0, sl], rs[:, 2 * q:2 * q + 1],
                                                       prob[:, 1, sl], ALU.mult, ALU.add)
                        i.then_inc(s_w, 1)
                    if 0 <= s - 18 < HEADS:
                        h = s - 18
                        dve.wait_ge(s_ors, HEADS * l + h + 1)
                        for q in range(NT):
                            i = V.tensor_scalar(osb[:, q * P:(q + 1) * P], osb[:, q * P:(q + 1) * P], ors[:, q:q + 1],
                                                None, ALU.mult)
                        i.then_inc(s_on, 1)
                    if s in (24, 25, 27, 29, 31):
                        out_block(l, {24: 12, 25: 13, 27: 14, 29: 15, 31: 16}[s])
                    if s == 29:
                        dve.wait_ge(s_accV, accv[0])
                        for q in range(NT):
                            i = V.tensor_tensor(gs[:, q, :], gs[:, q, :], ga[:, q, :], ALU.add)
                        i.then_inc(s_m, 1)
                        for g in range(4):
                            n = TR_AT[l, "mT", g]
                            thi[0] += 1
                            dve.wait_ge(s_thi, thi[0])
                            lo_of(hTl[:, 2 * g:2 * g + 2, :].rearrange("p k n -> p (k n)"), bank(4 + n % 2),
                                  hTh[:, 2 * g:2 * g + 2, :].rearrange("p k n -> p (k n)"), 0.5)
                out_block(l, 17)
                norm(2 + 2 * l)
                norm_lo(l, 1)
                if l == 0:
                    scale_c(1)
                    build_turns(V, own, 1, 0, wpow, tabt, s_tabd)
                    for j in range(NJ):
                        if j < NJ - 1:
                            split_ahead(dve_split, dve, 1, FFN_AT["g", j + 1] - AHEAD)
                            split_ahead(dve_split, dve, 1, FFN_AT["u", j + 1] - AHEAD)
                        for q in range(NT):
                            dve.wait_ge(s_sg, NT * j + q + 1)
                            V.tensor_tensor(act_t[:, q, :], sg[:, q, :], bank(6 + q)[:, FB:2 * FB],
                                            ALU.mult).then_inc(s_act, 1)
                        split_ahead(dve_split, dve, 1, FFN_AT["d", j] - AHEAD)
                        n = TR_AT[0, "act", j]
                        thi[0] += 1
                        dve.wait_ge(s_thi, thi[0])
                        V.tensor_tensor(aTl[:, :, :].rearrange("p k n -> p (k n)"), bank(4 + n % 2),
                                        aTh[:, :, :].rearrange("p k n -> p (k n)").bitcast(F32),
                                        ALU.subtract).then_inc(s_trf, 1)
                    for i in range(SEG - AHEAD, SEG):
                        split_ahead(dve_split, dve, 1, i)
                    dve.wait_ge(s_used, USED_MIX + USED_FFN)
                    for q in range(NT):
                        for c in range(2):
                            i = V.tensor_tensor(x[:, q, c * 512:(c + 1) * 512], x[:, q, c * 512:(c + 1) * 512],
                                                bank(2 * q + c), ALU.add)
                    i.then_inc(s_xn, 1)
                    dve.wait_ge(s_xn, 3)
                    norm(3)

            for i in range(RAHEAD):
                dve_split(dve, 3, i, PROLOGUE)

            n = TR_AT[1, "logits", 0]
            dve.wait_ge(s_tr, n + 1)
            V.tensor_copy(lg[:, :, :], bank(4 + n % 2)[:, 0:16].rearrange("p (t e) -> p t e", t=NT)).then_inc(s_trf, 1)
            dve.wait_ge(s_trf, n + 1)
            for q in range(NT):
                own.do(V.max(top[:, q, :], lg[:, q, :]))
            own.settle()
            for q in range(NT):
                own.do(V.max_index(topi[:, q, :], top[:, q, :], lg[:, q, :]))
            own.settle()
            own.do(V.tensor_copy(topf[:, :, :], topi[:, :, :]))
            V.tensor_tensor(ex2[:, :], top[:, :, 1], top[:, :, 0], ALU.subtract).then_inc(s_lg, 1)
            own.settle()
            dve.wait_ge(s_const, 2)
            for q in range(NT):
                own.do(V.tensor_scalar(oh1[:, q, :], iota8[:, :], topf[:, q, 0:1], None, ALU.is_equal))
                own.do(V.tensor_scalar(oh2[:, q, :], iota8[:, :], topf[:, q, 1:2], None, ALU.is_equal))
            own.settle()
            V.tensor_tensor(M[:, :, :], oh1[:, :, :], oh2[:, :, :], ALU.add).then_inc(s_M, 1)
            dve.wait_ge(s_lg, 2)
            own.do(V.tensor_scalar(g1[:, :], den[:, :], 1.0, None, ALU.add))
            own.settle()
            own.do(V.reciprocal(g1[:, :], g1[:, :]))
            own.settle()
            own.do(V.tensor_tensor(g2[:, :], g1[:, :], den[:, :], ALU.mult))
            own.settle()
            for q in range(NT):
                own.do(V.tensor_scalar(oh1[:, q, :], oh1[:, q, :], g1[:, q:q + 1], None, ALU.mult))
                own.do(V.tensor_scalar(oh2[:, q, :], oh2[:, q, :], g2[:, q:q + 1], None, ALU.mult))
            own.settle()
            own.do(V.tensor_tensor(G[:, :, :], oh1[:, :, :], oh2[:, :, :], ALU.add))
            n = TR_AT[1, "places", 0]
            dve.wait_ge(s_tr, n + 1)
            own.do(V.scalar_tensor_tensor(placed[:, :, :].rearrange("p t e -> p (t e)"), bank(4 + n % 2)[:, 0:16], 1.0,
                                          M[:, :, :].rearrange("p t e -> p (t e)"), ALU.add, ALU.mult))
            V.tensor_copy(cnt[:, :], bank(4 + n % 2)[:, 16:24]).then_inc(s_trf, 1)
            dve.wait_ge(s_trf, n + 1)
            own.do(V.tensor_scalar(over[:, :], cnt[:, :], float(P), None, ALU.is_gt))
            own.settle()
            own.do(V.tensor_tensor_scan(overc[:, :], ones[:, 0:8], over[:, :], 0.0, ALU.mult, ALU.add))
            own.settle()
            own.do(V.tensor_scalar(rF[:, :], overc[:, 7:8], float(EXPERTS), None, ALU.add))
            for k in range(3):
                own.do(V.tensor_scalar(ohr[:, k, :], overc[:, :], float(k + 1), None, ALU.is_equal))
            own.settle()
            for k in range(3):
                own.do(V.tensor_tensor(ohr[:, k, :], ohr[:, k, :], over[:, :], ALU.mult))
            own.do(V.memset(eF[:, 8:12], 0.0))
            own.do(V.tensor_copy(eF[:, 0:8], iota8[:, :]))
            for q in range(NT):
                own.do(V.tensor_scalar(placeR[:, q, 0:8], placed[:, q, :], -1.0, None, ALU.add))
                own.do(V.tensor_copy(gateR[:, q, 0:8], G[:, q, :]))
            own.settle()
            for k in range(3):
                for src, dst in ([(iota8[:, :], eF[:, 8 + k:9 + k])]
                                 + [(placed[:, q, :], placeR[:, q, 8 + k:9 + k]) for q in range(NT)]
                                 + [(G[:, q, :], gateR[:, q, 8 + k:9 + k]) for q in range(NT)]):
                    own.do(V.tensor_tensor(prod[:, :], ohr[:, k, :], src, ALU.mult))
                    own.settle()
                    own.do(V.tensor_reduce(dst, prod[:, :], AX_X, ALU.add))
                    own.settle()
            for q in range(NT):
                own.do(V.tensor_scalar(placeR[:, q, 8:11], placeR[:, q, 8:11], -1.0 - P, None, ALU.add))
                own.do(V.memset(placeR[:, q, 11:12], -1.0))
                own.do(V.memset(gateR[:, q, 11:12], 0.0))
            own.do(V.tensor_copy(eI[:, :], eF[:, :]))
            own.settle()
            V.tensor_copy(rI[:, :], rF[:, :]).then_inc(s_route, 1)
            dve.wait_ge(s_route, 1)
            rounds = dve.value_load(rI[0:1, 0:1], min_val=EXPERTS, max_val=MAX_ROUNDS)

            def select():
                own.settle()
                for q in range(NT):
                    i = V.tensor_scalar(S[:, q, :], iota128[:, :], pcol[:, q:q + 1], None, ALU.is_equal)
                    if q:
                        i.then_inc(s_S, 1)
                    else:
                        own.do(i)

            def hs_lo(b, g):
                for kk in range(4):
                    k = 4 * g + kk
                    lo_of(hsl[:, k, :], b[:, kk * P:(kk + 1) * P], hsh[:, k, :],
                          gains[:, 1, 1, k:k + 1], last=(kk == 3))

            own.do(V.tensor_copy(pcol[:, :], placeR[:, :, 0]))
            select()
            for g in range(2):
                n = TR_AT[1, "hs", g]
                thi[0] += 1
                dve.wait_ge(s_thi, thi[0])
                hs_lo(bank(4 + n % 2), g)
            own.per = 3
            base = own.n
            THI0 = thi[0]
            with dve.Fori(0, rounds) as r:
                own.r = r
                his = [0]

                def hi_taken(name):
                    his[0] += 1
                    dve.wait_ge(s_thi, r * (2 + NJ) + (THI0 + his[0]))
                    return bank(4 + (TR0 + ROUND_TR.index(name)) % 2)

                def act_lo(j):
                    b = hi_taken(f"act{j}")
                    V.tensor_tensor(bTl[:, j % 2].rearrange("p k n -> p (k n)"), b[:, 0:256],
                                    bTh[:, j % 2].rearrange("p k n -> p (k n)").bitcast(F32),
                                    ALU.subtract).then_inc(s_trf, 1)

                own.do(V.tensor_copy(gcol[:, :], gateR[:, :, bass.ds(r, 1)].rearrange("p t o -> p (t o)")))
                for i in range(SEG):
                    round_split(dve_split, dve, i, r)
                    kind, j = ROUND_SLOTS[i]
                    if i == 0:
                        n = TR0 + ROUND_TR.index("ST")
                        dve.wait_ge(s_tr, r * R_TR + (n + 1))
                        V.tensor_copy(ST[:, :], bank(4 + n % 2)[:, 0:256]).then_inc(s_trf, 1)
                    if i == SEG // 2:
                        own.do(V.tensor_copy(pcol[:, :], placeR[:, :, bass.ds(r + 1, 1)].rearrange("p t o -> p (t o)")))
                        select()
                    if kind == "u":
                        if j and j < NJ - 1:
                            act_lo(j - 1)
                        dve.wait_ge(s_sg, r * NJ + (GU0 + j + 1))
                        if j == NJ - 1:
                            dve.wait_ge(s_tr, r * R_TR + (TR0 + ROUND_TR.index(f"act{j - 1}") + 1))
                        V.tensor_tensor(act_t[:, 0, :], sg[:, 0, :], bank(6 + j % 2)[:, FB:2 * FB], ALU.mult).then_inc(s_act, 1)
                        if j == NJ - 1:
                            act_lo(j - 1)
                            hs_lo(hi_taken("hs0"), 0)
                            act_lo(j)
                            hs_lo(hi_taken("hs1"), 1)
                for q in range(NT):
                    for c in range(2):
                        dve.wait_ge(s_scat, r * 4 + (2 * q + c + 1))
                        V.scalar_tensor_tensor(x[:, q, c * 512:(c + 1) * 512], bank(2 + c), gcol[:, q:q + 1],
                                               x[:, q, c * 512:(c + 1) * 512], ALU.mult, ALU.add).then_inc(s_scatv, 1)
                dve.wait_ge(s_scatv, r * 4 + 4)
            assert own.n - base == own.per
            V.tensor_copy(pcol[:, 0:1], rF[:, :]).then_inc(s_xn, 1)
            dve.wait_ge(s_gf, 16)
            dve.wait_ge(s_rstd, 5)
            for q in range(NT):
                V.scalar_tensor_tensor(outt[:, q, :], x[:, q, :], rstd[:, q:q + 1], gfin[:, :], ALU.mult,
                                       ALU.mult).then_inc(s_fin, 1)

        @block.tensor
        def _(pe):
            mm = nc.tensor.matmul

            def mm3(out, lh, ll, rh, rl, start, stop):
                mm(out, lh, rh, start=start, stop=False)
                mm(out, ll, rh, start=False, stop=False)
                return mm(out, lh, rl, start=False, stop=stop)

            def tr_bank(n):
                if n >= 2:
                    pe.wait_ge(s_trf, n - 1)
                return bank(4 + n % 2)

            def tr_bank_r(r, name):
                n = TR0 + ROUND_TR.index(name)
                pe.wait_ge(s_trf, r * R_TR + (n - 1))
                return bank(4 + n % 2)

            def transposes(dst, srcs):
                for k, s in enumerate(srcs):
                    i = nc.tensor.transpose(dst[:, k * P:(k + 1) * P], s, ident[:, :])
                i.then_inc(s_tr, 1)

            def to_T(l, name, src):
                for g in range(4):
                    transposes(tr_bank(TR_AT[l, name, g]),
                               [src[:, q, k * P:(k + 1) * P] for k in (2 * g, 2 * g + 1) for q in range(NT)])

            def tail(l, s):
                for what, h in mixer_tail(s):
                    if what == "scores":
                        if h == 0:
                            acc_free(l, 5)
                            pe.wait_ge(s_trf, TR_AT[l, "qkT", 9] + 1)
                        else:
                            pe.wait_ge(s_ex, HEADS * l + h)
                        for c in range(2):
                            for q in (1, 0):
                                n, off = (q + 1) * P, (1 - q) * 256
                                mm(bank(2 + c)[:, off:off + n], qT[c * 64:(c + 1) * 64, h, q * P:(q + 1) * P],
                                   kT[c * 64:(c + 1) * 64, h, 0:n], start=(q == 1), stop=False)
                                i = mm(bank(2 + c)[:, off + q * P:off + n], identb[:, :], maskb[:, :],
                                       start=False, stop=(q == 0))
                        i.then_inc(s_sc, 1)
                    elif what == "wT":
                        b = tr_bank(TR_AT[l, "wT", h])
                        pe.wait_ge(s_w, HEADS * l + h + 1)
                        transposes(b, [prob[:, 0, k * P:(k + 1) * P] for k in range(3)])
                    elif what == "o":
                        b = tr_bank(TR_AT[l, "o", h])
                        pe.wait_ge(s_trf, TR_AT[l, "wT", h] + 1)
                        if h == 0:
                            pe.wait_ge(s_accA, ACCA_L * l + 6)
                        vh = [v[:, q, h * P:(h + 1) * P] for q in range(NT)]
                        mm(b[:, 0:P], wT[:, 0:P], vh[0], start=True, stop=False)
                        mm(b[:, P:2 * P], wT[:, P:2 * P], vh[0], start=False, stop=False)
                        mm(b[:, P:2 * P], wT[:, 2 * P:3 * P], vh[1], start=False, stop=True).then_inc(s_tr, 1)
                    elif what == "oT":
                        b = tr_bank(TR_AT[l, "oT", h])
                        pe.wait_ge(s_on, HEADS * l + h + 1)
                        transposes(b, [osb[:, q * P:(q + 1) * P] for q in range(NT)])
                    elif what == "qkT":
                        for q in range(NT):
                            b = tr_bank(TR_AT[l, "qkT", 2 * h + q])
                            pe.wait_ge(s_rope, 8 * l + 2 * (h - 1) + q + 1)
                            src = ropeA if q == 0 else ropeC
                            transposes(b, [src[:, k * P:(k + 1) * P] for k in range(4)])
                    elif what == "bu":
                        kt, q = h // 4, h % 4
                        if h == 0:
                            pe.wait_ge(s_accA, ACCA_L * l + 2)
                            pe.wait_ge(s_b, 256 * (l + 1))
                        if h or l:
                            pe.wait_ge(s_buf, PAIRS * l + h)
                        rows = slice(32 * q, 32 * q + 32)
                        mm(bank(6)[:, 0:256], Bre[rows, kt, :], uT[rows, kt, :], start=True, stop=False)
                        mm(bank(6)[:, 256:512], Bim[rows, kt, :], uT[rows, kt, :], start=False, stop=True).then_inc(s_bu, 1)
                    elif what == "y":
                        pe.wait_ge(s_rot, CHUNKS * l + h + 1)
                        kt = h // 2
                        if h == 0:
                            pe.wait_ge(s_prep, l + 1)
                        if kt >= 2:
                            pe.wait_ge(s_yv, CT * l + kt - 1)
                        for k in range(2):
                            p = 2 * h + k
                            q = p % 4
                            o = PS[32 * q:32 * q + 32, 7, (kt % 2) * 256:(kt % 2 + 1) * 256]
                            mm(o, Cre[:, p, :], sr[:, h % 2, k, :], start=True, stop=False)
                            i = mm(o, Cin[:, p, :], ri[:, h % 2, k, :], start=False, stop=True)
                        i.then_inc(s_yc, 1)

            def acc_free(l, b):
                if b in EVAC_BY_ACT:
                    pe.wait_ge(s_accA, ACCA_L * l + 2 * sum(1 for k in range(b + 1) if k in EVAC_BY_ACT))
                else:
                    pe.wait_ge(s_accV, ACCV_L * l + 2 * sum(1 for k in range(b + 1) if k not in EVAC_BY_ACT))

            pe.wait_ge(s_const, 1)
            for l in range(DEPTH):
                seg = 2 * l
                pe.wait_ge(s_xn, 1 if l == 0 else 4)
                to_T(l, "h1", xn)
                pe.wait_ge(s_trf, TR_AT[l, "h1", 3] + 1)
                for s in range(SEG):
                    blk, h, nh = slot_block(s)
                    pair = PAIR_OF[blk]
                    if h == 0:
                        before = [k for k in range(blk) if PAIR_OF[k] == pair]
                        if before:
                            acc_free(l, before[-1])
                        if blk == PS0 + 1:
                            pe.wait_ge(s_ex, HEADS * (l + 1))
                    if blk == GLU:
                        pe.wait_ge(s_ygl, 2 * l + 1)
                    if blk == PS0:
                        pe.wait_ge(s_ygl, 2 * l + 2)
                    if blk == PA0:
                        pe.wait_ge(s_trf, TR_AT[l, "oT", 3 + 4 * h] + 1)
                    if blk == WO0 and h == 0:
                        pe.wait_ge(s_trf, TR_AT[l, "mT", 3] + 1)
                    pe.wait_ge(s_lo, nslot(seg, s) + 1)
                    H, L = parts(seg, s, 4)
                    if blk in (U_BLOCK, GLU):
                        ah, al = (hTh, hTl) if blk == U_BLOCK else (ySh, ySl)
                        for c in range(CT):
                            o = bank(2 * pair + c // 2)[:, (c % 2) * 256:(c % 2 + 1) * 256]
                            for kk in range(4):
                                k = 4 * h + kk
                                cs = slice(c * P, (c + 1) * P)
                                i = mm3(o, H[:, kk, cs], L[:, kk, cs], ah[:, k, :], al[:, k, :],
                                        start=(k == 0 and c % 2 == 0), stop=(kk == 3 and h == nh - 1 and c % 2 == 1))
                            if h == nh - 1 and c % 2:
                                i.then_inc(s_acc, 1)
                            elif h < nh - 1 and c == CT - 1:
                                i.then_inc(s_used, 1)
                    else:
                        ah, al = ((ySh, ySl) if blk in (PS0, PS0 + 1) else (yBh, yBl) if blk in (PA0, PA0 + 1)
                                  else (hTh, hTl))
                        for q in range(NT):
                            o = bank(2 * pair + q)
                            for kk in range(4):
                                k = 4 * h + kk
                                tk = slice(q * P, (q + 1) * P)
                                i = mm3(o, ah[:, k, tk], al[:, k, tk], H[:, kk, :], L[:, kk, :],
                                        start=(k == 0), stop=(kk == 3 and h == nh - 1))
                            if h == nh - 1:
                                i.then_inc(s_acc, 1)
                            elif q == NT - 1:
                                i.then_inc(s_used, 1)
                    tail(l, s)
                    if s == 28:
                        pe.wait_ge(s_m, l + 1)
                        to_T(l, "mT", gs)
                pe.wait_ge(s_xn, 2 + 3 * l)
                to_T(l, "h2", xn)
                pe.wait_ge(s_trf, TR_AT[l, "h2", 3] + 1)
                if l == 0:
                    def turn2(j):
                        b = tr_bank(TR_AT[0, "act", j])
                        pe.wait_ge(s_act, NT * (j + 1))
                        transposes(b, [act_t[:, q, k * P:(k + 1) * P] for k in range(2) for q in range(NT)])

                    def gate_up2(j):
                        ig, iu = FFN_AT["g", j], FFN_AT["u", j]
                        for q in range(NT):
                            if q and j:
                                turn2(j - 1)
                            tk = slice(q * P, (q + 1) * P)
                            if j:
                                pe.wait_ge(s_act, NT * (j - 1) + q + 1)
                            for n, i_ in enumerate((ig, iu)):
                                if q == 0:
                                    pe.wait_ge(s_lo, nslot(1, i_) + 1)
                                H, L = parts(1, i_, KD)
                                for k in range(KD):
                                    i = mm3(bank(6 + q)[:, n * FB:(n + 1) * FB], hTh[:, k, tk], hTl[:, k, tk],
                                            H[:, k, :], L[:, k, :], start=(k == 0 and n == 0), stop=(k == KD - 1 and n == 1))
                                if n == 0 and q == NT - 1:
                                    i.then_inc(s_used, 1)
                            i.then_inc(s_gu, 1)

                    gate_up2(0)
                    for j in range(NJ):
                        if j < NJ - 1:
                            gate_up2(j + 1)
                        if j == NJ - 1:
                            turn2(j)
                        i_ = FFN_AT["d", j]
                        pe.wait_ge(s_trf, TR_AT[0, "act", j] + 1)
                        pe.wait_ge(s_lo, nslot(1, i_) + 1)
                        H, L = parts(1, i_, 2)
                        for q in range(NT):
                            for c in range(2):
                                for k in range(2):
                                    i = mm3(bank(2 * q + c), aTh[:, k, q * P:(q + 1) * P], aTl[:, k, q * P:(q + 1) * P],
                                            H[:, k, c * 512:(c + 1) * 512], L[:, k, c * 512:(c + 1) * 512],
                                            start=(j == 0 and k == 0), stop=(j == NJ - 1 and k == 1))
                        i.then_inc(s_used, 1)

            pe.wait_ge(s_rw, 16)
            b = tr_bank(TR_AT[1, "logits", 0])
            for q in range(NT):
                for k in range(KD):
                    for n, a in enumerate((hTh, hTl)):
                        i = mm(b[:, q * 8:(q + 1) * 8], a[:, k, q * P:(q + 1) * P].bitcast(F32), rw[:, k, :],
                               start=(q == 0 and k == 0 and n == 0), stop=(q == 1 and k == KD - 1 and n == 1))
            i.then_inc(s_tr, 1)
            b = tr_bank(TR_AT[1, "places", 0])
            pe.wait_ge(s_M, 1)
            mm(b[:, 0:8], below[:, :], M[:, 0, :], start=True, stop=False)
            mm(b[:, 8:16], ones[:, :], M[:, 0, :], start=False, stop=False)
            mm(b[:, 8:16], below[:, :], M[:, 1, :], start=False, stop=False)
            mm(b[:, 16:24], ones[:, :], M[:, 0, :], start=False, stop=False)
            mm(b[:, 16:24], ones[:, :], M[:, 1, :], start=False, stop=True).then_inc(s_tr, 1)
            pe.wait_ge(s_route, 1)

            def gather(b, g):
                for kk in range(4):
                    k = 4 * g + kk
                    for q in range(NT):
                        i = mm(b[:, kk * P:(kk + 1) * P], xn[:, q, k * P:(k + 1) * P], S[:, q, :],
                               start=(kk == 0 and q == 0), stop=(kk == 3 and q == 1))
                i.then_inc(s_tr, 1)

            pe.wait_ge(s_S, 1)
            for g in range(2):
                gather(tr_bank(TR_AT[1, "hs", g]), g)
            pe.wait_ge(s_trf, TR_AT[1, "hs", 1] + 1)
            rounds = pe.value_load(rI[0:1, 0:1], min_val=EXPERTS, max_val=MAX_ROUNDS)
            with pe.Fori(0, rounds) as r:
                transposes(tr_bank_r(r, "ST"), [S[:, q, :] for q in range(NT)])
                pe.wait_ge(s_trf, r * R_TR + TR0)

                def up(i):
                    kind, j = ROUND_SLOTS[i]
                    n = "gu".index(kind)
                    if n == 0 and j >= 2:
                        pe.wait_ge(s_act, r * NJ + (GU0 + j - 1))
                    pe.wait_ge(s_lo, nslot(3, i, r) + 1)
                    H, L = parts(3, i, KD)
                    for k in range(KD):
                        m = mm3(bank(6 + j % 2)[:, n * FB:(n + 1) * FB], hsh[:, k, :], hsl[:, k, :],
                                H[:, k, :], L[:, k, :], start=(k == 0 and n == 0), stop=(k == KD - 1 and n == 1))
                    m.then_inc(s_gu if n else s_used, 1)

                def turn(j):
                    b = tr_bank_r(r, f"act{j}")
                    pe.wait_ge(s_act, r * NJ + (GU0 + j + 1))
                    transposes(b, [act_t[:, 0, k * P:(k + 1) * P] for k in range(2)])

                def down(i):
                    j = ROUND_SLOTS[i][1]
                    pe.wait_ge(s_lo, nslot(3, i, r) + 1)
                    pe.wait_ge(s_trf, r * R_TR + (TR0 + ROUND_TR.index(f"act{j}") + 1))
                    H, L = parts(3, i, 2)
                    for c in range(2):
                        for k in range(2):
                            m = mm3(bank(c), bTh[:, j % 2, k, :], bTl[:, j % 2, k, :], H[:, k, c * 512:(c + 1) * 512],
                                    L[:, k, c * 512:(c + 1) * 512], start=(j == 0 and k == 0),
                                    stop=(j == NJ - 1 and k == 1))
                    m.then_inc(s_used, 1)

                for i in range(SEG):
                    kind, j = ROUND_SLOTS[i]
                    if kind == "d":
                        down(i)
                        continue
                    up(i)
                    if kind == "u" and j:
                        turn(j - 1)
                        if j == NJ - 1:
                            pe.wait_ge(s_S, r + 2)
                            gather(tr_bank_r(r, "hs0"), 0)
                            turn(j)
                            gather(tr_bank_r(r, "hs1"), 1)
                for q in range(NT):
                    for c in range(2):
                        if q == 0:
                            pe.wait_ge(s_ysb, r * 2 + (c + 1))
                        if q:
                            pe.wait_ge(s_scatv, r * 4 + (c + 1))
                        mm(bank(2 + c), ST[:, q * P:(q + 1) * P], ysb[:, c * 512:(c + 1) * 512],
                           start=True, stop=True).then_inc(s_scat, 1)


INPUTS = {
    "x": lambda a: a["x"].reshape(SEQ, D),
    "positions": lambda a: a["positions"].reshape(NT, P).transpose(1, 0),
    "mix_norm": lambda a: a["mix_norm"].reshape(DEPTH, KD, P).transpose(2, 0, 1),
    "ffn_norm": lambda a: a["ffn_norm"].reshape(DEPTH, KD, P).transpose(2, 0, 1),
    "subln": lambda a: a["subln"].transpose(1, 0),
    "b_glu": lambda a: a["b_glu"].reshape(DEPTH, CT, P).transpose(2, 0, 1),
    "ssm_d": lambda a: a["ssm_d"].reshape(DEPTH, CT, P).transpose(2, 0, 1),
    "lam_re": lambda a: a["ssm_lambda_re"].reshape(DEPTH, PAIRS, P).transpose(2, 0, 1),
    "lam_im": lambda a: a["ssm_lambda_im"].reshape(DEPTH, PAIRS, P).transpose(2, 0, 1),
    "log_dt": lambda a: a["ssm_log_dt"].reshape(DEPTH, PAIRS, 2).transpose(2, 0, 1),
    "b_re": lambda a: a["ssm_b_re"].transpose(0, 1, 3, 2).reshape(DEPTH, SSM_W, STATE),
    "b_im": lambda a: a["ssm_b_im"].transpose(0, 1, 3, 2).reshape(DEPTH, SSM_W, STATE),
    "c_re": lambda a: a["ssm_c_re"].reshape(DEPTH, PAIRS, 2, GCH, STATE).transpose(0, 2, 4, 1, 3).reshape(DEPTH, P, PAIRS, GCH),
    "c_im": lambda a: a["ssm_c_im"].reshape(DEPTH, PAIRS, 2, GCH, STATE).transpose(0, 2, 4, 1, 3).reshape(DEPTH, P, PAIRS, GCH),
    "inv_freq": lambda a: (10000.0 ** (-np.arange(0, HD, 2, dtype=np.float32) / HD)).astype(np.float32),
    "router_w": lambda a: a["router_w"].reshape(D, EXPERTS),
    "moe_w_gate": lambda a: a["moe_w_gate"].reshape(EXPERTS, D, FF),
    "moe_w_up": lambda a: a["moe_w_up"].reshape(EXPERTS, D, FF),
    "moe_w_down": lambda a: a["moe_w_down"].reshape(EXPERTS, FF, D),
}
for _n in ("w_in", "w_glu", "w_proj_ssm", "w_proj_attn", "w_out", "lambda_q1", "lambda_k1", "lambda_q2", "lambda_k2",
           "dense_w_gate", "dense_w_up", "dense_w_down", "final_norm"):
    INPUTS[_n] = (lambda n: lambda a: a[n])(_n)


def kernel(**inputs):
    import concourse.bacc as bacc
    from concourse.bass_utils import run_bass_kernel_spmd

    nc = bacc.Bacc("TRN2", target_bir_lowering=False, num_devices=1)
    arrays, t = {}, {}
    given = {k: np.asarray(v) for k, v in inputs.items()}
    for name, lay in INPUTS.items():
        a = np.ascontiguousarray(lay(given))
        arrays[f"in_{name}"] = a
        t[name] = nc.dram_tensor(f"in_{name}", a.shape, mybir.dt.from_np(a.dtype), kind="ExternalInput").ap()
    t["out"] = nc.dram_tensor("out_trunk", (SEQ, D), F32, kind="ExternalOutput").ap()
    trunk(nc, t)
    r = run_bass_kernel_spmd(nc, [arrays], core_ids=[0])
    return r.results[0]["out_trunk"].reshape(1, SEQ, D)
```

```python
import math
from contextlib import ExitStack

import numpy as np

import concourse.bass as bass
from concourse import mybir

F32 = mybir.dt.float32
F32R = mybir.dt.float32r
BF16 = mybir.dt.bfloat16
I32 = mybir.dt.int32
U32 = mybir.dt.uint32
ALU = mybir.AluOpType
ACT = mybir.ActivationFunctionType
AX_X = mybir.AxisListType.X

P = 128
SEQ, D, DEPTH = 256, 1024, 2
NT = SEQ // P
KD = D // P
GROUPS, GCH, STATE = 32, 16, 64
PAIRS = GROUPS * STATE // P
SSM_W = GROUPS * GCH
CT = SSM_W // P
CHUNKS = PAIRS // 2
HEADS, HD = 8, 64
SCALE = HD ** -0.5
FF, EXPERTS = 2816, 8
FB = 256
NJ = FF // FB
EPS, SUB_EPS = 1e-6, 1e-5
DOUBLINGS = [1 << n for n in range(8)]
PROLOGUE = 0
NEG = -1.0e30
MAX_ROUNDS = EXPERTS + 3
TWO_PI_HI, TWO_PI_MID = 6.28125, 0.0019350051879882812
TWO_PI_LO = 2 * math.pi - TWO_PI_HI - TWO_PI_MID
ROUND = 12582912.0
PI_IN = 3.1415925

SLOT = 2048
SEG = 33
NRAW, NW, AHEAD = 4, 3, 2
RAW_POS = [i % 4 if i < 24 else (i - 24) % 3 for i in range(SEG)]
RAW_USES = [RAW_POS.count(p) for p in range(NRAW)]
GROUP_BLOCK = 512
BLOCK_COUNT = 18
U_BLOCK, GLU, PS0, PA0, WO0 = 0, 11, 12, 13, 16
PAIR_OF = [0, 1, 0, 1, 0, 1, 0, 0, 0, 0, 0, 0, 0, 1, 0, 1, 0, 1]
LATE_SLOTS = [(11, 0, 1), (13, 0, 2), (12, 0, 1), (13, 1, 2), (14, 0, 1), (15, 0, 2), (15, 1, 2),
              (16, 0, 2), (17, 0, 2), (16, 1, 2), (17, 1, 2)]
EVAC_BY_ACT = {0, 5, 6, 7, 8, 9, 10, 11}
ACCA_L = 2 * len(EVAC_BY_ACT)
ACCV_L = 2 * (BLOCK_COUNT - len(EVAC_BY_ACT))


def slot_block(i):
    if i < 22:
        return i // 2, i % 2, 2
    return LATE_SLOTS[i - 22]


GELU_FROM = {9: 0, 13: 1, 17: 2, 21: 3}
GELU_TO = {10: 0, 14: 1, 18: 2, 21: 3}


def block_column(b):
    return ((b - PS0) // 2 if b < WO0 else b - WO0) * 512


def lam_init(l):
    return 0.8 - 0.6 * math.exp(-0.3 * l)


FFN_SLOTS = [("g", 0), ("u", 0)]
for _j in range(NJ - 1):
    FFN_SLOTS += [("g", _j + 1), ("u", _j + 1), ("d", _j)]
FFN_SLOTS += [("d", NJ - 1)]
FFN_AT = {what: i for i, what in enumerate(FFN_SLOTS)}

ROUND_SLOTS = [("g", 0), ("u", 0), ("g", 1), ("u", 1)]
for _j in range(NJ - 2):
    ROUND_SLOTS += [("g", _j + 2), ("d", _j), ("u", _j + 2)]
ROUND_SLOTS += [("d", NJ - 2), ("d", NJ - 1)]
ROUND_AT = {what: i for i, what in enumerate(ROUND_SLOTS)}
SCATTER_BANKS = [2, 3, 7, 2]
NR, RAHEAD = 5, 3
LOADED = NR + RAHEAD
ROUND_POS = [i % 5 if i < 25 else (i - 25) % 4 for i in range(SEG)]
ROUND_USES = [ROUND_POS.count(p) for p in range(NR)]


COLUMN_ARRAYS = [
    ("norms", 2 * DEPTH * KD, lambda a: np.stack([by_chunk(a["mix_norm"], KD), by_chunk(a["ffn_norm"], KD)], 1)),
    ("b_glu", DEPTH * CT, lambda a: by_chunk(a["b_glu"], CT)),
    ("ssm_d", DEPTH * CT, lambda a: by_chunk(a["ssm_d"], CT)),
    ("lam_re", DEPTH * PAIRS, lambda a: by_chunk(a["ssm_lambda_re"], PAIRS)),
    ("lam_im", DEPTH * PAIRS, lambda a: by_chunk(a["ssm_lambda_im"], PAIRS)),
    ("log_dt", DEPTH * PAIRS, lambda a: np.repeat(a["ssm_log_dt"].reshape(DEPTH, PAIRS, 2).transpose(2, 0, 1), STATE, 0)),
    ("subln", DEPTH, lambda a: a["subln"].transpose(1, 0)),
]
COL_AT = {n: sum(k for _, k, _ in COLUMN_ARRAYS[:i]) for i, (n, _, _) in enumerate(COLUMN_ARRAYS)}
COLUMNS = sum(k for _, k, _ in COLUMN_ARRAYS)


def before_in(pos, i):
    for back in range(i - 1, i - 1 - SEG, -1):
        if pos[back % SEG] == pos[i]:
            return back


def mixer_mid(s):
    todo = []
    if s in (6, 8, 10, 12):
        todo.append(("qkT", (s - 4) // 2))
    if 0 <= s - 15 < HEADS:
        todo.append(("scores", s - 15))
    if 0 <= s - 16 < HEADS:
        todo.append(("wT", s - 16))
    return todo


def mixer_tail(s):
    todo = []
    if 0 <= s - 16 < HEADS:
        todo.append(("o", s - 16))
    if 0 <= s - 17 < HEADS:
        todo.append(("oT", s - 17))
    if 0 <= s - 2 < PAIRS:
        todo.append(("bu", s - 2))
    if s >= 6 and (s - 6) % 2 == 0 and (s - 6) // 2 < CHUNKS:
        todo.append(("y", (s - 6) // 2))
    if s in (27, 29):
        todo.append(("mT", (s - 27) // 2))
    return todo


TR = []
for _l in range(DEPTH):
    TR += [(_l, "h1", g) for g in range(4)]
    for _s in range(SEG):
        for _w, _h in mixer_mid(_s) + mixer_tail(_s):
            if _w in ("wT", "o", "oT"):
                TR.append((_l, _w, _h))
            if _w in ("qkT", "mT"):
                TR += [(_l, _w, 2 * _h), (_l, _w, 2 * _h + 1)]
    TR += [(_l, "h2", g) for g in range(4)]
    TR += [(_l, "act", j) for j in range(NJ)] if _l == 0 else [(1, "logitsT", 0), (1, "logits", 0), (1, "places", 0),
                                                                    (1, "hs", 0), (1, "hs", 1)]
TR_AT = {what: n for n, what in enumerate(TR)}
ROUND_TR = ["ST"] + [f"act{j}" for j in range(NJ - 1)] + ["hs0", f"act{NJ - 1}", "hs1"]


def trunk(nc, t):
    ctx = ExitStack()
    with ctx:
        here = [(nc.sbuf_base + 63) // 64 * 64]

        def at(name, shape, dt, addr):
            return nc.alloc_sbuf_tensor_at(name, list(shape), dt, offset=addr)

        def size(shape, dt):
            n = 2 if dt == BF16 else 4
            for s in shape[1:]:
                n *= s
            return (n + 31) // 32 * 32

        def sb(name, shape, dt=F32):
            a = here[0]
            here[0] += size(shape, dt)
            return at(name, shape, dt, a)

        def room(nbytes):
            a = here[0]
            here[0] += nbytes
            return a

        def sem(name):
            return ctx.enter_context(nc.semaphore(name))

        x = sb("x_tok", [P, NT, D])
        hTh = sb("hT_hi", [P, KD, SEQ], F32R)
        hTl = sb("hT_lo", [P, KD, SEQ], F32R)
        raw = sb("w_raw", [P, NRAW, SLOT])
        wh = sb("w_hi", [P, NW, SLOT], F32R)
        wl = sb("w_lo", [P, NW, SLOT], F32R)
        ident = sb("ident", [P, P])
        identb = sb("identb", [P, P], BF16)
        maskb = sb("maskb", [P, P], BF16)
        cosT = sb("rope_cos", [P, NT, 32])
        sinT = sb("rope_sin", [P, NT, 32])
        nsinT = sb("rope_nsin", [P, NT, 32])
        cols = sb("columns", [P, COLUMNS])

        def column(name, k, **split):
            inner = " ".join(split)
            return cols[:, COL_AT[name]:COL_AT[name] + k].rearrange(f"p ({inner} k) -> p {inner} k", **split)

        gains = column("norms", 2 * DEPTH * KD, w=2, l=DEPTH)
        subg = cols[:, COL_AT["subln"]:COL_AT["subln"] + DEPTH]
        bglu = column("b_glu", DEPTH * CT, l=DEPTH)
        dskip = column("ssm_d", DEPTH * CT, l=DEPTH)
        lre = column("lam_re", DEPTH * PAIRS, l=DEPTH)
        lim = column("lam_im", DEPTH * PAIRS, l=DEPTH)
        ldt = column("log_dt", DEPTH * PAIRS, l=DEPTH)
        nlam = sb("minus_lambda", [P, DEPTH])
        mhalf = sb("minus_half", [P, 4])
        s5m = sb("s5_mag", [P, DEPTH, PAIRS])
        s5c = sb("s5_cos", [P, DEPTH, PAIRS])
        s5s = sb("s5_sin", [P, DEPTH, PAIRS])
        s5fr = sb("s5_fr", [P, DEPTH, PAIRS])
        s5fi = sb("s5_fi", [P, DEPTH, PAIRS])
        stat = sb("norm_stat", [P, 4])
        mean = sb("norm_mean", [P, 4])
        rstd = sb("norm_rstd", [P, 4])
        mx = sb("score_max", [P, 4])
        nb = sb("exp_bias", [P, 4])
        sm = sb("exp_sum", [P, 4])
        rs = sb("exp_rsum", [P, 4])
        c2 = sb("second_map_coef", [P, 2])
        oss = sb("o_stat", [P, 2])
        oms = sb("o_mean", [P, 2])
        ors = sb("o_rstd", [P, 2])
        wpow = sb("turn_dve", [P, 8, 4])
        wpowp = sb("turn_pool", [P, 8, 4])

        a_q, a_k, a_v = room(8192), room(8192), room(8192)
        a_u, a_yh, a_yl = room(4096), room(4096), room(4096)
        a_tab = room(32768)
        a_rr, a_ri, a_sr, a_tt, a_t12 = room(4096), room(4096), room(4096), room(2048), room(2048)
        a_att = room(6144)
        qT = at("qT", [P, HEADS, SEQ], F32, a_q)
        kT = at("kT", [P, HEADS, SEQ], F32, a_k)
        v = at("v_tok", [P, NT, D], F32, a_v)
        outsq = at("square_out", [P, NT, D], F32, a_q)
        xn = at("x_normed", [P, NT, D], F32, a_v)
        uT = at("uT", [P, CT, SEQ], F32, a_u)
        ySh = at("yS_hi", [P, CT, SEQ], F32R, a_yh)
        ySl = at("yS_lo", [P, CT, SEQ], F32R, a_yl)
        tab = at("s5_turns", [P, PAIRS, 2, SEQ], F32, a_tab)
        gs = at("gate_ssm", [P, NT, D], F32, a_tab)
        ga = at("gate_attn", [P, NT, D], F32, a_tab + 8192)
        yBh = at("yB_hi", [P, KD, SEQ], F32R, a_tab + 16384)
        yBl = at("yB_lo", [P, KD, SEQ], F32R, a_tab + 24576)
        rr = at("s5_r_re", [P, 2, 2, SEQ], F32, a_rr)
        ri = at("s5_r_im", [P, 2, 2, SEQ], F32, a_ri)
        sr = at("s5_s_re", [P, 2, 2, SEQ], F32, a_sr)
        tt = at("s5_pool_tmp", [P, 2, SEQ], F32, a_tt)
        t12 = at("s5_dve_tmp", [P, 2, SEQ], F32, a_t12)
        tabt = at("turn_tmp_dve", [P, 8, P], F32, a_rr)
        tabp = at("turn_tmp_pool", [P, 8, P], F32, a_sr)
        gel = at("gelu_tmp", [P, CT, SEQ], F32, a_yl)
        gth = at("gelu_tanh", [P, CT, SEQ], F32, a_yh)
        glt = at("glu_tanh", [P, CT, SEQ], F32, a_rr)
        ropeA = at("rope_a", [P, 512], F32, a_att)
        ropeB = at("rope_b", [P, 512], F32, a_att + 2048)
        ropeC = at("rope_c", [P, 512], F32, a_att + 4096)
        prob = at("prob", [P, 2, 384], F32, a_att)
        wT = at("attn_wT", [P, 384], F32, a_att + 3072)
        osq = sb("o_square_out", [P, 256])
        osb = at("o_tok", [P, 256], F32, a_att + 4608)
        Bst = sb("s5_b", [P, 2, CT, P])
        Cre = sb("s5_c_re", [P, PAIRS, 32])
        Cin = sb("s5_c_nim", [P, PAIRS, 32])
        act_t = at("act_tok", [P, NT, FB], F32, a_q)
        sg = at("silu_g", [P, NT, FB], F32, a_q + 2048)
        aTh = at("actT_hi", [P, 2, SEQ], F32R, a_q + 4096)
        aTl = at("actT_lo", [P, 2, SEQ], F32R, a_q + 6144)
        hsh = at("hsT_hi", [P, KD, P], F32R, a_k)
        hsl = at("hsT_lo", [P, KD, P], F32R, a_k + 4096)
        bTh = at("eactT_hi", [P, 2, 2, P], F32R, a_yl)
        bTl = at("eactT_lo", [P, 2, 2, P], F32R, a_yl + 2048)
        rawx = at("w_raw_more", [P, 1, SLOT], F32, a_tab + 8192)
        whx = [at("w_hi_more0", [P, 1, SLOT], F32R, a_rr), at("w_hi_more1", [P, 1, SLOT], F32R, a_tab + 16384)]
        wlx = [at("w_lo_more0", [P, 1, SLOT], F32R, a_rr + 8192), at("w_lo_more1", [P, 1, SLOT], F32R, a_tab + 24576)]
        ysb = at("y_slots", [P, D], F32, a_yh)
        S = at("select", [P, NT, P], F32, a_att)
        ST = at("selectT", [P, SEQ], F32, a_att + 1024)
        gfin = at("final_gain", [P, D], F32, a_u)
        outt = at("out_tok", [P, NT, D], F32, a_k)
        mp = [a_tab]

        def rt(name, shape, dt=F32):
            a = mp[0]
            mp[0] += size(shape, dt)
            return at(name, shape, dt, a)

        rw = rt("router_w", [P, KD, EXPERTS])
        rwh = rt("router_w_hi", [P, KD, EXPERTS], F32R)
        rwl = rt("router_w_lo", [P, KD, EXPERTS], F32R)
        lgT = rt("logits_by_expert", [P, SEQ])
        lg = rt("logits", [P, NT, 8])
        top = rt("top8", [P, NT, 8])
        topi = rt("top8_at", [P, NT, 8], U32)
        topf = rt("top_at_f", [P, NT, 8])
        five = rt("per_expert", [P, 1 + 2 * NT, 8])
        iota8, placed, G = five[:, 0], five[:, 1:1 + NT], five[:, 1 + NT:]
        oh1 = rt("first_choice", [P, NT, 8])
        oh2 = rt("second_choice", [P, NT, 8])
        ex2 = rt("second_exp", [P, NT])
        den = rt("gate_den", [P, NT])
        g1 = rt("gate_first", [P, NT])
        g2 = rt("gate_second", [P, NT])
        M = rt("chosen", [P, NT, 8])
        below = rt("below", [P, P])
        ones = rt("ones", [P, P])
        cnt = rt("expert_counts", [P, 8])
        over = rt("over", [P, 8])
        overc = rt("over_cum", [P, 8])
        ohr = rt("over_round", [P, 3, 8])
        prod = rt("over_prod", [P, 3, 1 + 2 * NT, 8])
        picked = rt("over_picked", [P, 3, 1 + 2 * NT])
        placeR = rt("round_place", [P, NT, 12])
        gateR = rt("round_gate", [P, NT, 12])
        eF = rt("round_expert_f", [P, 12])
        eI = rt("round_expert", [P, 12], I32)
        rF = rt("rounds_f", [P, 1])
        rI = rt("rounds", [P, 1], I32)
        iota128 = rt("iota128", [P, P])
        iotai = rt("iota_int", [P, P], I32)
        pcol = rt("place_now", [P, NT])
        gcol = rt("gate_now", [P, NT])
        sp_ = [a_k]

        def su(name, shape, dt=F32):
            a = sp_[0]
            sp_[0] += size(shape, dt)
            return at(name, shape, dt, a)

        posi = su("positions_int", [P, NT], I32)
        posf = su("positions_f", [P, NT])
        ang = su("angle", [P, NT * 32 + DEPTH * PAIRS])
        angk = su("angle_turns", [P, NT * 32 + DEPTH * PAIRS])
        angr = su("angle_rest", [P, NT * 32 + DEPTH * PAIRS])
        rows_ = su("rows", [P, 4 * DEPTH * HD + HD // 2])
        lamv = rows_[:, 0:4 * DEPTH * HD].rearrange("p (n l d) -> p n l d", n=4, l=DEPTH)
        invf = rows_[:, 4 * DEPTH * HD:]
        lamp = su("lambda_prod", [P, 2, DEPTH, HD])
        lams = su("lambda_sum", [P, 2, DEPTH])
        lame = su("lambda_exp", [P, 2, DEPTH])
        dtt = su("ssm_dt", [P, DEPTH, PAIRS])
        q1 = su("ssm_q1", [P, DEPTH, PAIRS])
        q2 = su("ssm_q2", [P, DEPTH, PAIRS])
        q3 = su("ssm_q3", [P, DEPTH, PAIRS])
        q4 = su("ssm_q4", [P, DEPTH, PAIRS])
        Craw = at("s5_c_raw", [P, 2, PAIRS, GCH], F32, a_att)
        Ctmp = at("s5_c_tmp", [P, 2, PAIRS, GCH], F32, a_att + 2048)
        assert here[0] <= nc.sbuf_usable_end, (here[0], nc.sbuf_usable_end)
        assert mp[0] <= a_tab + 8192 and sp_[0] <= a_k + 8192

        PS = ctx.enter_context(nc.psum_tensor("psum", [P, 8, 512], F32))

        def bank(b):
            return PS[:, b, :]

        s_raw = [sem(f"raw_landed{p}") for p in range(NR)]
        s_hi, s_lo, s_used = sem("w_hi_ready"), sem("w_lo_ready"), sem("w_used")
        s_x0, s_set, s_cols, s_c, s_b = sem("x_landed"), sem("rows_landed"), sem("columns_landed"), sem("c_landed"), sem("b_landed")
        s_gf, s_rw, s_out = sem("final_gain_landed"), sem("router_landed"), sem("out_stored")
        s_pool, s_dve, s_actc = sem("pool_step"), sem("dve_step"), sem("act_step")
        s_const = sem("constants_ready")
        s_ang, s_trig, s_dt = sem("angles_ready"), sem("trig_ready"), sem("dt_ready")
        s_tabp, s_prep = sem("turns_by_pool"), sem("c_scaled")
        s_ss, s_rstd, s_xn = sem("norm_sum"), sem("norm_rstd_ready"), sem("x_normed_ready")
        s_tr, s_thi, s_trf = sem("tr_written"), sem("tr_hi_taken"), sem("tr_free")
        s_acc, s_accA, s_accV = sem("acc_written"), sem("acc_taken_act"), sem("acc_taken_dve")
        s_rope = sem("roped")
        s_bu, s_buf, s_scan, s_rot = sem("bu_written"), sem("bu_taken"), sem("scanned"), sem("turned_back")
        s_yc, s_yv = sem("y_products"), sem("y_taken")
        s_gsq, s_gin, s_gth, s_yg, s_ygh, s_ygl = (sem("gelu_square"), sem("gelu_inner"), sem("gelu_tanh_ready"),
                                                   sem("gelu_ready"), sem("yS_hi_ready"), sem("yS_lo_ready"))
        s_sc, s_nb, s_ex, s_w = sem("scores_written"), sem("exp_bias_ready"), sem("exp_ready"), sem("attn_w_ready")
        s_osq, s_ors, s_on = sem("o_squared"), sem("o_rstd_ready"), sem("o_normed")
        s_m = sem("m_ready")
        s_gu, s_sg, s_act = sem("gate_up_written"), sem("silu_ready"), sem("act_ready")
        s_lg, s_route = sem("exp_second_ready"), sem("routed")
        s_M = sem("choices_ready")
        s_rwh, s_rwl = sem("router_w_hi_ready"), sem("router_w_lo_ready")
        s_S, s_ysb, s_scat, s_scatv = sem("select_ready"), sem("y_copied"), sem("scattered"), sem("scatter_taken")
        s_fin = sem("out_ready")

        R_TR = len(ROUND_TR)
        TR0 = len(TR)
        USED_MIX, USED_FFN = 15, 2 * NJ
        GU0 = NT * NJ

        def used(seg, i, r=None):
            if seg in (0, 2):
                blk, h, n = slot_block(i)
                if h == n - 1:
                    return s_acc, 2 * (BLOCK_COUNT * (seg // 2) + blk + 1)
                mine = sum(1 for k in range(i + 1) if slot_block(k)[1] != slot_block(k)[2] - 1)
                return s_used, (0 if seg == 0 else USED_MIX + USED_FFN) + mine
            slots = FFN_SLOTS if seg == 1 else ROUND_SLOTS
            kind, j = slots[i]
            if kind == "u":
                return s_gu, NT * (j + 1) if seg == 1 else r * NJ + (GU0 + j + 1)
            mine = sum(1 for k in range(i + 1) if slots[k][0] != "u")
            if seg == 1:
                return s_used, USED_MIX + mine
            return s_used, r * USED_FFN + (2 * USED_MIX + USED_FFN + mine)

        def nslot(seg, i, r=None):
            return seg * SEG + i if seg < 3 else r * SEG + (3 * SEG + i)

        def raw_of(seg, i):
            p = (RAW_POS if seg < 3 else ROUND_POS)[i]
            return raw[:, p, :] if p < NRAW else rawx[:, 0, :]

        def split_of(seg, i):
            p = i % NW if seg < 3 else ROUND_POS[i]
            if p < NW:
                return wh[:, p, :], wl[:, p, :]
            return whx[p - NW][:, 0, :], wlx[p - NW][:, 0, :]

        def landed(seg, i, r=None):
            if seg < 3:
                p = RAW_POS[i]
                return s_raw[p], 16 * (seg * RAW_USES[p] + RAW_POS[:i + 1].count(p))
            p = ROUND_POS[i]
            n = (3 * RAW_USES[p] if p < NRAW else 0) + ROUND_POS[:i + 1].count(p)
            return s_raw[p], r * (16 * ROUND_USES[p]) + 16 * n

        def act_split(act, seg, i, r=None, ahead=False):
            s, val = landed(seg, i, r)
            act.wait_ge(s, val + 16 * ROUND_USES[ROUND_POS[i]] if ahead else val)
            if seg == 3 and (r is not PROLOGUE):
                back = before_in(ROUND_POS, i)
                if ahead:
                    s, val = used(3, back + SEG, r)
                elif back >= 0:
                    s, val = used(3, back, r)
                else:
                    s, val = used(3, back + SEG, r)
                    val = val - (NJ if s is s_gu else USED_FFN)
                act.wait_ge(s, val)
            elif seg == 3 or i < NW:
                if seg:
                    act.wait_ge(*used(seg - 1, i - NW + SEG))
            else:
                act.wait_ge(*used(seg, i - NW))
            nc.scalar.activation(split_of(seg, i)[0], raw_of(seg, i), ACT.Copy).then_inc(s_hi, 1)

        def dve_split(dve, seg, i, r=None, ahead=False):
            dve.wait_ge(s_hi, nslot(seg, i + (SEG + 1 if ahead else 1), r))
            h, l_ = split_of(seg, i)
            nc.vector.tensor_tensor(l_, raw_of(seg, i), h.bitcast(F32), ALU.subtract).then_inc(s_lo, 1)

        def split_ahead(split, eng, seg, i):
            if i + AHEAD < SEG:
                split(eng, seg, i + AHEAD)
            elif seg < 2:
                split(eng, seg + 1, i + AHEAD - SEG)

        def parts(seg, i, k):
            return [a.rearrange("p (k n) -> p k n", k=k) for a in split_of(seg, i)]

        def round_split(split, eng, i, r):
            n = i + RAHEAD
            split(eng, 3, n % SEG, r, ahead=n >= SEG)

        class Own:

            def __init__(self, eng, s):
                self.eng, self.s, self.n, self.r, self.per = eng, s, 0, None, 0

            def do(self, ins):
                ins.then_inc(self.s, 1)
                self.n += 1

            def settle(self):
                if self.r is None:
                    self.eng.wait_ge(self.s, self.n)
                else:
                    self.eng.wait_ge(self.s, self.r * self.per + self.n)

        block = ctx.enter_context(nc.Block())

        @block.sync
        def _(sp):
            win = t["w_in"].rearrange("l (c p) n -> l p c n", p=P)
            wglu = t["w_glu"].rearrange("l (c p) n -> l p c n", p=P)
            wps = t["w_proj_ssm"].rearrange("l (c p) n -> l p c n", p=P)
            wpa = t["w_proj_attn"].rearrange("l (c p) n -> l p c n", p=P)
            wo = t["w_out"].rearrange("l (c p) n -> l p c n", p=P)

            def ffn_src(wg, wu, wd, what, e):
                kind, j = what
                if kind == "d":
                    return wd.rearrange("e (c p) n -> p (e c) n", p=P)[:, bass.ds(e * (FF // P) + 2 * j, 2), :]
                w = wg if kind == "g" else wu
                one = slice(0, 1) if isinstance(e, int) else bass.ds(e, 1)
                return w.rearrange("e (c p) n -> e p c n", p=P)[one, :, :, j * FB:(j + 1) * FB].rearrange("e p c n -> (e p) c n")

            def mixer_src(l, i):
                blk, h, n = slot_block(i)
                half = slice(4 * h, 4 * h + 4)
                if blk < GLU:
                    return win[l, :, half, blk * 512:(blk + 1) * 512]
                if blk == GLU:
                    return wglu[l]
                c = block_column(blk)
                if blk in (PS0, PS0 + 2):
                    return wps[l, :, :, c:c + 512]
                return (wpa if blk < WO0 else wo)[l, :, half, c:c + 512]

            def load(seg, i, src, r=None, ahead=False):
                if seg < 3:
                    before = seg * SEG + before_in(RAW_POS, i)
                    if before >= 0:
                        sp.wait_ge(s_lo, before + 1)
                elif r is PROLOGUE:
                    sp.wait_ge(s_lo, 3 * SEG + before_in(RAW_POS, i) + 1)
                else:
                    sp.wait_ge(s_lo, nslot(3, before_in(ROUND_POS, i) + (SEG + 1 if ahead else 1), r))
                k = src.shape[1]
                sp.dma_start(raw_of(seg, i).rearrange("p (k n) -> p k n", k=k), src).then_inc(landed(seg, i, 0)[0], 16)

            sp.dma_start(x[:, :, :], t["x"].rearrange("(t p) d -> p t d", p=P)).then_inc(s_x0, 16)

            def load_s5(l):
                sp.dma_start(Bst[:, :, :, :], t["s5_b"][l]).then_inc(s_b, 16)
                sp.dma_start(Craw[:, :, :, :], t["s5_c"][l]).then_inc(s_c, 16)

            sp.wait_ge(s_cols, 16)
            sp.wait_ge(s_set, 32)
            for seg in range(3):
                for i in range(SEG):
                    if seg == 1:
                        src = ffn_src(t["dense_w_gate"], t["dense_w_up"], t["dense_w_down"], FFN_SLOTS[i], 0)
                    else:
                        src = mixer_src(seg // 2, i)
                    load(seg, i, src)
                    if (seg, i) == (0, 1):
                        load_s5(0)
                    if (seg, i) == (1, 4):
                        load_s5(1)
            moe = (t["moe_w_gate"], t["moe_w_up"], t["moe_w_down"])
            for i in range(LOADED):
                if i == NRAW:
                    sp.wait_ge(s_m, 4)
                load(3, i, ffn_src(*moe, ROUND_SLOTS[i], 0), PROLOGUE)
            sp.wait_ge(s_route, 1)
            rounds = sp.value_load(rI[0:1, 0:1], min_val=EXPERTS, max_val=MAX_ROUNDS)

            def load_round(r, ahead):
                e = sp.value_load(eI[0:1, bass.ds(r, 1)], min_val=0, max_val=EXPERTS - 1)
                for i in range(LOADED, SEG):
                    load(3, i, ffn_src(*moe, ROUND_SLOTS[i], e), r)
                e = sp.value_load(eI[0:1, bass.ds(r + 1, 1)], min_val=0, max_val=EXPERTS - 1)
                for i in range(ahead):
                    load(3, i, ffn_src(*moe, ROUND_SLOTS[i], e), r, ahead=True)

            with sp.Fori(0, rounds - 1) as r:
                load_round(r, LOADED)
            load_round(rounds - 1, RAHEAD)
            o = t["out"].rearrange("(t p) d -> p t d", p=P)
            for q in range(NT):
                sp.wait_ge(s_fin, q + 1)
                sp.dma_start(o[:, q, :], outt[:, q, :]).then_inc(s_out, 16)
            sp.wait_ge(s_out, 16 * NT)

        def start_turns(e, own, l, p0, w):
            T = tab[:, p0:p0 + 8]
            own.do(e.memset(T[:, :, 0, 0:1], 1.0))
            own.do(e.memset(T[:, :, 1, 0:1], 0.0))
            own.do(e.tensor_copy(w[:, :, 0:1], s5c[:, l, p0:p0 + 8].rearrange("p (q o) -> p q o", o=1)))
            own.do(e.tensor_copy(w[:, :, 1:2], s5s[:, l, p0:p0 + 8].rearrange("p (q o) -> p q o", o=1)))
            own.settle()

        def double_turns(e, own, p0, w, tmp, n):
            T = tab[:, p0:p0 + 8]
            wr, wi = w[:, :, 0:1].to_broadcast([P, 8, n]), w[:, :, 1:2].to_broadcast([P, 8, n])
            er, ei = T[:, :, 0, 0:n], T[:, :, 1, 0:n]
            fr, fi = T[:, :, 0, n:2 * n], T[:, :, 1, n:2 * n]
            u = tmp[:, :, 0:n]
            own.do(e.tensor_tensor(fr, er, wr, ALU.mult))
            own.do(e.tensor_tensor(u, ei, wi, ALU.mult))
            own.do(e.tensor_tensor(fi, ei, wr, ALU.mult))
            own.settle()
            own.do(e.tensor_tensor(fr, fr, u, ALU.subtract))
            own.settle()
            own.do(e.tensor_tensor(u, er, wi, ALU.mult))
            own.do(e.tensor_tensor(w[:, :, 2:3], w[:, :, 0:1], w[:, :, 0:1], ALU.mult))
            own.do(e.tensor_tensor(w[:, :, 3:4], w[:, :, 1:2], w[:, :, 1:2], ALU.mult))
            own.settle()
            own.do(e.tensor_tensor(fi, fi, u, ALU.add))
            own.do(e.tensor_tensor(w[:, :, 1:2], w[:, :, 0:1], w[:, :, 1:2], ALU.mult))
            own.settle()
            own.do(e.tensor_tensor(w[:, :, 0:1], w[:, :, 2:3], w[:, :, 3:4], ALU.subtract))
            own.do(e.tensor_tensor(w[:, :, 1:2], w[:, :, 1:2], w[:, :, 1:2], ALU.add))
            own.settle()

        @block.gpsimd
        def _(pool):
            own = Own(pool, s_pool)

            own.do(nc.gpsimd.memset(ident[:, :], 0.0))
            own.do(nc.gpsimd.memset(maskb[:, :], 0.0))
            own.settle()
            own.do(nc.gpsimd.affine_select(out=ident[:, :], in_=ident[:, :], compare_op=ALU.not_equal, fill=1.0,
                                           base=0, pattern=[[-1, P]], channel_multiplier=1))
            own.do(nc.gpsimd.affine_select(out=maskb[:, :], in_=maskb[:, :], compare_op=ALU.is_ge, fill=NEG,
                                           base=0, pattern=[[-1, P]], channel_multiplier=1))
            own.do(nc.gpsimd.memset(mhalf[:, :], -0.5))
            own.settle()
            nc.gpsimd.tensor_copy(identb[:, :], ident[:, :]).then_inc(s_const, 1)

            def rms_power(n, m, src, dst, k, scale, eps, got, tell):
                pool.wait_ge(got, n)
                own.do(nc.gpsimd.tensor_scalar(m[:, 0:k], src[:, 0:k], scale, eps, ALU.mult, ALU.add))
                own.settle()
                nc.gpsimd.tensor_tensor(dst[:, 0:k], m[:, 0:k], mhalf[:, 0:k], ALU.pow).then_inc(tell, 1)

            rms_power(1, mean, stat, rstd, NT, 1.0 / D, EPS, s_ss, s_rstd)
            for l in range(DEPTH):
                pool.wait_ge(s_trig, 3)
                if l == 1:
                    pool.wait_ge(s_xn, 2)
                start_turns(nc.gpsimd, own, l, 8, wpowp)
                for n in DOUBLINGS:
                    double_turns(nc.gpsimd, own, 8, wpowp, tabp, n)
                nc.gpsimd.memset(wpowp[:, :, 2:3], 0.0).then_inc(s_tabp, 1)
                if l == 1:
                    rms_power(3, mean, stat, rstd, NT, 1.0 / D, EPS, s_ss, s_rstd)
                for s in range(SEG):
                    if 4 <= s < 12:
                        q = s % 2
                        pool.wait_ge(s_accV, ACCV_L * l + s - 3)
                        A = ropeA if q == 0 else ropeC
                        nc.gpsimd.tensor_tensor(A[:, :], A[:, :], ropeB[:, :], ALU.add).then_inc(s_rope, 1)
                    if s >= 5 and (s - 5) % 2 == 0 and (s - 5) // 2 < CHUNKS:
                        c = (s - 5) // 2
                        b = c % 2
                        pool.wait_ge(s_scan, CHUNKS * l + c + 1)
                        if c >= 2:
                            pool.wait_ge(s_yc, CHUNKS * l + c - 1)
                        er, ei = tab[:, 2 * c:2 * c + 2, 0, :], tab[:, 2 * c:2 * c + 2, 1, :]
                        own.do(nc.gpsimd.tensor_tensor(sr[:, b], er, rr[:, b], ALU.mult))
                        own.do(nc.gpsimd.tensor_tensor(tt[:, :, :], ei, ri[:, b], ALU.mult))
                        own.settle()
                        own.do(nc.gpsimd.tensor_tensor(ri[:, b], er, ri[:, b], ALU.mult))
                        own.do(nc.gpsimd.tensor_tensor(rr[:, b], ei, rr[:, b], ALU.mult))
                        own.do(nc.gpsimd.tensor_tensor(sr[:, b], sr[:, b], tt[:, :, :], ALU.subtract))
                        own.settle()
                        nc.gpsimd.tensor_tensor(ri[:, b], ri[:, b], rr[:, b], ALU.add).then_inc(s_rot, 1)
                    if 0 <= s - 17 < HEADS:
                        rms_power(HEADS * l + s - 16, oms, oss, ors, 2, 1.0 / P, SUB_EPS, s_osq, s_ors)
                rms_power(2 + 2 * l, mean, stat, rstd, NT, 1.0 / D, EPS, s_ss, s_rstd)
            own.do(nc.gpsimd.memset(below[:, :], 1.0))
            own.do(nc.gpsimd.iota(iotai[:, :], pattern=[[1, P]], base=0, channel_multiplier=0))
            own.settle()
            own.do(nc.gpsimd.memset(ones[:, :], 1.0))
            own.do(nc.gpsimd.tensor_copy(iota128[:, :], iotai[:, :]))
            own.do(nc.gpsimd.tensor_copy(iota8[:, :], iotai[:, 0:8]))
            nc.gpsimd.affine_select(out=below[:, :], in_=below[:, :], compare_op=ALU.is_gt, fill=0.0,
                                    base=0, pattern=[[1, P]], channel_multiplier=-1).then_inc(s_const, 1)
            rms_power(5, mean, stat, rstd, NT, 1.0 / D, EPS, s_ss, s_rstd)

        @block.scalar
        def _(act):
            own = Own(act, s_actc)
            act.dma_start(cols[:, :], t["columns"]).then_inc(s_cols, 16)
            act.dma_start(rows_[:, :], t["rows"].to_broadcast([P, 4 * DEPTH * HD + HD // 2])).then_inc(s_set, 16)
            act.dma_start(posi[:, :], t["positions"]).then_inc(s_set, 16)

            def norm_sums(row_tile=None):
                for q in range(NT):
                    if row_tile:
                        row_tile(q)
                    i = nc.scalar.activation(outsq[:, q, :], x[:, q, :], ACT.Square, accum_out=stat[:, q:q + 1])
                    if q == NT - 1:
                        i.then_inc(s_ss, 1)

            act.wait_ge(s_x0, 16)
            norm_sums()
            act.wait_ge(s_cols, 16)
            nc.scalar.activation(dtt[:, :, :], ldt[:, :, :], ACT.Exp).then_inc(s_dt, 1)
            act.wait_ge(s_ang, 1)
            own.do(nc.scalar.activation(s5m[:, :, :], q1[:, :, :], ACT.Exp))
            nc.scalar.activation(lame[:, :, :], lams[:, :, :], ACT.Exp).then_inc(s_trig, 1)
            act.wait_ge(s_ang, 2)
            NA = NT * 32
            own.do(nc.scalar.activation(sinT[:, :, :], angr[:, 0:NA].rearrange("p (t f) -> p t f", t=NT), ACT.Sin))
            nc.scalar.activation(s5s[:, :, :], angr[:, NA:].rearrange("p (l q) -> p l q", l=DEPTH), ACT.Sin).then_inc(s_trig, 1)
            own.do(nc.scalar.activation(cosT[:, :, :], angk[:, 0:NA].rearrange("p (t f) -> p t f", t=NT), ACT.Sin))
            nc.scalar.activation(s5c[:, :, :], angk[:, NA:].rearrange("p (l q) -> p l q", l=DEPTH), ACT.Sin).then_inc(s_trig, 1)
            act_split(act, 0, 0)
            act_split(act, 0, 1)

            def norm_hi(l, which):
                for g in range(4):
                    n = TR_AT[l, ("h1", "h2")[which], g]
                    act.wait_ge(s_tr, n + 1)
                    for kk in range(2):
                        k = 2 * g + kk
                        i = nc.scalar.activation(hTh[:, k, :], bank(4 + n % 2)[:, kk * 256:(kk + 1) * 256], ACT.Copy,
                                                 scale=gains[:, which, l, k:k + 1])
                        if kk:
                            i.then_inc(s_thi, 1)

            for l in range(DEPTH):
                seg = 2 * l
                norm_hi(l, 0)
                B0 = BLOCK_COUNT * l
                for s in range(SEG):
                    if s == 2:
                        for q in range(2):
                            act.wait_ge(s_acc, 2 * B0 + q + 1)
                            nc.scalar.activation(uT[:, 2 * q:2 * q + 2, :],
                                                 bank(q).rearrange("p (c n) -> p c n", c=2), ACT.Copy).then_inc(s_accA, 1)
                    if s == 23:
                        for c in range(CT):
                            act.wait_ge(s_acc, 2 * (B0 + GLU) + c // 2 + 1)
                            i = nc.scalar.activation(glt[:, c, :], bank(c // 2)[:, (c % 2) * 256:(c % 2 + 1) * 256],
                                                     ACT.Tanh, scale=0.5, bias=bglu[:, l, c:c + 1])
                            if c % 2:
                                i.then_inc(s_accA, 1)
                    if s in (12, 14):
                        b = 5 + (s - 12) // 2
                        for q in range(NT):
                            act.wait_ge(s_acc, 2 * (B0 + b) + q + 1)
                            nc.scalar.activation(v[:, q, (b - 5) * 512:(b - 4) * 512],
                                                 bank(2 * PAIR_OF[b] + q), ACT.Copy).then_inc(s_accA, 1)
                    if s in (16, 18, 20, 22):
                        b = 7 + (s - 16) // 2
                        dst = gs if b < 9 else ga
                        if s == 16:
                            act.wait_ge(s_rot, CHUNKS * l + 4)
                        for q in range(NT):
                            act.wait_ge(s_acc, 2 * (B0 + b) + q + 1)
                            nc.scalar.activation(dst[:, q, ((b - 7) % 2) * 512:((b - 7) % 2 + 1) * 512],
                                                 bank(q), ACT.Tanh, scale=0.5).then_inc(s_accA, 1)
                    if 0 <= s - 18 < HEADS:
                        h = s - 18
                        n = TR_AT[l, "oT", h]
                        act.wait_ge(s_tr, n + 1)
                        act.wait_ge(s_rot, CHUNKS * l + 5 + h // 4)
                        nc.scalar.activation(yBh[:, h, :], bank(4 + n % 2)[:, 0:256], ACT.Copy,
                                             scale=subg[:, l:l + 1]).then_inc(s_thi, 1)
                    if 0 <= s - 17 < HEADS:
                        act.wait_ge(s_trf, TR_AT[l, "o", s - 17] + 1)
                        for q in range(NT):
                            i = nc.scalar.activation(osq[:, q * P:(q + 1) * P], osb[:, q * P:(q + 1) * P], ACT.Square,
                                                     accum_out=oss[:, q:q + 1])
                        i.then_inc(s_osq, 1)
                    kt, ke = GELU_FROM.get(s), GELU_TO.get(s)
                    if kt is not None:
                        act.wait_ge(s_yv, CT * l + kt + 1)
                        nc.scalar.activation(gel[:, kt, :], uT[:, kt, :], ACT.Square).then_inc(s_gsq, 1)
                    split_ahead(act_split, act, seg, s)
                    if kt is not None:
                        act.wait_ge(s_gin, CT * l + kt + 1)
                        nc.scalar.activation(gth[:, kt, :], gel[:, kt, :], ACT.Tanh, scale=math.sqrt(2 / math.pi)).then_inc(s_gth, 1)
                    if ke is not None:
                        act.wait_ge(s_yg, (CT + 1) * l + ke + 1)
                        nc.scalar.activation(ySh[:, ke, :], uT[:, ke, :], ACT.Copy, scale=0.5).then_inc(s_ygh, 1)
                    if s in (6, 8, 10, 12):
                        b = (s - 4) // 2
                        dst = qT if b < 3 else kT
                        for q in range(NT):
                            n = TR_AT[l, "qkT", 2 * b + q]
                            act.wait_ge(s_tr, n + 1)
                            h0 = ((b - 1) % 2) * 4
                            nc.scalar.activation(dst[:, h0:h0 + 4, q * P:(q + 1) * P],
                                                 bank(4 + n % 2).rearrange("p (h n) -> p h n", h=4), ACT.Copy).then_inc(s_trf, 1)
                    if 0 <= s - 15 < HEADS:
                        h = s - 15
                        act.wait_ge(s_nb, HEADS * l + h + 1)
                        if h:
                            act.wait_ge(s_tr, TR_AT[l, "wT", h - 1] + 1)
                        for q in range(NT):
                            n, off = (q + 1) * P, q * P
                            for c in range(2):
                                src = bank(2 + c)[:, (1 - q) * 256:(1 - q) * 256 + n]
                                i = nc.scalar.activation(prob[:, c, off:off + n], src, ACT.Exp, scale=SCALE,
                                                         bias=nb[:, 2 * q + c:2 * q + c + 1],
                                                         accum_out=sm[:, 2 * q + c:2 * q + c + 1])
                        i.then_inc(s_ex, 1)
                    if s == 23:
                        act.wait_ge(s_yg, (CT + 1) * (l + 1))
                        nc.scalar.activation(ySh[:, :, :], uT[:, :, :], ACT.Copy, scale=0.25).then_inc(s_ygh, 1)
                    if s in (28, 30):
                        for g in (s - 28, s - 27):
                            n = TR_AT[l, "mT", g]
                            act.wait_ge(s_tr, n + 1)
                            nc.scalar.activation(hTh[:, 2 * g:2 * g + 2, :],
                                                 bank(4 + n % 2).rearrange("p (k n) -> p k n", k=2), ACT.Copy,
                                                 scale=0.5).then_inc(s_thi, 1)
                norm_sums(lambda q: act.wait_ge(s_accV, ACCV_L * (l + 1) - (NT - 1) + q))
                if l == 1:
                    act.dma_start(rw[:, :, :], t["router_w"].rearrange("(c p) e -> p c e", p=P)).then_inc(s_rw, 16)
                    act.dma_start(gfin[:, :], t["final_norm"].rearrange("(o d) -> o d", o=1).to_broadcast([P, D])).then_inc(s_gf, 16)
                norm_hi(l, 1)
                if l == 0:
                    for j in range(NJ):
                        if j < NJ - 1:
                            split_ahead(act_split, act, 1, FFN_AT["g", j + 1] - AHEAD)
                            split_ahead(act_split, act, 1, FFN_AT["u", j + 1] - AHEAD)
                        for q in range(NT):
                            act.wait_ge(s_gu, NT * j + q + 1)
                            nc.scalar.activation(sg[:, q, :], bank(6 + q)[:, 0:FB], ACT.Silu).then_inc(s_sg, 1)
                        split_ahead(act_split, act, 1, FFN_AT["d", j] - AHEAD)
                        n = TR_AT[0, "act", j]
                        act.wait_ge(s_tr, n + 1)
                        nc.scalar.activation(aTh[:, :, :], bank(4 + n % 2).rearrange("p (k n) -> p k n", k=2),
                                             ACT.Copy).then_inc(s_thi, 1)
                    for i in range(SEG - AHEAD, SEG):
                        split_ahead(act_split, act, 1, i)
                    act.wait_ge(s_xn, 3)
                    norm_sums()

            act.wait_ge(s_rw, 16)
            nc.scalar.activation(rwh[:, :, :], rw[:, :, :], ACT.Copy).then_inc(s_rwh, 1)
            for i in range(RAHEAD):
                act_split(act, 3, i, PROLOGUE)

            def hs_hi(b, g):
                for kk in range(4):
                    k = 4 * g + kk
                    i = nc.scalar.activation(hsh[:, k, :], b[:, kk * P:(kk + 1) * P], ACT.Copy,
                                             scale=gains[:, 1, 1, k:k + 1])
                i.then_inc(s_thi, 1)

            act.wait_ge(s_lg, 1)
            nc.scalar.activation(den[:, :], ex2[:, :], ACT.Exp).then_inc(s_lg, 1)
            for g in range(2):
                n = TR_AT[1, "hs", g]
                act.wait_ge(s_tr, n + 1)
                hs_hi(bank(4 + n % 2), g)
            act.wait_ge(s_route, 1)
            rounds = act.value_load(rI[0:1, 0:1], min_val=EXPERTS, max_val=MAX_ROUNDS)
            with act.Fori(0, rounds) as r:
                def written(name):
                    n = TR0 + ROUND_TR.index(name)
                    act.wait_ge(s_tr, r * R_TR + (n + 1))
                    return bank(4 + n % 2)

                def act_hi(j):
                    b = written(f"act{j}")
                    nc.scalar.activation(bTh[:, j % 2], b[:, 0:256].rearrange("p (k n) -> p k n", k=2),
                                         ACT.Copy).then_inc(s_thi, 1)

                for i in range(SEG):
                    kind, j = ROUND_SLOTS[i]
                    if i == SEG - 2:
                        act_hi(NJ - 1)
                    if (kind, j) != ("u", NJ - 1):
                        round_split(act_split, act, i, r)
                    if i == SEG - 2:
                        hs_hi(written("hs1"), 1)
                    if kind == "u":
                        if j:
                            act_hi(j - 1) if j < NJ - 1 else None
                        act.wait_ge(s_gu, r * NJ + (GU0 + j + 1))
                        if j:
                            act.wait_ge(s_act, r * NJ + (GU0 + j))
                        nc.scalar.activation(sg[:, 0, :], bank(6 + j % 2)[:, 0:FB], ACT.Silu).then_inc(s_sg, 1)
                        if j == NJ - 1:
                            act_hi(j - 1)
                            hs_hi(written("hs0"), 0)
                            round_split(act_split, act, i, r)
                act.wait_ge(s_used, r * USED_FFN + (2 * USED_MIX + 2 * USED_FFN))
                for c in range(2):
                    nc.scalar.activation(ysb[:, c * 512:(c + 1) * 512], bank(c), ACT.Copy).then_inc(s_ysb, 1)
            act.wait_ge(s_xn, 6)
            norm_sums()

        @block.vector
        def _(dve):
            own = Own(dve, s_dve)
            V = nc.vector

            def norm(n):
                dve.wait_ge(s_rstd, n)
                for q in range(NT):
                    i = V.tensor_scalar(xn[:, q, :], x[:, q, :], rstd[:, q:q + 1], None, ALU.mult)
                i.then_inc(s_xn, 1)

            own.do(V.memset(Cre[:, :, :], 0.0))
            own.do(V.memset(Cin[:, :, :], 0.0))
            norm(1)
            dve.wait_ge(s_set, 32)
            own.do(V.tensor_tensor(lamp[:, 0], lamv[:, 0], lamv[:, 1], ALU.mult))
            own.do(V.tensor_tensor(lamp[:, 1], lamv[:, 2], lamv[:, 3], ALU.mult))
            own.settle()
            own.do(V.tensor_reduce(lams[:, :, :], lamp[:, :, :, :], AX_X, ALU.add))
            NA = NT * 32
            own.do(V.tensor_copy(posf[:, :], posi[:, :]))
            own.settle()
            for q in range(NT):
                own.do(V.tensor_scalar(ang[:, q * 32:(q + 1) * 32], invf[:, :], posf[:, q:q + 1], None, ALU.mult))
            dve.wait_ge(s_dt, 1)
            own.do(V.tensor_tensor(ang[:, NA:].rearrange("p (l q) -> p l q", l=DEPTH), lim[:, :, :], dtt[:, :, :], ALU.mult))
            V.tensor_tensor(q1[:, :, :], lre[:, :, :], dtt[:, :, :], ALU.mult).then_inc(s_ang, 1)
            own.settle()
            own.do(V.tensor_scalar(angk[:, :], ang[:, :], 1 / (2 * math.pi), ROUND, ALU.mult, ALU.add))
            own.settle()
            own.do(V.tensor_scalar(angk[:, :], angk[:, :], -ROUND, None, ALU.add))
            own.settle()
            own.do(V.scalar_tensor_tensor(angr[:, :], angk[:, :], -TWO_PI_HI, ang[:, :], ALU.mult, ALU.add))
            own.settle()
            own.do(V.scalar_tensor_tensor(angr[:, :], angk[:, :], -TWO_PI_MID, angr[:, :], ALU.mult, ALU.add))
            own.settle()
            own.do(V.scalar_tensor_tensor(angr[:, :], angk[:, :], -TWO_PI_LO, angr[:, :], ALU.mult, ALU.add))
            own.settle()
            own.do(V.tensor_scalar(angr[:, :], angr[:, :], PI_IN, -PI_IN, ALU.min, ALU.max))
            own.settle()
            own.do(V.tensor_scalar(angk[:, :], angr[:, :], -1.0, None, ALU.mult))
            own.settle()
            own.do(V.tensor_tensor(angk[:, :], angk[:, :], angr[:, :], ALU.min))
            own.settle()
            V.tensor_scalar(angk[:, :], angk[:, :], math.pi / 2, None, ALU.add).then_inc(s_ang, 1)
            def constants():
                dve.wait_ge(s_trig, 3)
                own.do(V.tensor_tensor(nlam[:, :], lame[:, 1], lame[:, 0], ALU.subtract))
                own.do(V.tensor_scalar(nsinT[:, :, :], sinT[:, :, :], -1.0, None, ALU.mult))
                own.do(V.tensor_scalar(bglu[:, :, :], bglu[:, :, :], 0.5, None, ALU.mult))
                own.settle()
                for l in range(DEPTH):
                    own.do(V.tensor_scalar(nlam[:, l:l + 1], nlam[:, l:l + 1], -lam_init(l), None, ALU.add))
                    own.do(V.tensor_scalar(subg[:, l:l + 1], subg[:, l:l + 1], 1.0 - lam_init(l), None, ALU.mult))
                f = lambda a: a[:, :, :]
                own.do(V.tensor_tensor(f(q1), f(s5m), f(s5c), ALU.mult))
                own.do(V.tensor_tensor(f(q2), f(s5m), f(s5s), ALU.mult))
                own.settle()
                own.do(V.tensor_scalar(f(q1), f(q1), -1.0, None, ALU.add))
                own.do(V.tensor_tensor(f(q3), f(lre), f(lre), ALU.mult))
                own.do(V.tensor_tensor(f(q4), f(lim), f(lim), ALU.mult))
                own.settle()
                own.do(V.tensor_tensor(f(q3), f(q3), f(q4), ALU.add))
                own.settle()
                own.do(V.reciprocal(f(dtt), f(q3)))
                own.settle()
                own.do(V.tensor_tensor(f(s5fr), f(q1), f(lre), ALU.mult))
                own.do(V.tensor_tensor(f(q4), f(q2), f(lim), ALU.mult))
                own.do(V.tensor_tensor(f(s5fi), f(q2), f(lre), ALU.mult))
                own.do(V.tensor_tensor(f(q3), f(q1), f(lim), ALU.mult))
                own.settle()
                own.do(V.tensor_tensor(f(s5fr), f(s5fr), f(q4), ALU.add))
                own.do(V.tensor_tensor(f(s5fi), f(s5fi), f(q3), ALU.subtract))
                own.settle()
                own.do(V.tensor_tensor(f(s5fr), f(s5fr), f(dtt), ALU.mult))
                own.do(V.tensor_tensor(f(s5fi), f(s5fi), f(dtt), ALU.mult))
                own.settle()

            def scale_c(l):
                dve.wait_ge(s_c, 16 * (l + 1))
                fr = s5fr[:, l, :].rearrange("p (q o) -> p q o", o=1).to_broadcast([P, PAIRS, GCH])
                fi = s5fi[:, l, :].rearrange("p (q o) -> p q o", o=1).to_broadcast([P, PAIRS, GCH])
                own.do(V.tensor_tensor(Ctmp[:, 0], Craw[:, 0], fr, ALU.mult))
                own.do(V.tensor_tensor(Ctmp[:, 1], Craw[:, 1], fi, ALU.mult))
                own.settle()
                for g in range(2):
                    a, b = slice(g * 64, g * 64 + 64), slice(g * 16, g * 16 + 16)
                    own.do(V.tensor_tensor(Cre[a, :, b], Ctmp[a, 0], Ctmp[a, 1], ALU.subtract))
                own.settle()
                own.do(V.tensor_tensor(Ctmp[:, 0], Craw[:, 0], fi, ALU.mult))
                own.do(V.tensor_tensor(Ctmp[:, 1], Craw[:, 1], fr, ALU.mult))
                own.settle()
                own.do(V.tensor_scalar(Ctmp[:, 0], Ctmp[:, 0], -1.0, None, ALU.mult))
                own.settle()
                for g in range(2):
                    a, b = slice(g * 64, g * 64 + 64), slice(g * 16, g * 16 + 16)
                    i = V.tensor_tensor(Cin[a, :, b], Ctmp[a, 0], Ctmp[a, 1], ALU.subtract)
                    if g:
                        i.then_inc(s_prep, 1)

            thi = [0]

            def lo_of(dst, src, hi, scale, last=True):
                i = V.scalar_tensor_tensor(dst, src, scale, hi.bitcast(F32), ALU.mult, ALU.subtract)
                if last:
                    i.then_inc(s_trf, 1)

            def norm_lo(l, which):
                for g in range(4):
                    n = TR_AT[l, ("h1", "h2")[which], g]
                    thi[0] += 1
                    dve.wait_ge(s_thi, thi[0])
                    for kk in range(2):
                        k = 2 * g + kk
                        lo_of(hTl[:, k, :], bank(4 + n % 2)[:, kk * 256:(kk + 1) * 256], hTh[:, k, :],
                              gains[:, which, l, k:k + 1], last=bool(kk))

            def rope(l, b, q):
                blk = BLOCK_COUNT * l + b
                dve.wait_ge(s_acc, 2 * blk + q + 1)
                if b > 1 and q == 0:
                    dve.wait_ge(s_tr, TR_AT[l, "qkT", 2 * (b - 1) + 1] + 1)
                if rp[0]:
                    dve.wait_ge(s_rope, rp[0])
                src = bank(2 * PAIR_OF[b] + q).rearrange("p (g h f) -> p g h f", g=8, h=2)
                A = ropeA if q == 0 else ropeC
                Av = A[:, :].rearrange("p (g h f) -> p g h f", g=8, h=2)
                Bv = ropeB[:, :].rearrange("p (g h f) -> p g h f", g=8, h=2)
                cs, sn, ns = cosT[:, q, :], sinT[:, q, :], nsinT[:, q, :]
                bc3 = lambda a: a.rearrange("p (g f) -> p g f", g=1).to_broadcast([P, 8, 32])
                own.do(V.tensor_tensor(Av[:, :, 0, :], src[:, :, 0, :], bc3(cs), ALU.mult))
                own.do(V.tensor_tensor(Av[:, :, 1, :], src[:, :, 1, :], bc3(cs), ALU.mult))
                own.do(V.tensor_tensor(Bv[:, :, 0, :], src[:, :, 1, :], bc3(ns), ALU.mult))
                V.tensor_tensor(Bv[:, :, 1, :], src[:, :, 0, :], bc3(sn), ALU.mult).then_inc(s_accV, 1)
                accv[0] += 1
                rp[0] += 1

            accv, rp = [0], [0]

            def out_block(l, b):
                pair, cs = PAIR_OF[b], slice(block_column(b), block_column(b) + 512)
                for q in range(NT):
                    dve.wait_ge(s_acc, 2 * (BLOCK_COUNT * l + b) + q + 1)
                    src = bank(2 * pair + q)
                    if b < WO0:
                        g_ = gs if b in (PS0, PS0 + 2) else ga
                        i = V.scalar_tensor_tensor(g_[:, q, cs], g_[:, q, cs], 1.0, src, ALU.add, ALU.mult)
                    else:
                        i = V.tensor_tensor(x[:, q, cs], x[:, q, cs], src, ALU.add)
                    i.then_inc(s_accV, 1)
                    accv[0] += 1

            def turns(ns):
                for n in ns:
                    double_turns(V, own, 0, wpow, tabt, n)

            constants()
            start_turns(V, own, 0, 0, wpow)
            turns(DOUBLINGS[:3])
            dve_split(dve, 0, 0)
            dve_split(dve, 0, 1)
            for l in range(DEPTH):
                seg = 2 * l
                norm_lo(l, 0)
                B0 = BLOCK_COUNT * l
                for s in range(SEG):
                    kt, ke = GELU_FROM.get(s), GELU_TO.get(s)
                    if kt is not None:
                        dve.wait_ge(s_yc, CHUNKS * l + 2 * kt + 2)
                        V.scalar_tensor_tensor(uT[:, kt, :], uT[:, kt, :], dskip[:, l, kt:kt + 1],
                                               bank(7)[:, (kt % 2) * 256:(kt % 2 + 1) * 256],
                                               ALU.mult, ALU.add).then_inc(s_yv, 1)
                    if 0 <= s - 17 < HEADS:
                        h = s - 17
                        n = TR_AT[l, "o", h]
                        dve.wait_ge(s_tr, n + 1)
                        if h:
                            dve.wait_ge(s_tr, TR_AT[l, "oT", h - 1] + 1)
                        V.tensor_copy(osb[:, :], bank(4 + n % 2)[:, 0:256]).then_inc(s_trf, 1)
                    if 0 <= s - 16 < HEADS:
                        h = s - 16
                        dve.wait_ge(s_ex, HEADS * l + h + 1)
                        own.do(V.reciprocal(rs[:, :], sm[:, :]))
                        own.settle()
                        own.do(V.tensor_scalar(c2[:, :], rs[:, 1:4:2], nlam[:, l:l + 1], None, ALU.mult))
                        own.settle()
                        for q in range(NT):
                            sl = slice(q * P, q * P + (q + 1) * P)
                            own.do(V.tensor_scalar(prob[:, 1, sl], prob[:, 1, sl], c2[:, q:q + 1], None, ALU.mult))
                        own.settle()
                        for q in range(NT):
                            sl = slice(q * P, q * P + (q + 1) * P)
                            i = V.scalar_tensor_tensor(prob[:, 0, sl], prob[:, 0, sl], rs[:, 2 * q:2 * q + 1],
                                                       prob[:, 1, sl], ALU.mult, ALU.add)
                        i.then_inc(s_w, 1)
                    if kt is not None:
                        dve.wait_ge(s_gsq, CT * l + kt + 1)
                        own.do(V.tensor_scalar(gel[:, kt, :], gel[:, kt, :], 0.044715, 1.0, ALU.mult, ALU.add))
                        own.settle()
                        V.tensor_tensor(gel[:, kt, :], gel[:, kt, :], uT[:, kt, :], ALU.mult).then_inc(s_gin, 1)
                    if 0 <= s - 18 < HEADS:
                        h = s - 18
                        n = TR_AT[l, "oT", h]
                        thi[0] += 1
                        dve.wait_ge(s_thi, thi[0])
                        dve.wait_ge(s_rot, CHUNKS * l + 7 + h // 4)
                        lo_of(yBl[:, h, :], bank(4 + n % 2)[:, 0:256], yBh[:, h, :], subg[:, l:l + 1])
                    if 0 <= s - 16 < HEADS:
                        h = s - 16
                        n = TR_AT[l, "wT", h]
                        dve.wait_ge(s_tr, n + 1)
                        if h:
                            dve.wait_ge(s_tr, TR_AT[l, "o", h - 1] + 1)
                        V.tensor_copy(wT[:, :], bank(4 + n % 2)[:, 0:384]).then_inc(s_trf, 1)
                    if ke is not None:
                        dve.wait_ge(s_gth, CT * l + ke + 1)
                        V.scalar_tensor_tensor(uT[:, ke, :], gth[:, ke, :], 1.0, uT[:, ke, :],
                                               ALU.add, ALU.mult).then_inc(s_yg, 1)
                    if 0 <= s - 15 < HEADS:
                        h = s - 15
                        dve.wait_ge(s_sc, HEADS * l + h + 1)
                        own.do(V.tensor_reduce(mx[:, 0:2], PS[:, 2:4, 256:384], AX_X, ALU.max))
                        own.do(V.tensor_reduce(mx[:, 2:4], PS[:, 2:4, 0:256], AX_X, ALU.max))
                        own.settle()
                        V.tensor_scalar(nb[:, :], mx[:, :], -SCALE, None, ALU.mult).then_inc(s_nb, 1)
                    if 0 <= s - 17 < HEADS:
                        h = s - 17
                        dve.wait_ge(s_ors, HEADS * l + h + 1)
                        for q in range(NT):
                            i = V.tensor_scalar(osb[:, q * P:(q + 1) * P], osb[:, q * P:(q + 1) * P], ors[:, q:q + 1],
                                                None, ALU.mult)
                        i.then_inc(s_on, 1)
                    if ke is not None:
                        dve.wait_ge(s_ygh, (CT + 1) * l + ke + 1)
                        V.scalar_tensor_tensor(ySl[:, ke, :], uT[:, ke, :], 0.5, ySh[:, ke, :].bitcast(F32),
                                               ALU.mult, ALU.subtract).then_inc(s_ygl, 1)
                    if l == 0 and s < 3:
                        split_ahead(dve_split, dve, seg, s)
                    if l == 0 and s < 3:
                        turns(DOUBLINGS[(3, 6, 7)[s]:(6, 7, 8)[s]])
                    if 0 <= s - 3 < PAIRS:
                        p = s - 3
                        c, b = p // 2, (p // 2) % 2
                        dve.wait_ge(s_bu, PAIRS * l + p + 1)
                        if p == 8:
                            dve.wait_ge(s_tabp, l + 1)
                        if p % 2 == 0 and c >= 2:
                            dve.wait_ge(s_yc, CHUNKS * l + c - 1)
                        R_, I_ = rr[:, b, p % 2, :], ri[:, b, p % 2, :]
                        br, bi = bank(6)[:, 0:256], bank(6)[:, 256:512]
                        own.do(V.tensor_tensor(R_, br, tab[:, p, 0, :], ALU.mult))
                        own.do(V.tensor_tensor(t12[:, 0, :], bi, tab[:, p, 1, :], ALU.mult))
                        own.do(V.tensor_tensor(I_, bi, tab[:, p, 0, :], ALU.mult))
                        V.tensor_tensor(t12[:, 1, :], br, tab[:, p, 1, :], ALU.mult).then_inc(s_buf, 1)
                        dve.wait_ge(s_buf, PAIRS * l + p + 1)
                        own.do(V.tensor_tensor(R_, R_, t12[:, 0, :], ALU.add))
                        own.do(V.tensor_tensor(I_, I_, t12[:, 1, :], ALU.subtract))
                        own.settle()
                        m = s5m[:, l, p:p + 1].to_broadcast([P, SEQ])
                        own.do(V.tensor_tensor_scan(R_, m, R_, 0.0, ALU.mult, ALU.add))
                        i = V.tensor_tensor_scan(I_, m, I_, 0.0, ALU.mult, ALU.add)
                        if p % 2:
                            i.then_inc(s_scan, 1)
                        else:
                            own.do(i)
                    if l == 0 and s == 3:
                        scale_c(0)
                    if s in (4, 6, 8, 10):
                        rope(l, (s - 2) // 2, 0)
                    if s in (5, 7, 9, 11):
                        rope(l, (s - 3) // 2, 1)
                    if s == 23:
                        dve.wait_ge(s_accA, ACCA_L * (l + 1))
                        V.scalar_tensor_tensor(uT[:, :, :].rearrange("p c n -> p (c n)"), glt[:, :, :].rearrange("p c n -> p (c n)"), 1.0,
                                               uT[:, :, :].rearrange("p c n -> p (c n)"), ALU.add, ALU.mult).then_inc(s_yg, 1)
                        dve.wait_ge(s_ygh, (CT + 1) * (l + 1))
                        V.scalar_tensor_tensor(ySl[:, :, :].rearrange("p c n -> p (c n)"), uT[:, :, :].rearrange("p c n -> p (c n)"), 0.25,
                                               ySh[:, :, :].rearrange("p c n -> p (c n)").bitcast(F32), ALU.mult,
                                               ALU.subtract).then_inc(s_ygl, 1)
                    if l or s >= 3:
                        split_ahead(dve_split, dve, seg, s)
                    if s in (25, 26, 27, 29, 32):
                        out_block(l, {25: 12, 26: 13, 27: 14, 29: 15, 32: 16}[s])
                    if s in (26, 29):
                        cs = slice(0, 512) if s == 26 else slice(512, 1024)
                        dve.wait_ge(s_accV, accv[0])
                        for q in range(NT):
                            i = V.tensor_tensor(gs[:, q, cs], gs[:, q, cs], ga[:, q, cs], ALU.add)
                        i.then_inc(s_m, 1)
                    if s in (28, 30):
                        for g in (s - 28, s - 27):
                            n = TR_AT[l, "mT", g]
                            thi[0] += 1
                            dve.wait_ge(s_thi, thi[0])
                            lo_of(hTl[:, 2 * g:2 * g + 2, :].rearrange("p k n -> p (k n)"), bank(4 + n % 2),
                                  hTh[:, 2 * g:2 * g + 2, :].rearrange("p k n -> p (k n)"), 0.5)
                out_block(l, 17)
                norm(2 + 2 * l)
                norm_lo(l, 1)
                if l == 0:
                    for j in range(NJ):
                        if j < NJ - 1:
                            split_ahead(dve_split, dve, 1, FFN_AT["g", j + 1] - AHEAD)
                            split_ahead(dve_split, dve, 1, FFN_AT["u", j + 1] - AHEAD)
                        for q in range(NT):
                            dve.wait_ge(s_sg, NT * j + q + 1)
                            V.tensor_tensor(act_t[:, q, :], sg[:, q, :], bank(6 + q)[:, FB:2 * FB],
                                            ALU.mult).then_inc(s_act, 1)
                        split_ahead(dve_split, dve, 1, FFN_AT["d", j] - AHEAD)
                        if j == 1:
                            scale_c(1)
                            start_turns(V, own, 1, 0, wpow)
                        if 2 <= j < 10:
                            turns(DOUBLINGS[j - 2:j - 1])
                        n = TR_AT[0, "act", j]
                        thi[0] += 1
                        dve.wait_ge(s_thi, thi[0])
                        V.tensor_tensor(aTl[:, :, :].rearrange("p k n -> p (k n)"), bank(4 + n % 2),
                                        aTh[:, :, :].rearrange("p k n -> p (k n)").bitcast(F32),
                                        ALU.subtract).then_inc(s_trf, 1)
                    for i in range(SEG - AHEAD, SEG):
                        split_ahead(dve_split, dve, 1, i)
                    dve.wait_ge(s_used, USED_MIX + USED_FFN)
                    for q in range(NT):
                        for c in range(2):
                            i = V.tensor_tensor(x[:, q, c * 512:(c + 1) * 512], x[:, q, c * 512:(c + 1) * 512],
                                                bank(2 * q + c), ALU.add)
                    i.then_inc(s_xn, 1)
                    dve.wait_ge(s_xn, 3)
                    norm(3)

            dve.wait_ge(s_rwh, 1)
            V.tensor_tensor(rwl[:, :, :], rw[:, :, :], rwh[:, :, :].bitcast(F32), ALU.subtract).then_inc(s_rwl, 1)
            dve_split(dve, 3, 0, PROLOGUE)

            def select():
                own.settle()
                for q in range(NT):
                    i = V.tensor_scalar(S[:, q, :], iota128[:, :], pcol[:, q:q + 1], None, ALU.is_equal)
                    if q:
                        i.then_inc(s_S, 1)
                    else:
                        own.do(i)

            n = TR_AT[1, "logitsT", 0]
            dve.wait_ge(s_tr, n + 1)
            V.tensor_copy(lgT[0:EXPERTS, :], bank(4 + n % 2)[0:EXPERTS, 0:SEQ]).then_inc(s_trf, 1)
            n = TR_AT[1, "logits", 0]
            dve.wait_ge(s_tr, n + 1)
            V.tensor_copy(lg[:, :, :], bank(4 + n % 2)[:, 0:16].rearrange("p (t e) -> p t e", t=NT)).then_inc(s_trf, 1)
            dve.wait_ge(s_trf, n + 1)
            for q in range(NT):
                own.do(V.max(top[:, q, :], lg[:, q, :]))
            own.settle()
            for q in range(NT):
                own.do(V.max_index(topi[:, q, :], top[:, q, :], lg[:, q, :]))
            own.settle()
            own.do(V.tensor_copy(topf[:, :, :], topi[:, :, :]))
            V.tensor_tensor(ex2[:, :], top[:, :, 1], top[:, :, 0], ALU.subtract).then_inc(s_lg, 1)
            own.settle()
            dve.wait_ge(s_const, 2)
            for q in range(NT):
                own.do(V.tensor_scalar(oh1[:, q, :], iota8[:, :], topf[:, q, 0:1], None, ALU.is_equal))
                own.do(V.tensor_scalar(oh2[:, q, :], iota8[:, :], topf[:, q, 1:2], None, ALU.is_equal))
            own.settle()
            V.tensor_tensor(M[:, :, :], oh1[:, :, :], oh2[:, :, :], ALU.add).then_inc(s_M, 1)
            dve.wait_ge(s_lg, 2)
            own.do(V.tensor_scalar(g1[:, :], den[:, :], 1.0, None, ALU.add))
            own.settle()
            own.do(V.reciprocal(g1[:, :], g1[:, :]))
            own.settle()
            own.do(V.tensor_tensor(g2[:, :], g1[:, :], den[:, :], ALU.mult))
            own.settle()
            for q in range(NT):
                own.do(V.tensor_scalar(oh1[:, q, :], oh1[:, q, :], g1[:, q:q + 1], None, ALU.mult))
                own.do(V.tensor_scalar(oh2[:, q, :], oh2[:, q, :], g2[:, q:q + 1], None, ALU.mult))
            own.settle()
            own.do(V.tensor_tensor(G[:, :, :], oh1[:, :, :], oh2[:, :, :], ALU.add))
            n = TR_AT[1, "places", 0]
            dve.wait_ge(s_tr, n + 1)
            own.do(V.scalar_tensor_tensor(placed[:, :, :].rearrange("p t e -> p (t e)"), bank(4 + n % 2)[:, 0:16], 1.0,
                                          M[:, :, :].rearrange("p t e -> p (t e)"), ALU.add, ALU.mult))
            V.tensor_copy(cnt[:, :], bank(4 + n % 2)[:, 16:24]).then_inc(s_trf, 1)
            dve.wait_ge(s_trf, n + 1)
            own.do(V.tensor_scalar(pcol[:, :], placed[:, :, 0], -1.0, None, ALU.add))
            select()
            for i in range(1, RAHEAD):
                dve_split(dve, 3, i, PROLOGUE)
            own.do(V.tensor_scalar(over[:, :], cnt[:, :], float(P), None, ALU.is_gt))
            own.settle()
            own.do(V.tensor_tensor_scan(overc[:, :], ones[:, 0:8], over[:, :], 0.0, ALU.mult, ALU.add))
            own.settle()
            own.do(V.tensor_scalar(rF[:, :], overc[:, 7:8], float(EXPERTS), None, ALU.add))
            for k in range(3):
                own.do(V.tensor_scalar(ohr[:, k, :], overc[:, :], float(k + 1), None, ALU.is_equal))
            own.settle()
            for k in range(3):
                own.do(V.tensor_tensor(ohr[:, k, :], ohr[:, k, :], over[:, :], ALU.mult))
            own.do(V.memset(eF[:, 8:12], 0.0))
            own.do(V.tensor_copy(eF[:, 0:8], iota8[:, :]))
            for q in range(NT):
                own.do(V.tensor_scalar(placeR[:, q, 0:8], placed[:, q, :], -1.0, None, ALU.add))
                own.do(V.tensor_copy(gateR[:, q, 0:8], G[:, q, :]))
            own.settle()
            for k in range(3):
                one = ohr[:, k, :].rearrange("p (o e) -> p o e", o=1).to_broadcast([P, 1 + 2 * NT, 8])
                own.do(V.tensor_tensor(prod[:, k], five[:, :, :], one, ALU.mult))
            own.settle()
            own.do(V.tensor_reduce(picked[:, :, :], prod[:, :, :, :], AX_X, ALU.add))
            own.settle()
            own.do(V.tensor_copy(eF[:, 8:11], picked[:, :, 0]))
            for q in range(NT):
                own.do(V.tensor_copy(gateR[:, q, 8:11], picked[:, :, 1 + NT + q]))
            for q in range(NT):
                own.do(V.tensor_scalar(placeR[:, q, 8:11], picked[:, :, 1 + q], -1.0 - P, None, ALU.add))
                own.do(V.memset(placeR[:, q, 11:12], -1.0))
                own.do(V.memset(gateR[:, q, 11:12], 0.0))
            own.settle()
            own.do(V.tensor_copy(eI[:, :], eF[:, :]))
            own.settle()
            V.tensor_copy(rI[:, :], rF[:, :]).then_inc(s_route, 1)
            dve.wait_ge(s_route, 1)
            rounds = dve.value_load(rI[0:1, 0:1], min_val=EXPERTS, max_val=MAX_ROUNDS)

            def hs_lo(b, g):
                for kk in range(4):
                    k = 4 * g + kk
                    lo_of(hsl[:, k, :], b[:, kk * P:(kk + 1) * P], hsh[:, k, :],
                          gains[:, 1, 1, k:k + 1], last=(kk == 3))

            for g in range(2):
                n = TR_AT[1, "hs", g]
                thi[0] += 1
                dve.wait_ge(s_thi, thi[0])
                hs_lo(bank(4 + n % 2), g)
            V.memset(prod[:, 0, 0, :], 0.0).then_inc(s_scatv, 4)
            own.per = 3
            base = own.n
            THI0 = thi[0]
            with dve.Fori(0, rounds) as r:
                own.r = r
                his = [0]

                def hi_taken(name):
                    his[0] += 1
                    dve.wait_ge(s_thi, r * (2 + NJ) + (THI0 + his[0]))
                    return bank(4 + (TR0 + ROUND_TR.index(name)) % 2)

                def act_lo(j):
                    b = hi_taken(f"act{j}")
                    V.tensor_tensor(bTl[:, j % 2].rearrange("p k n -> p (k n)"), b[:, 0:256],
                                    bTh[:, j % 2].rearrange("p k n -> p (k n)").bitcast(F32),
                                    ALU.subtract).then_inc(s_trf, 1)

                own.do(V.tensor_copy(gcol[:, :], gateR[:, :, bass.ds(r, 1)].rearrange("p t o -> p (t o)")))
                for i in range(SEG):
                    kind, j = ROUND_SLOTS[i]
                    if i == SEG - 2:
                        act_lo(NJ - 1)
                    if (kind, j) != ("u", NJ - 1):
                        round_split(dve_split, dve, i, r)
                    if i == SEG - 2:
                        hs_lo(hi_taken("hs1"), 1)
                    if i == 0:
                        n = TR0 + ROUND_TR.index("ST")
                        dve.wait_ge(s_tr, r * R_TR + (n + 1))
                        V.tensor_copy(ST[:, :], bank(4 + n % 2)[:, 0:256]).then_inc(s_trf, 1)
                    if i == SEG // 2:
                        own.do(V.tensor_copy(pcol[:, :], placeR[:, :, bass.ds(r + 1, 1)].rearrange("p t o -> p (t o)")))
                        select()
                    if kind == "u":
                        if j and j < NJ - 1:
                            act_lo(j - 1)
                        dve.wait_ge(s_sg, r * NJ + (GU0 + j + 1))
                        if j == NJ - 1:
                            dve.wait_ge(s_tr, r * R_TR + (TR0 + ROUND_TR.index(f"act{j - 1}") + 1))
                        V.tensor_tensor(act_t[:, 0, :], sg[:, 0, :], bank(6 + j % 2)[:, FB:2 * FB], ALU.mult).then_inc(s_act, 1)
                        if j == NJ - 1:
                            act_lo(j - 1)
                            hs_lo(hi_taken("hs0"), 0)
                            round_split(dve_split, dve, i, r)
                for q in range(NT):
                    for c in range(2):
                        dve.wait_ge(s_scat, r * 4 + (2 * q + c + 1))
                        V.scalar_tensor_tensor(x[:, q, c * 512:(c + 1) * 512], bank(SCATTER_BANKS[2 * q + c]), gcol[:, q:q + 1],
                                               x[:, q, c * 512:(c + 1) * 512], ALU.mult, ALU.add).then_inc(s_scatv, 1)
                dve.wait_ge(s_scatv, r * 4 + 8)
            assert own.n - base == own.per
            V.tensor_copy(pcol[:, 0:1], rF[:, :]).then_inc(s_xn, 1)
            dve.wait_ge(s_gf, 16)
            dve.wait_ge(s_rstd, 5)
            for q in range(NT):
                V.scalar_tensor_tensor(outt[:, q, :], x[:, q, :], rstd[:, q:q + 1], gfin[:, :], ALU.mult,
                                       ALU.mult).then_inc(s_fin, 1)

        @block.tensor
        def _(pe):
            mm = nc.tensor.matmul

            def mm3(out, lh, ll, rh, rl, start, stop):
                mm(out, lh, rh, start=start, stop=False)
                mm(out, ll, rh, start=False, stop=False)
                return mm(out, lh, rl, start=False, stop=stop)

            def tr_bank(n):
                if n >= 2:
                    pe.wait_ge(s_trf, n - 1)
                return bank(4 + n % 2)

            def tr_bank_r(r, name):
                n = TR0 + ROUND_TR.index(name)
                pe.wait_ge(s_trf, r * R_TR + (n - 1))
                return bank(4 + n % 2)

            def transposes(dst, srcs):
                for k, s in enumerate(srcs):
                    i = nc.tensor.transpose(dst[:, k * P:(k + 1) * P], s, ident[:, :])
                i.then_inc(s_tr, 1)

            def to_T(l, name, src):
                for g in range(4):
                    transposes(tr_bank(TR_AT[l, name, g]),
                               [src[:, q, k * P:(k + 1) * P] for k in (2 * g, 2 * g + 1) for q in range(NT)])

            def between(l, todo):
                for what, h in todo:
                    if what == "scores":
                        if h == 0:
                            acc_free(l, 5)
                            pe.wait_ge(s_trf, TR_AT[l, "qkT", 9] + 1)
                        else:
                            pe.wait_ge(s_ex, HEADS * l + h)
                        for c in range(2):
                            for q in (1, 0):
                                n, off = (q + 1) * P, (1 - q) * 256
                                mm(bank(2 + c)[:, off:off + n], qT[c * 64:(c + 1) * 64, h, q * P:(q + 1) * P],
                                   kT[c * 64:(c + 1) * 64, h, 0:n], start=(q == 1), stop=False)
                                i = mm(bank(2 + c)[:, off + q * P:off + n], identb[:, :], maskb[:, :],
                                       start=False, stop=(q == 0))
                        i.then_inc(s_sc, 1)
                    elif what == "wT":
                        b = tr_bank(TR_AT[l, "wT", h])
                        pe.wait_ge(s_w, HEADS * l + h + 1)
                        transposes(b, [prob[:, 0, k * P:(k + 1) * P] for k in range(3)])
                    elif what == "o":
                        b = tr_bank(TR_AT[l, "o", h])
                        pe.wait_ge(s_trf, TR_AT[l, "wT", h] + 1)
                        if h == 0:
                            pe.wait_ge(s_accA, ACCA_L * l + 6)
                        vh = [v[:, q, h * P:(h + 1) * P] for q in range(NT)]
                        mm(b[:, 0:P], wT[:, 0:P], vh[0], start=True, stop=False)
                        mm(b[:, P:2 * P], wT[:, P:2 * P], vh[0], start=False, stop=False)
                        mm(b[:, P:2 * P], wT[:, 2 * P:3 * P], vh[1], start=False, stop=True).then_inc(s_tr, 1)
                    elif what == "oT":
                        b = tr_bank(TR_AT[l, "oT", h])
                        pe.wait_ge(s_on, HEADS * l + h + 1)
                        transposes(b, [osb[:, q * P:(q + 1) * P] for q in range(NT)])
                    elif what == "qkT":
                        for q in range(NT):
                            b = tr_bank(TR_AT[l, "qkT", 2 * h + q])
                            pe.wait_ge(s_rope, 8 * l + 2 * (h - 1) + q + 1)
                            src = ropeA if q == 0 else ropeC
                            transposes(b, [src[:, k * P:(k + 1) * P] for k in range(4)])
                    elif what == "bu":
                        kt, q = h // 4, h % 4
                        if h == 0:
                            pe.wait_ge(s_accA, ACCA_L * l + 2)
                            pe.wait_ge(s_b, 16 * (l + 1))
                        if h or l:
                            pe.wait_ge(s_buf, PAIRS * l + h)
                        rows = slice(32 * q, 32 * q + 32)
                        mm(bank(6)[:, 0:256], Bst[rows, 0, kt, :], uT[rows, kt, :], start=True, stop=False)
                        mm(bank(6)[:, 256:512], Bst[rows, 1, kt, :], uT[rows, kt, :], start=False, stop=True).then_inc(s_bu, 1)
                    elif what == "y":
                        pe.wait_ge(s_rot, CHUNKS * l + h + 1)
                        kt = h // 2
                        if h == 0:
                            pe.wait_ge(s_prep, l + 1)
                        if kt >= 2:
                            pe.wait_ge(s_yv, CT * l + kt - 1)
                        for k in range(2):
                            p = 2 * h + k
                            q = p % 4
                            o = PS[32 * q:32 * q + 32, 7, (kt % 2) * 256:(kt % 2 + 1) * 256]
                            mm(o, Cre[:, p, :], sr[:, h % 2, k, :], start=True, stop=False)
                            i = mm(o, Cin[:, p, :], ri[:, h % 2, k, :], start=False, stop=True)
                        i.then_inc(s_yc, 1)
                    elif what == "mT":
                        pe.wait_ge(s_m, 2 * l + h + 1)
                        for g in (2 * h, 2 * h + 1):
                            transposes(tr_bank(TR_AT[l, "mT", g]),
                                       [gs[:, q, k * P:(k + 1) * P] for k in (2 * g, 2 * g + 1) for q in range(NT)])

            def acc_free(l, b, q=1):
                if b in EVAC_BY_ACT:
                    pe.wait_ge(s_accA, ACCA_L * l + 2 * sum(1 for k in range(b) if k in EVAC_BY_ACT) + q + 1)
                else:
                    pe.wait_ge(s_accV, ACCV_L * l + 2 * sum(1 for k in range(b) if k not in EVAC_BY_ACT) + q + 1)

            pe.wait_ge(s_const, 1)
            for l in range(DEPTH):
                seg = 2 * l
                pe.wait_ge(s_xn, 1 if l == 0 else 4)
                to_T(l, "h1", xn)
                for s in range(SEG):
                    blk, h, nh = slot_block(s)
                    pair = PAIR_OF[blk]
                    before = [k for k in range(blk) if PAIR_OF[k] == pair]
                    if h == 0:
                        if before:
                            acc_free(l, before[-1], q=0)
                        if blk == PA0:
                            pe.wait_ge(s_ex, HEADS * (l + 1))
                    if blk == U_BLOCK:
                        pe.wait_ge(s_trf, TR_AT[l, "h1", 2 * h + 1] + 1)
                    if blk == GLU:
                        pe.wait_ge(s_ygl, (CT + 1) * l + CT)
                    if blk == PS0:
                        pe.wait_ge(s_ygl, (CT + 1) * (l + 1))
                    if blk == PA0:
                        pe.wait_ge(s_trf, TR_AT[l, "oT", 3 + 4 * h] + 1)
                    if blk == WO0:
                        pe.wait_ge(s_trf, TR_AT[l, "mT", 1 + 2 * h] + 1)
                    pe.wait_ge(s_lo, nslot(seg, s) + 1)
                    H, L = parts(seg, s, 4)
                    if blk in (U_BLOCK, GLU):
                        ah, al = (hTh, hTl) if blk == U_BLOCK else (ySh, ySl)
                        for c in range(CT):
                            if c == 2:
                                if h == 0 and before:
                                    acc_free(l, before[-1], q=1)
                                between(l, mixer_mid(s))
                            o = bank(2 * pair + c // 2)[:, (c % 2) * 256:(c % 2 + 1) * 256]
                            for kk in range(4):
                                k = 4 * h + kk
                                cs = slice(c * P, (c + 1) * P)
                                i = mm3(o, H[:, kk, cs], L[:, kk, cs], ah[:, k, :], al[:, k, :],
                                        start=(k == 0 and c % 2 == 0), stop=(kk == 3 and h == nh - 1 and c % 2 == 1))
                            if h == nh - 1 and c % 2:
                                i.then_inc(s_acc, 1)
                            elif h < nh - 1 and c == CT - 1:
                                i.then_inc(s_used, 1)
                    else:
                        ah, al = ((ySh, ySl) if blk in (PS0, PS0 + 2) else (yBh, yBl) if blk in (PA0, PA0 + 2)
                                  else (hTh, hTl))
                        for q in range(NT):
                            if q:
                                if h == 0 and before:
                                    acc_free(l, before[-1], q=1)
                                between(l, mixer_mid(s))
                            o = bank(2 * pair + q)
                            for kk in range(4):
                                k = 4 * h + kk
                                tk = slice(q * P, (q + 1) * P)
                                i = mm3(o, ah[:, k, tk], al[:, k, tk], H[:, kk, :], L[:, kk, :],
                                        start=(k == 0), stop=(kk == 3 and h == nh - 1))
                            if h == nh - 1:
                                i.then_inc(s_acc, 1)
                            elif q == NT - 1:
                                i.then_inc(s_used, 1)
                    between(l, mixer_tail(s))
                pe.wait_ge(s_xn, 2 + 3 * l)
                to_T(l, "h2", xn)
                if l:
                    pe.wait_ge(s_trf, TR_AT[l, "h2", 3] + 1)
                if l == 0:
                    def turn2(j):
                        b = tr_bank(TR_AT[0, "act", j])
                        pe.wait_ge(s_act, NT * (j + 1))
                        transposes(b, [act_t[:, q, k * P:(k + 1) * P] for k in range(2) for q in range(NT)])

                    def gate_up2(j):
                        ig, iu = FFN_AT["g", j], FFN_AT["u", j]
                        for q in range(NT):
                            if q and j:
                                turn2(j - 1)
                            tk = slice(q * P, (q + 1) * P)
                            if j:
                                pe.wait_ge(s_act, NT * (j - 1) + q + 1)
                            for n, i_ in enumerate((ig, iu)):
                                if q == 0:
                                    pe.wait_ge(s_lo, nslot(1, i_) + 1)
                                H, L = parts(1, i_, KD)
                                for k in range(KD):
                                    if (j, q, n, k % 2) == (0, 0, 0, 0):
                                        pe.wait_ge(s_trf, TR_AT[0, "h2", k // 2] + 1)
                                    i = mm3(bank(6 + q)[:, n * FB:(n + 1) * FB], hTh[:, k, tk], hTl[:, k, tk],
                                            H[:, k, :], L[:, k, :], start=(k == 0 and n == 0), stop=(k == KD - 1 and n == 1))
                                if n == 0 and q == NT - 1:
                                    i.then_inc(s_used, 1)
                            i.then_inc(s_gu, 1)

                    gate_up2(0)
                    for j in range(NJ):
                        if j < NJ - 1:
                            gate_up2(j + 1)
                        if j == NJ - 1:
                            turn2(j)
                        i_ = FFN_AT["d", j]
                        pe.wait_ge(s_trf, TR_AT[0, "act", j] + 1)
                        pe.wait_ge(s_lo, nslot(1, i_) + 1)
                        H, L = parts(1, i_, 2)
                        for q in range(NT):
                            for c in range(2):
                                for k in range(2):
                                    i = mm3(bank(2 * q + c), aTh[:, k, q * P:(q + 1) * P], aTl[:, k, q * P:(q + 1) * P],
                                            H[:, k, c * 512:(c + 1) * 512], L[:, k, c * 512:(c + 1) * 512],
                                            start=(j == 0 and k == 0), stop=(j == NJ - 1 and k == 1))
                        i.then_inc(s_used, 1)

            pe.wait_ge(s_rwl, 1)
            b = tr_bank(TR_AT[1, "logitsT", 0])
            for k in range(KD):
                i = mm3(b[0:EXPERTS, 0:SEQ], rwh[:, k, :], rwl[:, k, :], hTh[:, k, :], hTl[:, k, :],
                        start=(k == 0), stop=(k == KD - 1))
            i.then_inc(s_tr, 1)
            b = tr_bank(TR_AT[1, "logits", 0])
            pe.wait_ge(s_trf, TR_AT[1, "logitsT", 0] + 1)
            for q in range(NT):
                i = nc.tensor.transpose(b[:, q * 8:(q + 1) * 8], lgT[0:EXPERTS, q * P:(q + 1) * P],
                                        ident[0:EXPERTS, 0:EXPERTS])
            i.then_inc(s_tr, 1)
            b = tr_bank(TR_AT[1, "places", 0])
            pe.wait_ge(s_M, 1)
            mm(b[:, 0:8], below[:, :], M[:, 0, :], start=True, stop=False)
            mm(b[:, 8:16], ones[:, :], M[:, 0, :], start=False, stop=False)
            mm(b[:, 8:16], below[:, :], M[:, 1, :], start=False, stop=False)
            mm(b[:, 16:24], ones[:, :], M[:, 0, :], start=False, stop=False)
            mm(b[:, 16:24], ones[:, :], M[:, 1, :], start=False, stop=True).then_inc(s_tr, 1)

            def gather(b, g):
                for kk in range(4):
                    k = 4 * g + kk
                    for q in range(NT):
                        i = mm(b[:, kk * P:(kk + 1) * P], xn[:, q, k * P:(k + 1) * P], S[:, q, :],
                               start=(kk == 0 and q == 0), stop=(kk == 3 and q == 1))
                i.then_inc(s_tr, 1)

            pe.wait_ge(s_S, 1)
            for g in range(2):
                gather(tr_bank(TR_AT[1, "hs", g]), g)
            pe.wait_ge(s_trf, TR_AT[1, "hs", 1] + 1)
            pe.wait_ge(s_route, 1)
            rounds = pe.value_load(rI[0:1, 0:1], min_val=EXPERTS, max_val=MAX_ROUNDS)
            with pe.Fori(0, rounds) as r:
                transposes(tr_bank_r(r, "ST"), [S[:, q, :] for q in range(NT)])
                pe.wait_ge(s_trf, r * R_TR + TR0)

                def up(i):
                    kind, j = ROUND_SLOTS[i]
                    n = "gu".index(kind)
                    if n == 0 and j >= 2:
                        pe.wait_ge(s_act, r * NJ + (GU0 + j - 1))
                    if n == 0 and j == 1:
                        pe.wait_ge(s_scatv, r * 4 + 3)
                    pe.wait_ge(s_lo, nslot(3, i, r) + 1)
                    H, L = parts(3, i, KD)
                    for k in range(KD):
                        m = mm3(bank(6 + j % 2)[:, n * FB:(n + 1) * FB], hsh[:, k, :], hsl[:, k, :],
                                H[:, k, :], L[:, k, :], start=(k == 0 and n == 0), stop=(k == KD - 1 and n == 1))
                    m.then_inc(s_gu if n else s_used, 1)

                def turn(j):
                    b = tr_bank_r(r, f"act{j}")
                    pe.wait_ge(s_act, r * NJ + (GU0 + j + 1))
                    transposes(b, [act_t[:, 0, k * P:(k + 1) * P] for k in range(2)])

                def down(i):
                    j = ROUND_SLOTS[i][1]
                    pe.wait_ge(s_lo, nslot(3, i, r) + 1)
                    pe.wait_ge(s_trf, r * R_TR + (TR0 + ROUND_TR.index(f"act{j}") + 1))
                    H, L = parts(3, i, 2)
                    for c in range(2):
                        for k in range(2):
                            m = mm3(bank(c), bTh[:, j % 2, k, :], bTl[:, j % 2, k, :], H[:, k, c * 512:(c + 1) * 512],
                                    L[:, k, c * 512:(c + 1) * 512], start=(j == 0 and k == 0),
                                    stop=(j == NJ - 1 and k == 1))
                    m.then_inc(s_used, 1)

                for i in range(SEG):
                    kind, j = ROUND_SLOTS[i]
                    if kind == "d":
                        down(i)
                        if i == SEG - 2:
                            turn(NJ - 1)
                            gather(tr_bank_r(r, "hs1"), 1)
                        continue
                    up(i)
                    if kind == "u" and j:
                        turn(j - 1)
                        if j == NJ - 1:
                            pe.wait_ge(s_S, r + 2)
                            gather(tr_bank_r(r, "hs0"), 0)
                for q in range(NT):
                    for c in range(2):
                        if q == 0:
                            pe.wait_ge(s_ysb, r * 2 + (c + 1))
                        if q and c:
                            pe.wait_ge(s_scatv, r * 4 + 5)
                        mm(bank(SCATTER_BANKS[2 * q + c]), ST[:, q * P:(q + 1) * P], ysb[:, c * 512:(c + 1) * 512],
                           start=True, stop=True).then_inc(s_scat, 1)


def by_chunk(a, n):
    return a.reshape(DEPTH, n, P).transpose(2, 0, 1)


def inv_freq():
    return (10000.0 ** (-np.arange(0, HD, 2, dtype=np.float32) / HD)).astype(np.float32).reshape(1, -1)


def wide_b(b):
    w = np.zeros((DEPTH, P, CT, P), b.dtype)
    v = b.transpose(0, 1, 3, 2).reshape(DEPTH, CT, P // GCH, GCH, STATE)
    for g in range(P // GCH):
        w[:, g * GCH:(g + 1) * GCH, :, (g % 2) * STATE:(g % 2 + 1) * STATE] = v[:, :, g].transpose(0, 2, 1, 3)
    return w


INPUTS = {
    "x": lambda a: a["x"].reshape(SEQ, D),
    "positions": lambda a: a["positions"].reshape(NT, P).transpose(1, 0),
    "columns": lambda a: np.concatenate([lay(a).reshape(P, -1) for _, _, lay in COLUMN_ARRAYS], 1),
    "rows": lambda a: np.concatenate([a["lambda_q1"].reshape(1, -1), a["lambda_k1"].reshape(1, -1),
                                      a["lambda_q2"].reshape(1, -1), a["lambda_k2"].reshape(1, -1), inv_freq()], 1),
    "s5_b": lambda a: np.stack([wide_b(a["ssm_b_re"]), wide_b(a["ssm_b_im"])], 2),
    "s5_c": lambda a: np.stack([a[n].reshape(DEPTH, PAIRS, 2, GCH, STATE).transpose(0, 2, 4, 1, 3)
                                .reshape(DEPTH, P, PAIRS, GCH) for n in ("ssm_c_re", "ssm_c_im")], 2),
    "router_w": lambda a: a["router_w"].reshape(D, EXPERTS),
    "moe_w_gate": lambda a: a["moe_w_gate"].reshape(EXPERTS, D, FF),
    "moe_w_up": lambda a: a["moe_w_up"].reshape(EXPERTS, D, FF),
    "moe_w_down": lambda a: a["moe_w_down"].reshape(EXPERTS, FF, D),
}
for _n in ("w_in", "w_glu", "w_proj_ssm", "w_proj_attn", "w_out", "dense_w_gate", "dense_w_up", "dense_w_down", "final_norm"):
    INPUTS[_n] = (lambda n: lambda a: a[n])(_n)


def kernel(**inputs):
    import concourse.bacc as bacc
    from concourse.bass_utils import run_bass_kernel_spmd

    nc = bacc.Bacc("TRN2", target_bir_lowering=False, num_devices=1)
    arrays, t = {}, {}
    given = {k: np.asarray(v) for k, v in inputs.items()}
    for name, lay in INPUTS.items():
        a = np.ascontiguousarray(lay(given))
        arrays[f"in_{name}"] = a
        t[name] = nc.dram_tensor(f"in_{name}", a.shape, mybir.dt.from_np(a.dtype), kind="ExternalInput").ap()
    t["out"] = nc.dram_tensor("out_trunk", (SEQ, D), F32, kind="ExternalOutput").ap()
    trunk(nc, t)
    r = run_bass_kernel_spmd(nc, [arrays], core_ids=[0])
    return r.results[0]["out_trunk"].reshape(1, SEQ, D)
```
